# Optimizing a Trainium2 kernel written in Bass

```python
import math
import jax, jax.numpy as jnp
from jax import lax
import numpy as np

D_MODEL = 1024
BATCH = 1
SEQ = 512
DEPTH = 2

CHUNK = 64
Q_BLOCK = 128
D_MIX = D_MODEL
SSD_WIDTH = D_MIX // 2
SSD_HEAD_DIM = 64
SSD_HEADS = SSD_WIDTH // SSD_HEAD_DIM
SSD_GROUPS = 2
SSD_HPG = SSD_HEADS // SSD_GROUPS
SSD_STATE = 128
SSD_CONV = 4
SSD_CONV_DIM = SSD_WIDTH + 2 * SSD_GROUPS * SSD_STATE
SSD_IN = SSD_WIDTH + SSD_CONV_DIM + SSD_HEADS
FOX_WIDTH = D_MIX // 4
FOX_HEAD_DIM = 64
FOX_HEADS = FOX_WIDTH // FOX_HEAD_DIM
FOX_IN = 3 * FOX_WIDTH + FOX_HEADS
SCONV_WIDTH = D_MIX - SSD_WIDTH - FOX_WIDTH
SCONV_K = 3
SCONV_IN = 3 * SCONV_WIDTH
D_IN_PROJ = SSD_IN + FOX_IN + SCONV_IN
D_FF = 2816
ALPHA = (2 * DEPTH) ** 0.25
BETA = (8 * DEPTH) ** -0.25
LN_EPS = 1e-5
RMS_EPS = 1e-5
N_SUB = 3


def layer_norm(x, g, b):
    xf = x.astype(jnp.float32)
    mu = jnp.mean(xf, axis=-1, keepdims=True)
    var = jnp.mean(jnp.square(xf - mu), axis=-1, keepdims=True)
    return ((xf - mu) * lax.rsqrt(var + LN_EPS) * g + b).astype(x.dtype)

def causal_depthwise_conv(x, w, b=None):
    k_w, ch = w.shape
    y = lax.conv_general_dilated(
        x, w[:, None, :], window_strides=(1,), padding=[(k_w - 1, 0)],
        dimension_numbers=("NWC", "WIO", "NWC"), feature_group_count=ch)
    return y if b is None else y + b

def swiglu_ffn(h, w_in, w_out):
    gate, up = jnp.split(h @ w_in, 2, axis=-1)
    return (jax.nn.silu(gate) * up) @ w_out

def segsum(a):
    t = a.shape[-1]
    cs = jnp.cumsum(a, axis=-1)
    diff = cs[..., :, None] - cs[..., None, :]
    mask = jnp.tril(jnp.ones((t, t), dtype=bool))
    return jnp.where(mask, diff, -jnp.inf)

def ssd_chunked_scan(xdt, a, bm, cm):
    b, seq, g, e, p = xdt.shape
    n = bm.shape[-1]
    nc = seq // CHUNK
    xdt = xdt.reshape(b, nc, CHUNK, g, e, p)
    bm = bm.reshape(b, nc, CHUNK, g, n)
    cm = cm.reshape(b, nc, CHUNK, g, n)
    a = jnp.transpose(a.reshape(b, nc, CHUNK, g, e), (0, 3, 4, 1, 2))
    a_cs = jnp.cumsum(a, axis=-1)
    l_mat = jnp.exp(segsum(a))
    cb = jnp.einsum("bclgn,bcsgn->bgcls", cm, bm)
    y_diag = jnp.einsum("bgcls,bgecls,bcsgep->bclgep", cb, l_mat, xdt)
    decay_states = jnp.exp(a_cs[..., -1:] - a_cs)
    states = jnp.einsum("bclgn,bgecl,bclgep->bcgepn", bm, decay_states, xdt)
    chunk_a = jnp.pad(a_cs[..., -1], ((0, 0), (0, 0), (0, 0), (1, 0)))
    decay_chunk = jnp.exp(segsum(chunk_a))
    states = jnp.concatenate([jnp.zeros_like(states[:, :1]), states], axis=1)
    states_in = jnp.einsum("bgezc,bcgepn->bzgepn", decay_chunk, states)[:, :-1]
    y_off = jnp.einsum("bclgn,bcgepn,bgecl->bclgep", cm, states_in, jnp.exp(a_cs))
    return (y_diag + y_off).reshape(b, seq, g, e, p)

def mamba2_group(proj, conv_w, conv_b, dt_bias, a_log, d_skip, norm_g):
    b, seq, _ = proj.shape
    z, xbc, dt_raw = jnp.split(proj, [SSD_WIDTH, SSD_WIDTH + SSD_CONV_DIM], axis=-1)
    xbc = jax.nn.silu(causal_depthwise_conv(xbc, conv_w, conv_b))
    xs, bm, cm = jnp.split(xbc, [SSD_WIDTH, SSD_WIDTH + SSD_GROUPS * SSD_STATE], axis=-1)
    xs = xs.astype(jnp.float32).reshape(b, seq, SSD_GROUPS, SSD_HPG, SSD_HEAD_DIM)
    bm = bm.astype(jnp.float32).reshape(b, seq, SSD_GROUPS, SSD_STATE)
    cm = cm.astype(jnp.float32).reshape(b, seq, SSD_GROUPS, SSD_STATE)
    dt = jax.nn.softplus(dt_raw.astype(jnp.float32) + dt_bias.astype(jnp.float32))
    dt = dt.reshape(b, seq, SSD_GROUPS, SSD_HPG)
    a_head = -jnp.exp(a_log.astype(jnp.float32)).reshape(SSD_GROUPS, SSD_HPG)
    y = ssd_chunked_scan(xs * dt[..., None], dt * a_head, bm, cm)
    y = y + d_skip.astype(jnp.float32).reshape(SSD_GROUPS, SSD_HPG)[:, :, None] * xs
    y = y.reshape(b, seq, SSD_WIDTH) * jax.nn.silu(z.astype(jnp.float32))
    yg = y.reshape(b, seq, SSD_GROUPS, SSD_WIDTH // SSD_GROUPS)
    yg = yg * lax.rsqrt(jnp.mean(jnp.square(yg), axis=-1, keepdims=True) + RMS_EPS)
    return (yg.reshape(b, seq, SSD_WIDTH) * norm_g).astype(proj.dtype)

def fox_group(proj, f_bias):
    b, seq, _ = proj.shape
    q, k, v, f = jnp.split(proj, [FOX_WIDTH, 2 * FOX_WIDTH, 3 * FOX_WIDTH], axis=-1)
    q = q.reshape(b, seq, FOX_HEADS, FOX_HEAD_DIM)
    k = k.reshape(b, seq, FOX_HEADS, FOX_HEAD_DIM)
    v = v.reshape(b, seq, FOX_HEADS, FOX_HEAD_DIM)
    log_f = jax.nn.log_sigmoid(f.astype(jnp.float32) + f_bias.astype(jnp.float32))
    cum_f = jnp.transpose(jnp.cumsum(log_f, axis=1), (0, 2, 1))
    scale = FOX_HEAD_DIM ** -0.5
    outs = []
    for i in range(seq // Q_BLOCK):
        q0, end = i * Q_BLOCK, (i + 1) * Q_BLOCK
        s = jnp.einsum("bqhd,bkhd->bhqk", q[:, q0:end], k[:, :end]).astype(jnp.float32) * scale
        s = s + cum_f[:, :, q0:end, None] - cum_f[:, :, None, :end]
        mask = jnp.arange(q0, end)[:, None] >= jnp.arange(end)[None, :]
        prob = jax.nn.softmax(jnp.where(mask, s, -jnp.inf), axis=-1)
        outs.append(jnp.einsum("bhqk,bkhd->bqhd", prob.astype(v.dtype), v[:, :end]))
    return jnp.concatenate(outs, axis=1).reshape(b, seq, FOX_WIDTH)

def shortconv_group(proj, conv_w):
    bg, cg, xin = jnp.split(proj, 3, axis=-1)
    return bg * causal_depthwise_conv(cg * xin, conv_w)

def modulate(x, shift, scale):
    return x * (1.0 + scale) + shift

def first_inputs(seed: int = 0) -> dict:
    key = jax.random.key(seed)
    ks = jax.random.split(key, 24)

    def nrm(k, shape, s):
        return jax.random.normal(k, shape, jnp.float32) * s

    dt0 = jnp.exp(jax.random.uniform(ks[12], (DEPTH, SSD_HEADS), jnp.float32,
                                     minval=math.log(1e-3), maxval=math.log(1e-1)))
    return {
        "x": nrm(ks[0], (BATCH, SEQ, D_MODEL), 1.0),
        "c": nrm(ks[1], (BATCH, D_MODEL), 1.0),
        "ln_in_g": 1.0 + nrm(ks[2], (D_MODEL,), 0.01),
        "ln_in_b": nrm(ks[3], (D_MODEL,), 0.01),
        "ada_w": nrm(ks[4], (DEPTH, D_MODEL, N_SUB * 3 * D_MODEL), 0.5 * D_MODEL ** -0.5),
        "ada_b": nrm(ks[5], (DEPTH, N_SUB * 3 * D_MODEL), 0.01),
        "ffn1_w_in": nrm(ks[6], (DEPTH, D_MODEL, 2 * D_FF), D_MODEL ** -0.5),
        "ffn1_w_out": nrm(ks[7], (DEPTH, D_FF, D_MODEL), BETA * D_FF ** -0.5),
        "mix_w_in": nrm(ks[8], (DEPTH, D_MODEL, D_IN_PROJ), D_MODEL ** -0.5),
        "mix_w_out": nrm(ks[9], (DEPTH, D_MIX, D_MODEL), BETA * D_MIX ** -0.5),
        "ssd_conv_w": nrm(ks[10], (DEPTH, SSD_CONV, SSD_CONV_DIM), SSD_CONV ** -0.5),
        "ssd_conv_b": nrm(ks[11], (DEPTH, SSD_CONV_DIM), 0.01),
        "ssd_dt_bias": dt0 + jnp.log(-jnp.expm1(-dt0)),
        "ssd_a_log": jnp.log(jax.random.uniform(ks[13], (DEPTH, SSD_HEADS), jnp.float32,
                                                 minval=1.0, maxval=16.0)),
        "ssd_d": 1.0 + nrm(ks[14], (DEPTH, SSD_HEADS), 0.01),
        "ssd_norm_g": 1.0 + nrm(ks[15], (DEPTH, SSD_WIDTH), 0.01),
        "fox_f_bias": jax.random.uniform(ks[16], (DEPTH, FOX_HEADS), jnp.float32,
                                         minval=1.0, maxval=5.0),
        "sconv_w": nrm(ks[17], (DEPTH, SCONV_K, SCONV_WIDTH), SCONV_K ** -0.5),
        "ffn2_w_in": nrm(ks[18], (DEPTH, D_MODEL, 2 * D_FF), D_MODEL ** -0.5),
        "ffn2_w_out": nrm(ks[19], (DEPTH, D_FF, D_MODEL), BETA * D_FF ** -0.5),
        "ln_g": 1.0 + nrm(ks[20], (DEPTH, N_SUB, D_MODEL), 0.01),
        "ln_b": nrm(ks[21], (DEPTH, N_SUB, D_MODEL), 0.01),
    }

def first_block(x, c, ln_in_g, ln_in_b, ada_w, ada_b, ffn1_w_in, ffn1_w_out,
              mix_w_in, mix_w_out, ssd_conv_w, ssd_conv_b, ssd_dt_bias, ssd_a_log,
              ssd_d, ssd_norm_g, fox_f_bias, sconv_w, ffn2_w_in, ffn2_w_out,
              ln_g, ln_b):
    b = x.shape[0]
    x = layer_norm(x, ln_in_g, ln_in_b)
    c_act = jax.nn.silu(c)
    for l in range(DEPTH):
        mod = (c_act @ ada_w[l] + ada_b[l]).reshape(b, N_SUB, 3, 1, D_MODEL)

        h = modulate(x, mod[:, 0, 0], mod[:, 0, 1])
        y = swiglu_ffn(h, ffn1_w_in[l], ffn1_w_out[l])
        x = layer_norm(ALPHA * x + 0.5 * mod[:, 0, 2] * y, ln_g[l, 0], ln_b[l, 0])

        h = modulate(x, mod[:, 1, 0], mod[:, 1, 1])
        proj = h @ mix_w_in[l]
        p_ssd, p_fox, p_sc = jnp.split(proj, [SSD_IN, SSD_IN + FOX_IN], axis=-1)
        y_ssd = mamba2_group(p_ssd, ssd_conv_w[l], ssd_conv_b[l], ssd_dt_bias[l],
                             ssd_a_log[l], ssd_d[l], ssd_norm_g[l])
        y_fox = fox_group(p_fox, fox_f_bias[l])
        y_sc = shortconv_group(p_sc, sconv_w[l])
        y = jnp.concatenate([y_ssd, y_fox, y_sc], axis=-1) @ mix_w_out[l]
        x = layer_norm(ALPHA * x + mod[:, 1, 2] * y, ln_g[l, 1], ln_b[l, 1])

        h = modulate(x, mod[:, 2, 0], mod[:, 2, 1])
        y = swiglu_ffn(h, ffn2_w_in[l], ffn2_w_out[l])
        x = layer_norm(ALPHA * x + 0.5 * mod[:, 2, 2] * y, ln_g[l, 2], ln_b[l, 2])
    return x


_first_inputs = first_inputs


def first_inputs(seed=0):
    import zlib

    import numpy as np

    out = dict(_first_inputs(seed))
    spreads = {}
    factors = {'ln_in_g': 22.481,
     'ln_in_b': 24.184,
     'ada_b': 8.0,
     'ssd_conv_b': 8.0,
     'ssd_a_log': 7.722,
     'ssd_d': 50.471,
     'ssd_norm_g': 52.766,
     'fox_f_bias': 22.672}
    for name, (base, spread) in spreads.items():
        noise = np.random.default_rng([zlib.crc32(name.encode()), seed]).standard_normal(out[name].shape)
        drawn = base * np.exp(spread * noise) if base else spread * noise
        out[name] = __import__('jax').numpy.asarray(drawn.astype(out[name].dtype))
    for name, factor in factors.items():
        out[name] = (out[name] * factor).astype(out[name].dtype)
    return out


_narrow_inputs = first_inputs


def first_inputs(seed=0):
    out = dict(_narrow_inputs(seed))
    wider = {'ssd_dt_bias': 4.27,
     'ssd_a_log': 12.0,
     'ssd_d': 3.34,
     'ssd_norm_g': 3.77,
     'fox_f_bias': 12.0}
    for name, times in wider.items():
        mean = out[name].mean()
        out[name] = (mean + times * (out[name] - mean)).astype(out[name].dtype)
    return out


GRID_W = 64
CTX_LEN = 256
N_MIXERS = 2
GQA_HEADS = 16
GQA_KV_HEADS = 4
GQA_GROUP = GQA_HEADS // GQA_KV_HEADS
GQA_HEAD_DIM = D_MODEL // GQA_HEADS
MLA_HEADS = 16
MLA_Q_RANK = (3 * D_MODEL) // 8
MLA_KV_RANK = D_MODEL // 4
MLA_NOPE_DIM = 64
MLA_ROPE_DIM = 32
MLA_V_DIM = 64
FFN_HIDDEN = 4 * D_MODEL
ROPE_THETA = 10000.0
NORM_EPS = 1e-6
DEEPNORM_ALPHA = (2.0 * DEPTH) ** 0.25
DEEPNORM_BETA = (8.0 * DEPTH) ** -0.25


def layer_norm_2(x, g, b):
    xf = x.astype(jnp.float32)
    mu = jnp.mean(xf, axis=-1, keepdims=True)
    var = jnp.mean(jnp.square(xf - mu), axis=-1, keepdims=True)
    return ((xf - mu) * lax.rsqrt(var + NORM_EPS) * g.astype(jnp.float32) + b.astype(jnp.float32)).astype(x.dtype)

def rms_norm(x, g):
    xf = x.astype(jnp.float32)
    ms = jnp.mean(jnp.square(xf), axis=-1, keepdims=True)
    return (xf * lax.rsqrt(ms + NORM_EPS) * g.astype(jnp.float32)).astype(x.dtype)

def grid_rope_tables(n_tok, rot_dim):
    rows = n_tok // GRID_W
    row = jnp.broadcast_to(jnp.arange(rows, dtype=jnp.float32)[:, None], (rows, GRID_W)).reshape(-1)
    col = jnp.broadcast_to(jnp.arange(GRID_W, dtype=jnp.float32)[None, :], (rows, GRID_W)).reshape(-1)
    axis_dim = rot_dim // 2
    inv_freq = ROPE_THETA ** (-jnp.arange(0, axis_dim, 2, dtype=jnp.float32) / axis_dim)
    ang_row = row[:, None] * inv_freq[None, :]
    ang_col = col[:, None] * inv_freq[None, :]
    return (jnp.cos(ang_row), jnp.sin(ang_row), jnp.cos(ang_col), jnp.sin(ang_col))

def rotate_axis(x, cos, sin):
    x1, x2 = jnp.split(x, 2, axis=-1)
    c = cos[:, None, :]
    s = sin[:, None, :]
    return jnp.concatenate([x1 * c - x2 * s, x2 * c + x1 * s], axis=-1)

def apply_grid_rope(x, tables):
    cr, sr, cc, sc = tables
    half = x.shape[-1] // 2
    xf = x.astype(jnp.float32)
    out = jnp.concatenate([rotate_axis(xf[..., :half], cr, sr), rotate_axis(xf[..., half:], cc, sc)], axis=-1)
    return out.astype(x.dtype)

def block_attention(q, k, v):
    b, sq, kvh, g, dk = q.shape
    nb = sq // Q_BLOCK
    scale = dk ** -0.5
    qb = jnp.moveaxis(q.reshape(b, nb, Q_BLOCK, kvh, g, dk), 1, 0)

    def one_block(qi):
        s = jnp.einsum('bqhgd,bkhd->bhgqk', qi, k, preferred_element_type=jnp.float32) * scale
        p = jax.nn.softmax(s, axis=-1).astype(v.dtype)
        return jnp.einsum('bhgqk,bkhe->bqhge', p, v)

    o = lax.map(one_block, qb)
    return jnp.moveaxis(o, 0, 1).reshape(b, sq, kvh * g * v.shape[-1])

def gqa_mixer(h_lat, h_ctx, w_qkv, q_norm, k_norm, w_o, rope, need_ctx):
    def project(h, rotate):
        b, n, _ = h.shape
        q, k, v = jnp.split(h @ w_qkv, [GQA_HEADS * GQA_HEAD_DIM, (GQA_HEADS + GQA_KV_HEADS) * GQA_HEAD_DIM], axis=-1)
        q = rms_norm(q.reshape(b, n, GQA_HEADS, GQA_HEAD_DIM), q_norm)
        k = rms_norm(k.reshape(b, n, GQA_KV_HEADS, GQA_HEAD_DIM), k_norm)
        v = v.reshape(b, n, GQA_KV_HEADS, GQA_HEAD_DIM)
        if rotate:
            q = apply_grid_rope(q, rope)
            k = apply_grid_rope(k, rope)
        return q.reshape(b, n, GQA_KV_HEADS, GQA_GROUP, GQA_HEAD_DIM), k, v

    q_lat, k_lat, v_lat = project(h_lat, True)
    q_ctx, k_ctx, v_ctx = project(h_ctx, False)
    k_all = jnp.concatenate([k_ctx, k_lat], axis=1)
    v_all = jnp.concatenate([v_ctx, v_lat], axis=1)
    y_lat = block_attention(q_lat, k_all, v_all) @ w_o
    y_ctx = block_attention(q_ctx, k_ctx, v_ctx) @ w_o if need_ctx else None
    return y_lat, y_ctx

def mla_mixer(h_lat, h_ctx, w_in, q_norm, kv_norm, w_uq, w_ukv, w_o, rope, need_ctx):
    def project(h, rotate):
        b, n, _ = h.shape
        cq, ckv, k_pe = jnp.split(h @ w_in, [MLA_Q_RANK, MLA_Q_RANK + MLA_KV_RANK], axis=-1)
        q = (rms_norm(cq, q_norm) @ w_uq).reshape(b, n, MLA_HEADS, MLA_NOPE_DIM + MLA_ROPE_DIM)
        q_nope, q_pe = jnp.split(q, [MLA_NOPE_DIM], axis=-1)
        kv = (rms_norm(ckv, kv_norm) @ w_ukv).reshape(b, n, MLA_HEADS, MLA_NOPE_DIM + MLA_V_DIM)
        k_nope, v = jnp.split(kv, [MLA_NOPE_DIM], axis=-1)
        k_pe = k_pe[:, :, None, :]
        if rotate:
            q_pe = apply_grid_rope(q_pe, rope)
            k_pe = apply_grid_rope(k_pe, rope)
        q = jnp.concatenate([q_nope, q_pe], axis=-1)[:, :, :, None, :]
        k = jnp.concatenate([k_nope, jnp.broadcast_to(k_pe, (b, n, MLA_HEADS, MLA_ROPE_DIM))], axis=-1)
        return q, k, v

    q_lat, k_lat, v_lat = project(h_lat, True)
    q_ctx, k_ctx, v_ctx = project(h_ctx, False)
    k_all = jnp.concatenate([k_ctx, k_lat], axis=1)
    v_all = jnp.concatenate([v_ctx, v_lat], axis=1)
    y_lat = block_attention(q_lat, k_all, v_all) @ w_o
    y_ctx = block_attention(q_ctx, k_ctx, v_ctx) @ w_o if need_ctx else None
    return y_lat, y_ctx

def sq_relu_mlp(h, w1, w2):
    return jnp.square(jax.nn.relu(h @ w1)) @ w2

def second_inputs(seed: int = 0) -> dict:
    key = jax.random.key(seed)
    ks = jax.random.split(key, 20)
    d = D_MODEL
    n_a = (DEPTH + N_MIXERS - 1) // N_MIXERS
    n_b = DEPTH // N_MIXERS

    def w(k, shape, fan_in, gain=1.0):
        return jax.random.normal(k, shape, jnp.float32) * (gain * fan_in ** -0.5)

    def gain_vec(k, shape):
        return 1.0 + 0.02 * jax.random.normal(k, shape, jnp.float32)

    qkv_cols = (GQA_HEADS + 2 * GQA_KV_HEADS) * GQA_HEAD_DIM
    mla_in_cols = MLA_Q_RANK + MLA_KV_RANK + MLA_ROPE_DIM
    return {
        "x": jax.random.normal(ks[0], (BATCH, SEQ, d), jnp.float32),
        "c": jax.random.normal(ks[1], (BATCH, d), jnp.float32),
        "ctx": jax.random.normal(ks[2], (BATCH, CTX_LEN, d), jnp.float32),
        "c_ctx": jax.random.normal(ks[3], (d,), jnp.float32),
        "w_ada": w(ks[4], (DEPTH, d, 6 * d), d),
        "b_ada": 0.02 * jax.random.normal(ks[5], (DEPTH, 6 * d), jnp.float32),
        "ln_g": gain_vec(ks[6], (DEPTH, 2, d)),
        "ln_b": 0.02 * jax.random.normal(ks[7], (DEPTH, 2, d), jnp.float32),
        "mlp_w1": w(ks[8], (DEPTH, d, FFN_HIDDEN), d),
        "mlp_w2": w(ks[9], (DEPTH, FFN_HIDDEN, d), FFN_HIDDEN, DEEPNORM_BETA),
        "gqa_w_qkv": w(ks[10], (n_a, d, qkv_cols), d),
        "gqa_q_norm": gain_vec(ks[11], (n_a, GQA_HEAD_DIM)),
        "gqa_k_norm": gain_vec(ks[12], (n_a, GQA_HEAD_DIM)),
        "gqa_w_o": w(ks[13], (n_a, GQA_HEADS * GQA_HEAD_DIM, d), GQA_HEADS * GQA_HEAD_DIM, DEEPNORM_BETA),
        "mla_w_in": w(ks[14], (n_b, d, mla_in_cols), d),
        "mla_q_norm": gain_vec(ks[15], (n_b, MLA_Q_RANK)),
        "mla_kv_norm": gain_vec(ks[16], (n_b, MLA_KV_RANK)),
        "mla_w_uq": w(ks[17], (n_b, MLA_Q_RANK, MLA_HEADS * (MLA_NOPE_DIM + MLA_ROPE_DIM)), MLA_Q_RANK),
        "mla_w_ukv": w(ks[18], (n_b, MLA_KV_RANK, MLA_HEADS * (MLA_NOPE_DIM + MLA_V_DIM)), MLA_KV_RANK),
        "mla_w_o": w(ks[19], (n_b, MLA_HEADS * MLA_V_DIM, d), MLA_HEADS * MLA_V_DIM, DEEPNORM_BETA),
    }

def second_block(x, c, ctx, c_ctx, w_ada, b_ada, ln_g, ln_b, mlp_w1, mlp_w2,
              gqa_w_qkv, gqa_q_norm, gqa_k_norm, gqa_w_o,
              mla_w_in, mla_q_norm, mla_kv_norm, mla_w_uq, mla_w_ukv, mla_w_o):
    n_tok = x.shape[1]
    rope_gqa = grid_rope_tables(n_tok, GQA_HEAD_DIM)
    rope_mla = grid_rope_tables(n_tok, MLA_ROPE_DIM)
    alpha = DEEPNORM_ALPHA
    silu_c = jax.nn.silu(c)
    silu_cc = jax.nn.silu(c_ctx)
    xc = ctx
    for i in range(DEPTH):
        need_ctx = i < DEPTH - 1
        mod_lat = (silu_c @ w_ada[i] + b_ada[i])[:, None, :]
        mod_ctx = silu_cc @ w_ada[i] + b_ada[i]
        sh_a, sc_a, g_a, sh_m, sc_m, g_m = jnp.split(mod_lat, 6, axis=-1)
        csh_a, csc_a, cg_a, csh_m, csc_m, cg_m = jnp.split(mod_ctx, 6, axis=-1)

        h_lat = x * (1.0 + sc_a) + sh_a
        h_ctx = xc * (1.0 + csc_a) + csh_a
        j = i // N_MIXERS
        if i % N_MIXERS == 0:
            y_lat, y_ctx = gqa_mixer(h_lat, h_ctx, gqa_w_qkv[j], gqa_q_norm[j], gqa_k_norm[j],
                                     gqa_w_o[j], rope_gqa, need_ctx)
        else:
            y_lat, y_ctx = mla_mixer(h_lat, h_ctx, mla_w_in[j], mla_q_norm[j], mla_kv_norm[j],
                                     mla_w_uq[j], mla_w_ukv[j], mla_w_o[j], rope_mla, need_ctx)

        x = layer_norm_2(alpha * x + g_a * y_lat, ln_g[i, 0], ln_b[i, 0])
        x = layer_norm_2(alpha * x + g_m * sq_relu_mlp(x * (1.0 + sc_m) + sh_m, mlp_w1[i], mlp_w2[i]),
                       ln_g[i, 1], ln_b[i, 1])
        if need_ctx:
            xc = layer_norm_2(alpha * xc + cg_a * y_ctx, ln_g[i, 0], ln_b[i, 0])
            xc = layer_norm_2(alpha * xc + cg_m * sq_relu_mlp(xc * (1.0 + csc_m) + csh_m, mlp_w1[i], mlp_w2[i]),
                            ln_g[i, 1], ln_b[i, 1])
    return x


def setup_inputs(seed=0):
    out = dict(first_inputs(seed))
    for name, value in second_inputs(seed + 1).items():
        if name != "x":
            out[name + "_2"] = value
    return out


def reference(
    x, c, ln_in_g, ln_in_b, ada_w, ada_b, ffn1_w_in, ffn1_w_out, mix_w_in, mix_w_out,
    ssd_conv_w, ssd_conv_b, ssd_dt_bias, ssd_a_log, ssd_d, ssd_norm_g, fox_f_bias, sconv_w,
    ffn2_w_in, ffn2_w_out, ln_g, ln_b, c_2, ctx_2, c_ctx_2, w_ada_2, b_ada_2, ln_g_2, ln_b_2,
    mlp_w1_2, mlp_w2_2, gqa_w_qkv_2, gqa_q_norm_2, gqa_k_norm_2, gqa_w_o_2, mla_w_in_2,
    mla_q_norm_2, mla_kv_norm_2, mla_w_uq_2, mla_w_ukv_2, mla_w_o_2,
):
    x = first_block(
        x, c, ln_in_g, ln_in_b, ada_w, ada_b, ffn1_w_in, ffn1_w_out, mix_w_in, mix_w_out,
        ssd_conv_w, ssd_conv_b, ssd_dt_bias, ssd_a_log, ssd_d, ssd_norm_g, fox_f_bias, sconv_w,
        ffn2_w_in, ffn2_w_out, ln_g, ln_b,
    )
    return second_block(
        x, c_2, ctx_2, c_ctx_2, w_ada_2, b_ada_2, ln_g_2, ln_b_2, mlp_w1_2, mlp_w2_2,
        gqa_w_qkv_2, gqa_q_norm_2, gqa_k_norm_2, gqa_w_o_2, mla_w_in_2, mla_q_norm_2,
        mla_kv_norm_2, mla_w_uq_2, mla_w_ukv_2, mla_w_o_2,
    )


_drawn_inputs = setup_inputs


def setup_inputs(seed=0):
    import zlib

    import numpy as np

    out = dict(_drawn_inputs(seed))
    spreads = {}
    factors = {'fox_f_bias': 4.432,
     'ctx_2': 4.912,
     'gqa_q_norm_2': 8.0,
     'gqa_k_norm_2': 8.0,
     'mla_q_norm_2': 8.0,
     'mla_kv_norm_2': 8.0}
    for name, (base, spread) in spreads.items():
        noise = np.random.default_rng([zlib.crc32(name.encode()), seed]).standard_normal(out[name].shape)
        drawn = base * np.exp(spread * noise) if base else spread * noise
        out[name] = __import__('jax').numpy.asarray(drawn.astype(out[name].dtype))
    for name, factor in factors.items():
        out[name] = (out[name] * factor).astype(out[name].dtype)
    return out
```

```python
from contextlib import ExitStack

import concourse.bass as bass
from concourse import mybir

F32 = mybir.dt.float32
F32R = mybir.dt.float32r
ALU = mybir.AluOpType
ACT = mybir.ActivationFunctionType
AX_X = mybir.AxisListType.X

P = 128
D = 1024
DC = D // P
SEQ = 512
CTX = 256
KEYS = SEQ + CTX
DEPTH = 2
FF = 2816
FF_GROUPS = (12, 10)
FF2 = 4096
G2 = 8
SLOT = 2048
RAW = 4
UNROLL = 4
ALPHA = float((2 * DEPTH) ** 0.25)
LN_EPS, RMS_EPS, NORM_EPS = 1e-5, 1e-5, 1e-6
SSD_H, SSD_P = 8, 64
FOX_H, HD = 4, 64
XBC, Z, FQ, FK, CG, XIN, BG = 0, 8, 12, 14, 16, 18, 20
NPROJ = 22
NEG = -1e30
GQA_KV = 4
HEADS = 16
ROPE = 32
QC, KVC = 3, 2
MOD = 24
ADA_UNITS = MOD // 2
LOG1P = [1.0 / (2 * k + 1) for k in range(8)]


class Linear:

    def __init__(self, name, n, tpu, kc, evac, out=P, ada=None, streams=("lat",), src="h", row=0, dst=None):
        self.name, self.n, self.tpu, self.kc, self.evac, self.out = name, n, tpu, kc, evac, out
        self.ada, self.streams, self.src, self.row, self.dst = ada, streams, src, row, dst
        self.width = tpu * kc * out
        self.spu = 2 if ada else 1
        self.tiles = row if row else tpu
        self.events = 1 if evac == "gateup" else self.tiles
        self.nbuf = 4 if row or (self.tiles >= 2 and len(streams) == 1) else 2


def schedule(stop):
    both = ("lat", "ctx")
    s = [("ada0",), ("ln", "in", "lat", LN_EPS), ("mod", 0, "lat")]

    def lin(*a, **k):
        s.append(("lin", Linear(*a, **k)))

    def ffn(l, which, ada):
        for g, nc in enumerate(FF_GROUPS):
            lin(f"ffn{which}_in_{l}_{g}", nc, 2, DC, "gateup", ada=ada if g == 0 else None)
            lin(f"ffn{which}_out_{l}_{g}", DC, 1, nc, "resid", src="hid")

    for l in range(DEPTH):
        ffn(l, 1, (3 * l + 1, 0))
        s += [("ln", f"b1_{l}_0", "lat", LN_EPS), ("mod", 3 * l + 1, "lat")]
        if stop == 1:
            return s
        lin(f"mix_in_{l}", NPROJ // 2, 2, DC, "copy", ada=(3 * l + 2, 0), dst="proj")
        lin(f"mix_v_{l}", 1, 1, DC, "rowcopy", out=FOX_H * HD, ada=(3 * l + 2, NPROJ // 2), row=4, dst="vrow")
        lin(f"mix_dt_{l}", 1, 1, DC, "rowcopy", out=SSD_H + FOX_H, row=4, dst="dtrow")
        s.append(("mixer", l))
        lin(f"mix_out_{l}", DC // 2, 2, DC, "resid")
        s += [("ln", f"b1_{l}_1", "lat", LN_EPS), ("mod", 3 * l + 2, "lat")]
        if stop == 2:
            return s
        ffn(l, 2, (3 * l + 3, 0))
        s += [("ln", f"b1_{l}_2", "lat", LN_EPS), ("mod", 3 * l + 3, "lat")]
        if stop == 3:
            return s
    s.append(("mod", 6, "ctx"))
    if stop == 4:
        return s
    lin("gqa_q", DC // 2, 2, DC, "copy", streams=both, dst="q")
    lin("gqa_k", 1, 2, DC, "copy", streams=both, dst="k")
    lin("gqa_v", 1, 1, DC, "rowcopy", out=GQA_KV * HD, row=6, streams=both, dst="gv")
    s.append(("gqa",))
    lin("gqa_o", DC // 2, 2, DC, "resid", streams=both)
    for st in both:
        s += [("ln", "b2_0_0", st, NORM_EPS), ("mod", 7, st)]
    if stop == 5:
        return s
    for g in range(FF2 // P // G2):
        lin(f"mlp_in_0_{g}", G2 // 2, 2, DC, "relu2", streams=both, ada=(8, 4 * g) if g < 3 else None)
        lin(f"mlp_out_0_{g}", DC // 2, 2, G2, "resid", src="hid", streams=both, ada=(9, 4 * g) if g < 3 else None)
    for st in both:
        s += [("ln", "b2_0_1", st, NORM_EPS), ("mod", 8, st)]
    if stop == 6:
        return s
    lin("mla_ckv", 1, KVC, DC, "copy", streams=both, dst="ckv")
    lin("mla_kpe", 1, 1, DC, "copy", streams=both, dst="kpe")
    lin("mla_cq", QC, 1, DC, "copy", dst="cq")
    s.append(("mla_norm",))
    lin("mla_k", 1, 8, KVC, "copy", streams=both, src="ckvn", dst="mk")
    lin("mla_v", 2, 1, KVC, "rowcopy", out=512, row=6, streams=both, src="ckvn", dst="mv")
    lin("mla_q", 2, 4, QC, "copy", src="cqn", dst="mq")
    lin("mla_qpe", 1, 4, QC, "copy", src="cqn", dst="qpe")
    s.append(("mla",))
    lin("mla_o", DC // 2, 2, DC, "resid", src="y2")
    s += [("ln", "b2_1_0", "lat", NORM_EPS), ("mod", 9, "lat")]
    if stop == 7:
        return s
    for g in range(FF2 // P // G2):
        lin(f"mlp_in_1_{g}", G2 // 2, 2, DC, "relu2")
        lin(f"mlp_out_1_{g}", DC // 2, 2, G2, "resid", src="hid")
    s.append(("ln", "b2_1_1", "lat", NORM_EPS))
    return s


def number(sched):
    units = tiles = events = stream = ada = 0
    unit_tiles = []
    occupant = []
    ada_done = {}
    events = 4

    def take_ada(which, n):
        nonlocal ada
        occupant.append(("ada", ada))
        ada += 1
        ada_done[which] = ada

    for item in sched:
        if item[0] == "ada0":
            for i in range(ADA_UNITS):
                take_ada(0, i)
        elif item[0] == "mixer" and item[1] == DEPTH - 1:
            for i in range(ADA_UNITS):
                take_ada(7, i)
        elif item[0] == "lin":
            ln = item[1]
            ln.g0, ln.t0, ln.e0, ln.G0, ln.a0 = units, tiles, events, len(occupant), ada
            for i in range(ln.n):
                occupant.append(("main", units))
                if ln.ada:
                    take_ada(ln.ada[0], ln.ada[1] + i)
                units += 1
                tiles += ln.tiles
                unit_tiles.append(tiles)
            events += ln.n * ln.events
    return unit_tiles, occupant, ada_done


def steps(eng, lo, hi):
    full = (hi - lo) // UNROLL
    first = 0
    if full >= 2:
        with eng.Fori(0, full) as it:
            for u in range(UNROLL):
                yield it, u, it * UNROLL + (lo + u)
        first = full * UNROLL
    for i in range(first, hi - lo):
        yield i // UNROLL, i % UNROLL, lo + i


def at(i, n=1):
    return bass.ds(i, n)


def param_table():
    cols, n = {}, 0

    def add(name, width):
        nonlocal n
        cols[name] = (n, width)
        n += width

    add("c1", DC)
    add("c2", 2 * DC)
    for m in range(10):
        add(f"ada_b_{m}", MOD)
    for name in ["in"] + [f"b1_{l}_{i}" for l in range(DEPTH) for i in range(3)] + \
            [f"b2_{l}_{i}" for l in range(DEPTH) for i in range(2)]:
        add(f"ln_g_{name}", DC)
        add(f"ln_b_{name}", DC)
    for l in range(DEPTH):
        add(f"conv_w_{l}", 8 * 4)
        add(f"conv_b_{l}", 8)
        add(f"ssd_d_{l}", 4)
        add(f"norm_g_{l}", 4)
        add(f"sconv_w_{l}", 2 * 3)
        add(f"dt_bias_{l}", SSD_H + FOX_H)
        add(f"a_log_{l}", SSD_H)
    add("q_norm", 1)
    add("k_norm", 1)
    add("mq_norm", QC)
    add("mkv_norm", KVC)
    return cols, n


def build(nc, t_in, out, stop):
    sched = schedule(stop)
    unit_tiles, occupant, ada_done = number(sched)
    cols, n_params = param_table()

    with ExitStack() as ctx:
        arena_bytes = 212800
        arena = ctx.enter_context(nc.sbuf_tensor("arena", [P, arena_bytes // 4], F32))
        base = 16512
        used = {}

        def place(name, shape, dt, offset):
            size = 4
            for d in shape[1:]:
                size *= d
            used[name] = (offset, offset + size)
            assert offset + size <= arena_bytes, (name, offset + size)
            return nc.alloc_sbuf_tensor_at(name, shape, dt, offset=base + offset)

        def after(*names):
            return (max(used[n][1] for n in names) + 31) // 32 * 32

        def sem(name):
            return ctx.enter_context(nc.semaphore(name))

        x_lat = place("x_lat", [P, DC, SEQ], F32, 0)
        h_hi = place("h_hi", [P, DC, SEQ], F32R, after("x_lat"))
        h_lo = place("h_lo", [P, DC, SEQ], F32R, after("h_hi"))
        raw = place("raw", [P, RAW, SLOT], F32, after("h_lo"))
        w_hi = place("w_hi", [P, 2, SLOT], F32R, after("raw"))
        w_lo = place("w_lo", [P, 2, SLOT], F32R, after("w_hi"))
        par = place("par", [P, n_params], F32, after("w_lo"))
        ident = place("ident", [P, P], F32, after("par"))
        ones = place("ones", [P, P], F32, after("ident"))
        tri = place("tri", [P, P], F32, after("ones"))
        past = place("past", [P, 4, P], F32, after("tri"))
        negmask = place("negmask", [P, P], F32, after("past"))
        blocks = place("blocks", [P, P], F32, after("negmask"))
        swaps = place("swaps", [P, 2, P], F32, after("blocks"))
        mean_w = place("mean_w", [P, 1], F32, after("swaps"))
        c_act = place("c_act", [P, 3 * DC], F32, after("mean_w"))
        mod_lat = place("mod_lat", [P, MOD], F32, after("c_act"))
        mod_ctx = place("mod_ctx", [P, MOD], F32, after("mod_lat"))
        dev = place("dev", [P, 4], F32, after("mod_ctx"))
        rstd = place("rstd", [P, 4], F32, after("dev"))
        eps_t = place("eps_t", [P, 3], F32, after("rstd"))
        nmax = place("nmax", [P, HEADS], F32, after("eps_t"))
        psumr = place("psumr", [P, HEADS], F32, after("nmax"))
        ctx0 = (after("psumr") + 63) // 64 * 64
        x_ctx = place("x_ctx", [P, DC, CTX], F32, ctx0)
        hc_hi = place("hc_hi", [P, DC, CTX], F32R, after("x_ctx"))
        hc_lo = place("hc_lo", [P, DC, CTX], F32R, after("hc_hi"))
        A = after("hc_lo")
        hid_hi = place("hid_hi", [P, 12, SEQ], F32R, A)
        hid_lo = place("hid_lo", [P, 12, SEQ], F32R, after("hid_hi"))
        hid2_hi = place("hid2_hi", [P, G2, SEQ], F32R, A)
        hid2_lo = place("hid2_lo", [P, G2, SEQ], F32R, after("hid2_hi"))
        hidc_hi = place("hidc_hi", [P, G2, CTX], F32R, after("hid2_lo"))
        hidc_lo = place("hidc_lo", [P, G2, CTX], F32R, after("hidc_hi"))
        gate_t = place("gate_t", [P, 2, SEQ], F32, after("hid_lo"))
        val_t = place("val_t", [P, 2, SEQ], F32, after("gate_t"))
        relu_t = place("relu_t", [P, 2, KEYS], F32, after("hidc_lo"))
        sq = place("sq", [P, DC, SEQ], F32, A)
        h32 = place("h32", [P, 4, SEQ], F32, after("sq"))
        diag = place("diag", [P, 2, 4, P], F32, after("h32"))
        proj = place("proj", [P, NPROJ, SEQ], F32, A)
        vrow = place("vrow", [P, 4, FOX_H * HD], F32, after("proj"))
        xrow = place("xrow", [P, 4, SSD_H * SSD_P], F32, after("vrow"))
        brow = place("brow", [P, 4, 2 * P], F32, after("xrow"))
        dtrow = place("dtrow", [P, 4, 12], F32, after("brow"))
        sp = {n: place(f"sp_{n}", [P, 4, 12], F32, after("dtrow") + 192 * i)
              for i, n in enumerate(["v", "n", "e", "d", "z", "z2", "p", "dt"])}
        a_row = place("a_row", [P, 4, SSD_H], F32, after("sp_dt"))
        logf = place("logf", [P, 4, FOX_H], F32, after("a_row"))
        a_head = place("a_head", [P, SSD_H], F32, after("logf"))
        cacc = place("cacc", [P, 4, SEQ], F32, used["h_hi"][0])
        fcum = place("fcum", [P, 4, SEQ], F32, used["h_lo"][0])
        s_names = ["am", "ab", "lmat", "emat", "mmat", "cdec"]
        ss = {n: place(f"ss_{n}", [P, 4, P], F32, ctx0 + 2048 * i) for i, n in enumerate(s_names)}
        xdt = place("xdt", [P, 4, SSD_P], F32, after("ss_cdec"))
        xdec = place("xdec", [P, 4, SSD_P], F32, after("xdt"))
        state = place("state", [P, 2, 4 * SSD_P], F32, after("xdec"))
        cbm = place("cbm", [P, P], F32, after("state"))
        decs = place("decs", [P, 8], F32, after("cbm"))
        fprob = place("fprob", [P, SEQ], F32, after("decs"))
        fprobT = place("fprobT", [P, 4, P], F32, after("fprob"))
        assert after("fprobT") <= A
        q_t = place("q_t", [P, DC, KEYS], F32, A)
        k_t = place("k_t", [P, 2, KEYS], F32, after("q_t"))
        gv = place("gv", [P, 6, GQA_KV * HD], F32, after("k_t"))
        gp = place("gp", [P, 2, KEYS], F32, after("gv"))
        gpt = place("gpt", [P, 2, KEYS], F32, after("gp"))
        gyrow = place("gyrow", [P, D], F32, after("gpt"))
        gcos = place("gcos", [P, 2, SEQ], F32, after("gyrow"))
        gqs = place("gqs", [P, DC, P], F32, after("gcos"))
        mk = place("mk", [P, DC, KEYS], F32, A)
        mv = place("mv", [P, 6, D], F32, after("mk"))
        kpe = place("kpe", [P, KEYS], F32, after("mv"))
        mcos = place("mcos", [P, 2, SEQ], F32, after("kpe"))
        mp = place("mp", [P, 2, KEYS], F32, ctx0)
        mpt = place("mpt", [P, 2, KEYS], F32, after("mp"))
        myrow = place("myrow", [P, D], F32, after("mpt"))
        msq = place("msq", [P, QC + KVC, KEYS], F32, A)
        msd = place("msd", [P, 2, KEYS], F32, after("msq"))
        cq = place("cq", [P, QC, SEQ], F32, used["mv"][0])
        ckv = place("ckv", [P, KVC, KEYS], F32, after("cq"))
        mq = place("mq", [P, DC, SEQ], F32, used["h_hi"][0])
        qpe = place("qpe", [P, 4, SEQ], F32, after("mq"))
        mqs = place("mqs", [P, DC, P], F32, after("qpe"))
        qpes = place("qpes", [P, 4, P], F32, after("mqs"))
        assert after("qpes") <= used["raw"][0]
        cqn_hi = place("cqn_hi", [P, QC, SEQ], F32R, ctx0)
        cqn_lo = place("cqn_lo", [P, QC, SEQ], F32R, after("cqn_hi"))
        ckvn_hi = place("ckvn_hi", [P, KVC, KEYS], F32R, after("cqn_lo"))
        ckvn_lo = place("ckvn_lo", [P, KVC, KEYS], F32R, after("ckvn_hi"))
        assert after("ckvn_lo") <= A
        y2_hi = place("y2_hi", [P, DC, SEQ], F32R, A)
        y2_lo = place("y2_lo", [P, DC, SEQ], F32R, after("y2_hi"))

        ps = ctx.enter_context(nc.psum_tensor("ps", [P, 8, SEQ], F32))
        B_MEAN, B_RSTD, B_STAT, B_ADA = 4, 5, 6, 7

        X = {"lat": x_lat, "ctx": x_ctx}
        H = {"lat": (h_hi, h_lo), "ctx": (hc_hi, hc_lo)}
        HID = {"lat": (hid2_hi, hid2_lo), "ctx": (hidc_hi, hidc_lo)}
        MODT = {"lat": mod_lat, "ctx": mod_ctx}
        NT = {"lat": SEQ, "ctx": CTX}
        COL0 = {"lat": 0, "ctx": SEQ}

        def pc(name, i=0, n=1):
            return par[:, cols[name][0] + i:cols[name][0] + i + n]

        def operand(ln, st):
            if ln.src == "hid":
                return HID[st] if ln.name.startswith("mlp") else (hid_hi, hid_lo)
            if ln.src == "ckvn":
                return ckvn_hi[:, :, COL0[st]:COL0[st] + NT[st]], ckvn_lo[:, :, COL0[st]:COL0[st] + NT[st]]
            return {"h": H[st], "cqn": (cqn_hi, cqn_lo), "y2": (y2_hi, y2_lo)}[ln.src]

        def dest(ln, st, i):
            c0, n = COL0[st], NT[st]
            return {"proj": lambda: proj[:, at(i), :], "q": lambda: q_t[:, at(i), c0:c0 + n],
                    "k": lambda: k_t[:, at(i), c0:c0 + n], "ckv": lambda: ckv[:, at(i), c0:c0 + n],
                    "kpe": lambda: kpe[:, c0:c0 + n].unsqueeze(1), "cq": lambda: cq[:, at(i), :],
                    "mk": lambda: mk[:, at(i), c0:c0 + n], "mq": lambda: mq[:, at(i), :],
                    "qpe": lambda: qpe[:, at(i), :]}[ln.dst]()

        def row_dest(ln, unit, t):
            return {"vrow": lambda: vrow[:, t, :], "dtrow": lambda: dtrow[:, t, :], "gv": lambda: gv[:, t, :],
                    "mv": lambda: mv[:, t, unit * 512:(unit + 1) * 512]}[ln.dst]()

        def tile_bank(ln, tile, st):
            return tile % ln.nbuf + (2 if st == "ctx" else 0)

        s_par = sem("params_loaded")
        s_x = sem("x_loaded")
        s_rope = sem("rope_tables_loaded")
        s_raw = [sem(f"weights_loaded_{i}") for i in range(RAW)]
        s_out = sem("out_stored")
        s_const = sem("constants_ready")
        s_cact = sem("c_activated")
        s_whi = sem("weights_rounded")
        s_wlo = sem("weights_split")
        s_tile = sem("tile_ready")
        s_ada = sem("ada_unit_used")
        s_evac = sem("tile_evacuated")
        s_gate = sem("gate_activated")
        s_hidhi = sem("hidden_rounded")
        s_hid = sem("hidden_split")
        s_sum = sem("ln_sums")
        s_diag = sem("ln_diagonals")
        s_bc = sem("ln_broadcasts")
        s_cent = sem("ln_centred")
        s_sq = sem("ln_squared")
        s_dev = sem("ln_deviation")
        s_rstd = sem("ln_rstd")
        s_scal = sem("ln_scaled")
        s_aff = sem("ln_affine")
        s_mod = sem("modulation_steps")
        s_h32 = sem("h_modulated")
        s_hhi = sem("h_rounded")
        s_hlo = sem("h_split")
        s_xa = sem("x_times_alpha")

        m_sp = sem("softplus_steps")
        m_spe = sem("softplus_exp")
        m_ahd = sem("a_head_exp")
        m_conv = sem("conv_taps")
        m_silu = sem("conv_activated")
        m_tr = sem("rows_transposed")
        m_rows = sem("rows_copied")
        m_ab = sem("ssd_a_spread")
        m_am = sem("ssd_a_masked")
        m_pre = sem("ssd_exponents")
        m_sexp = sem("ssd_decays")
        m_mul = sem("ssd_operands")
        m_y = sem("ssd_products")
        m_sev = sem("ssd_evacuated")
        m_z = sem("z_activated")
        m_gate = sem("ssd_gated")
        m_ysq = sem("ssd_squared")
        m_ms = sem("ssd_mean_squares")
        m_sd = sem("ssd_deviations")
        m_rn = sem("ssd_normed")
        m_qs = sem("fox_q_scaled")
        m_fg = sem("fox_forget_rows")
        m_fs = sem("fox_scores")
        m_fmax = sem("fox_maxima")
        m_fp = sem("fox_exp")
        m_fn = sem("fox_normed")
        m_ftr = sem("fox_transposed")
        m_fpt = sem("fox_probs_copied")
        m_fo = sem("fox_outputs")
        m_fy = sem("fox_evacuated")
        m_sc = sem("sconv_steps")
        n_sq = sem("norm_squared")
        n_ms = sem("norm_mean_squares")
        n_sd = sem("norm_deviations")
        n_out = sem("normed")
        r_sw = sem("rope_swapped")
        r_out = sem("rope_steps")
        t_q = sem("att_queries_staged")
        t_s = sem("att_scores")
        t_max = sem("att_maxima")
        t_p = sem("att_exp")
        t_tr = sem("att_transposed")
        t_pt = sem("att_probs_copied")
        t_o = sem("att_outputs")
        t_row = sem("att_rows")
        t_yt = sem("att_rows_transposed")
        t_done = sem("att_queries_done")

        SEV = []
        for c in range(4):
            for g in range(2):
                SEV.append((SEV[-1] + last if SEV else 0))
                last = 2 + (1, 2, 2, 0)[c]
        SEV.append(SEV[-1] + last)
        PAIRS = ((4, 5), (6, 7), (0, 1), (2, 3))
        NSP = 20
        NSC = 2 + 6 + 2

        def flat(bank):
            return ps[:, bank:bank + 2, :].rearrange("p a t -> p (a t)")[:, 0:KEYS]

        ATT = {"gqa": dict(q=q_t, qs=gqs, k=k_t, v=gv, p=gp, pt=gpt, row=gyrow, scale=HD ** -0.5,
                           runs=[(SEQ // P, 0, 0, KEYS), (CTX // P, SEQ, SEQ, CTX)]),
               "mla": dict(q=mq, qs=mqs, k=mk, v=mv, p=mp, pt=mpt, row=myrow, scale=(HD + ROPE) ** -0.5,
                           runs=[(SEQ // P, 0, 0, KEYS)])}
        GQA_JOBS = [(q_t, j, "q_norm") for j in range(DC)] + [(k_t, j, "k_norm") for j in range(2)]

        early = {}
        for j, item in enumerate(sched):
            if item[0] == "ln" and sched[j - 1][0] == "lin":
                nxt = next((i for i in range(j, len(sched)) if sched[i][0] not in ("ln", "mod")), None)
                if nxt is not None and sched[nxt][0] == "lin":
                    early[j] = nxt

        class Walk:

            def __init__(self):
                self.ln = self.mod = self.mixer = 0
                self.hid = 0
                self.h_chunks = 0
                self.att = 0
                self.nsq = self.nms = self.nout = self.rope = 0
                self.events = 4

        def raw_ready(eng, g, lo_u, it, spu, o=0):
            eng.wait_ge(s_raw[g % RAW], 16 * (g // RAW + 1) + it * (16 * spu))

        block = ctx.enter_context(nc.Block())

        @block.sync
        def _(eng):
            eng.dma_start(par[:, :], t_in["params"]).then_inc(s_par, 16)
            eng.dma_start(swaps[:, :, :], t_in["swaps"]).then_inc(s_par, 16)
            eng.dma_start(x_lat[:, :, :], t_in["xT"].rearrange("(c p) t -> p c t", p=P)).then_inc(s_x, 16)

            def slot_free(n):
                if n >= RAW:
                    kind, i = occupant[n - RAW]
                    eng.wait_ge(s_wlo if kind == "main" else s_ada, i + 1)

            def load_ada(which, i, slot, dyn=None):
                eng.dma_start(raw[:, slot, :], t_in[f"ada_{which}"][at(i)].rearrange("a p w -> p (a w)"))\
                   .then_inc(s_raw[slot], 16)

            n = 0
            ctx_loaded = False
            for item in sched:
                if item[0] == "ada0" or (item[0] == "mixer" and item[1] == 1):
                    which = 0 if item[0] == "ada0" else 7
                    for i in range(ADA_UNITS):
                        slot_free(n)
                        load_ada(which, i, n % RAW)
                        n += 1
                elif item[0] == "lin":
                    ln = item[1]
                    peel = min(ln.n, RAW // ln.spu)
                    w = t_in[ln.name]

                    def load(i, g):
                        eng.dma_start(raw[:, g % RAW, 0:ln.width], w[at(i)].rearrange("a p w -> p (a w)"))\
                           .then_inc(s_raw[g % RAW], 16)

                    for i in range(peel):
                        g = n + i * ln.spu
                        slot_free(g)
                        load(i, g)
                        if ln.ada:
                            slot_free(g + 1)
                            load_ada(ln.ada[0], ln.ada[1] + i, (g + 1) % RAW)
                    for it, u, i in steps(eng, peel, ln.n):
                        g = n + (peel + u) * ln.spu
                        eng.wait_ge(s_wlo, i + (ln.g0 - peel + 1))
                        load(i, g)
                        if ln.ada:
                            eng.wait_ge(s_ada, i + (ln.a0 - peel + 1))
                            load_ada(ln.ada[0], i + ln.ada[1], (g + 1) % RAW)
                    n += ln.n * ln.spu
                elif item[0] == "mod" and item[2] == "ctx" and not ctx_loaded:
                    pass
                if item[0] == "lin" and item[1].name == "mix_out_1":
                    ln = item[1]
                    eng.wait_ge(s_tile, ln.t0 + 1)
                    eng.dma_start(x_ctx[:, :, :], t_in["ctxT"].rearrange("(c p) t -> p c t", p=P)).then_inc(s_x, 16)
                if item[0] == "lin" and item[1].name == "gqa_k":
                    eng.wait_ge(s_tile, item[1].t0 + 1)
                    eng.dma_start(gcos[:, :, :], t_in["rope_gqa"]).then_inc(s_rope, 16)
                if item[0] == "lin" and item[1].name == "mla_cq":
                    eng.wait_ge(s_tile, item[1].t0 + 1)
                    eng.dma_start(mcos[:, :, :], t_in["rope_mla"]).then_inc(s_rope, 16)
            n_ln = sum(i[0] == "ln" for i in sched)
            last_ln = max(j for j, i in enumerate(sched) if i[0] == "ln")
            n_aff = sum(DC for i in sched if i[0] == "ln")
            eng.wait_ge(s_aff, n_aff)
            if stop:
                eng.wait_ge(s_xa, sum(DC for i in sched if i[0] == "mod"))
            eng.dma_start(out.rearrange("(c p) t -> p c t", p=P), x_lat[:, :, :]).then_inc(s_out, 16)
            eng.wait_ge(s_out, 16)

        @block.gpsimd
        def _(eng):
            n = [0]

            def const(ins):
                ins.then_inc(s_const, 1)
                n[0] += 1

            const(eng.memset(ones[:, :], 1.0))
            const(eng.memset(ident[:, :], 0.0))
            const(eng.memset(negmask[:, :], 0.0))
            const(eng.memset(blocks[:, :], 0.0))
            const(eng.memset(past[:, :, :], 1.0))
            const(eng.memset(mean_w[:, :], 1.0 / D))
            for i, e in enumerate((LN_EPS, RMS_EPS, NORM_EPS)):
                const(eng.memset(eps_t[:, i:i + 1], e))
            eng.wait_ge(s_const, n[0])
            const(eng.affine_select(out=ident[:, :], in_=ident[:, :], compare_op=ALU.not_equal, fill=1.0, base=0,
                                    pattern=[[-1, P]], channel_multiplier=1))
            const(eng.affine_select(out=tri[:, :], in_=ones[:, :], compare_op=ALU.is_ge, fill=0.0, base=0,
                                    pattern=[[1, P]], channel_multiplier=-1))
            const(eng.affine_select(out=past[:, 3, :], in_=past[:, 3, :], compare_op=ALU.is_gt, fill=0.0, base=0,
                                    pattern=[[-1, P]], channel_multiplier=1))
            const(eng.affine_select(out=negmask[:, :], in_=negmask[:, :], compare_op=ALU.is_ge, fill=NEG, base=0,
                                    pattern=[[-1, P]], channel_multiplier=1))
            for b in range(2):
                eng.wait_ge(s_const, n[0])
                const(eng.memset(blocks[b * HD:(b + 1) * HD, b * HD:(b + 1) * HD], 1.0))
            w = Walk()
            for item in sched:
                if item[0] == "mod":
                    x, h0 = X[item[2]], DC * w.mod
                    for k in range(DC):
                        eng.wait_ge(s_h32, h0 + k + 1)
                        eng.tensor_scalar(x[:, k, :], x[:, k, :], ALPHA, None, ALU.mult).then_inc(s_xa, 1)
                    w.mod += 1
                elif item[0] == "mixer":
                    b = 8 * w.mixer
                    eng.wait_ge(m_sp, NSP * (w.mixer + 1))
                    for it in range(8):
                        c, g = divmod(it, 2)
                        if it or w.mixer:
                            eng.wait_ge(m_pre, b + it)
                        eng.tensor_copy(ss["ab"][:, :, :], a_row[:, c, 4 * g:4 * g + 4].unsqueeze(2)
                                        .broadcast_to([P, 4, P])).then_inc(m_ab, 1)
                    w.mixer += 1

        N_CONST = 6 + 3 + 4 + 2

        @block.scalar
        def _(eng):
            w = Walk()
            eng.wait_ge(s_par, 32)
            eng.wait_ge(s_const, N_CONST)
            eng.activation(c_act[:, 0:DC], pc("c1", 0, DC), ACT.Silu).then_inc(s_cact, 1)
            eng.activation(c_act[:, DC:3 * DC], pc("c2", 0, 2 * DC), ACT.Silu).then_inc(s_cact, 1)

            def round_weights(ln, i, it, pos):
                G = ln.G0 + pos * ln.spu
                raw_ready(eng, G, 0, it, ln.spu)
                slot = (ln.g0 + pos) % 2
                eng.activation(w_hi[:, slot, 0:ln.width], raw[:, G % RAW, 0:ln.width], ACT.Copy).then_inc(s_whi, 1)

            def prologue(ln):
                for i in range(min(2, ln.n)):
                    if ln.g0 + i >= 2:
                        eng.wait_ge(s_tile, unit_tiles[ln.g0 + i - 2])
                    round_weights(ln, i, 0, i)

            def evacuate(ln, i, it, pos):
                if ln.evac == "gateup":
                    t = w.hid + i
                    eng.wait_ge(s_tile, i * 2 + (ln.t0 + 2))
                    eng.activation(gate_t[:, pos % 2, 0:SEQ], ps[:, tile_bank(ln, 2 * pos, "lat"), :], ACT.Silu)\
                       .then_inc(s_gate, 1)
                    eng.wait_ge(s_evac, i + (ln.e0 + 1))
                    eng.activation(hid_hi[:, at(i), :], val_t[:, pos % 2, 0:SEQ].unsqueeze(1), ACT.Copy)\
                       .then_inc(s_hidhi, 1)
                elif ln.evac == "relu2":
                    for q in range(2):
                        eng.wait_ge(s_tile, i * 2 + (ln.t0 + q + 1))
                        eng.wait_ge(s_hid, i * 2 + (w.hid + q - 1))
                        for st in ln.streams:
                            a = eng.activation(relu_t[:, q, COL0[st]:COL0[st] + NT[st]],
                                               ps[:, tile_bank(ln, 2 * pos + q, st), 0:NT[st]], ACT.Relu)
                        a.then_inc(s_gate, 1)
                        eng.wait_ge(s_evac, i * 2 + (ln.e0 + q + 1))
                        for st in ln.streams:
                            a = eng.activation(HID[st][0][:, at(i * 2 + q), :],
                                               relu_t[:, q, COL0[st]:COL0[st] + NT[st]].unsqueeze(1), ACT.Copy)
                        a.then_inc(s_hidhi, 1)

            def linear(ln):
                lag = min(2, ln.n)
                for it, u, i in steps(eng, lag, ln.n):
                    eng.wait_ge(s_tile, (i - 2) * ln.tiles + (ln.t0 + ln.tiles))
                    round_weights(ln, i, it, lag + u)
                    evacuate(ln, i - 2, it, u)
                for i in range(ln.n - lag, ln.n):
                    evacuate(ln, i, 0, i)
                if ln.evac in ("gateup", "relu2"):
                    w.hid += ln.n * ln.events

            def layer_norm(name, st, eps):
                x, n, nt = X[st], w.ln, NT[st] // P
                for k in range(DC):
                    eng.wait_ge(s_cent, DC * n + k + 1)
                    eng.activation(sq[:, k, 0:NT[st]], x[:, k, :], ACT.Square).then_inc(s_sq, 1)
                eng.wait_ge(s_sum, 2 * n + 2)
                e = 0 if eps == LN_EPS else 2
                eng.activation(dev[:, 0:nt], ps[:, B_STAT, 8:8 + nt], ACT.Sqrt, bias=eps_t[:, e:e + 1])\
                   .then_inc(s_dev, 1)
                for k in range(DC):
                    eng.wait_ge(s_scal, DC * n + k + 1)
                    eng.activation(x[:, k, :], x[:, k, :], ACT.Identity, bias=pc("ln_b_" + name, k),
                                   scale=pc("ln_g_" + name, k)).then_inc(s_aff, 1)
                w.ln += 1

            def modulate(m, st):
                hi = H[st][0]
                for k in range(DC):
                    eng.wait_ge(s_h32, DC * w.mod + k + 1)
                    eng.activation(hi[:, k, :], h32[:, k % 4, 0:NT[st]], ACT.Copy).then_inc(s_hhi, 1)
                w.mod += 1
                w.h_chunks += DC

            def mixer(l):
                M = w.mixer
                eng.activation(a_head[:, :], pc(f"a_log_{l}", 0, SSD_H), ACT.Exp).then_inc(m_ahd, 1)
                eng.wait_ge(m_sp, NSP * M + 4)
                eng.activation(sp["e"][:, :, :], sp["n"][:, :, :], ACT.Exp).then_inc(m_spe, 1)
                for p, pair in enumerate(PAIRS):
                    eng.wait_ge(m_conv, 32 * M + 8 * (p + 1))
                    for q, t in enumerate(pair):
                        eng.activation(proj[:, XBC + t, :], cacc[:, 2 * (p % 2) + q, :], ACT.Silu,
                                       bias=pc(f"conv_b_{l}", t)).then_inc(m_silu, 1)
                for t in range(4):
                    eng.activation(proj[:, Z + t, :], proj[:, Z + t, :], ACT.Silu).then_inc(m_z, 1)
                for c in range(4):
                    eng.wait_ge(m_tr, 4 * M + c + 1)
                    eng.activation(xrow[:, c, :], ps[:, 4, :], ACT.Copy).then_inc(m_rows, 1)
                    eng.activation(brow[:, c, :], ps[:, 5, 0:2 * P], ACT.Copy).then_inc(m_rows, 1)

                def ssd_exp(it):
                    i = 8 * M + it
                    eng.wait_ge(m_pre, i + 1)
                    if i:
                        eng.wait_ge(m_mul, 5 * i)
                        eng.wait_ge(m_sev, SEV[8] * M + SEV[it])
                    eng.activation(ss["lmat"][:, :, :].rearrange("p a t -> p (a t)"), ps[:, 0, :], ACT.Exp)\
                       .then_inc(m_sexp, 1)
                    eng.activation(ss["emat"][:, :, :].rearrange("p a t -> p (a t)"), ps[:, 1, :], ACT.Exp)\
                       .then_inc(m_sexp, 1)
                    eng.activation(decs[:, :], ps[:, 2, 256:264], ACT.Exp).then_inc(m_sexp, 1)

                def fox_exp(f):
                    F, n = 16 * M + f, (f % 4 + 1) * P
                    eng.wait_ge(m_fmax, 2 * F + 2)
                    if F:
                        eng.wait_ge(m_ftr, F)
                    eng.activation(fprob[:, 0:n], ps[:, 4, 0:n], ACT.Exp, bias=nmax[:, f % 4:f % 4 + 1],
                                   accum_out=psumr[:, f % 4:f % 4 + 1]).then_inc(m_fp, 1)

                def fox_copy(f):
                    F, nb = 16 * M + f, f % 4 + 1
                    eng.wait_ge(m_ftr, F + 1)
                    if F:
                        eng.wait_ge(m_fo, F)
                    eng.activation(fprobT[:, 0:nb, :].rearrange("p a t -> p (a t)"), ps[:, 5, 0:nb * P], ACT.Copy)\
                       .then_inc(m_fpt, 1)

                for it in range(8):
                    ssd_exp(it)
                    for f in (2 * it, 2 * it + 1):
                        fox_exp(f)
                        fox_copy(f)
                for t in range(4):
                    eng.wait_ge(m_gate, 4 * M + t + 1)
                    eng.activation(proj[:, Z + t, :], proj[:, t, :], ACT.Square).then_inc(m_ysq, 1)
                for g in range(2):
                    eng.wait_ge(m_ms, 2 * M + g + 1)
                    eng.activation(ss[("am", "ab")[g]][:, :, :].rearrange("p a t -> p (a t)"), ps[:, g, :], ACT.Sqrt,
                                   scale=1.0 / 256, bias=eps_t[:, 1:2]).then_inc(m_sd, 1)
                src = {}
                for t in range(4):
                    src[t] = (proj[:, t, :], m_rn, 6 * M + 3 * (t // 2) + 2 + t % 2)
                for t in range(2):
                    src[4 + t] = (proj[:, FQ + t, :], m_fy, 16 * M + 8 * (t + 1))
                    src[6 + t] = (proj[:, BG + t, :], m_sc, NSC * (M + 1))
                for t in range(DC):
                    eng.wait_ge(src[t][1], src[t][2])
                    eng.activation(h_hi[:, t, :], src[t][0], ACT.Copy).then_inc(s_hhi, 1)
                w.h_chunks += DC
                w.mixer += 1

            def norm_gqa():
                eng.wait_ge(s_evac, w.events)
                for j, (x, t, _) in enumerate(GQA_JOBS):
                    b = j % 2
                    if j >= 2:
                        eng.wait_ge(r_out, 3 * (w.rope + j - 1))
                    eng.activation(gp[:, b, :], x[:, t, :], ACT.Square).then_inc(n_sq, 1)
                    eng.wait_ge(n_ms, w.nms + j + 1)
                    eng.activation(gpt[:, b, :], flat(2 * b), ACT.Sqrt, scale=1.0 / HD, bias=eps_t[:, 2:3])\
                       .then_inc(n_sd, 1)
                n = len(GQA_JOBS)
                w.nsq, w.nms, w.nout, w.rope = w.nsq + n, w.nms + n, w.nout + 2 * n, w.rope + n

            def norm_mla():
                eng.wait_ge(s_evac, w.events)
                eng.wait_ge(s_xa, DC * w.mod)
                for t in range(KVC):
                    eng.activation(msq[:, t, :], ckv[:, t, :], ACT.Square).then_inc(n_sq, 1)
                for t in range(QC):
                    eng.activation(msq[:, KVC + t, 0:SEQ], cq[:, t, :], ACT.Square).then_inc(n_sq, 1)
                eng.wait_ge(n_ms, w.nms + 1)
                eng.activation(msd[:, 0, :], flat(0), ACT.Sqrt, scale=1.0 / (KVC * P), bias=eps_t[:, 2:3])\
                   .then_inc(n_sd, 1)
                eng.wait_ge(n_ms, w.nms + 2)
                eng.activation(msd[:, 1, 0:SEQ], ps[:, 2, :], ACT.Sqrt, scale=1.0 / (QC * P), bias=eps_t[:, 2:3])\
                   .then_inc(n_sd, 1)
                for t in range(KVC):
                    eng.wait_ge(n_out, w.nout + 2 + t)
                    eng.activation(ckvn_hi[:, t, :], ckv[:, t, :], ACT.Copy).then_inc(s_hhi, 1)
                for t in range(QC):
                    eng.wait_ge(n_out, w.nout + KVC + 3 + t)
                    eng.activation(cqn_hi[:, t, :], cq[:, t, :], ACT.Copy).then_inc(s_hhi, 1)
                w.nms += 2
                w.nout += QC + KVC + 2
                w.h_chunks += QC + KVC

            def attention(kind):
                a = ATT[kind]
                for n_tiles, _, k0, nk in a["runs"]:
                    T0 = w.att
                    with eng.Fori(0, n_tiles) as it:
                        for s in range(HEADS + 1):
                            if s < HEADS:
                                eng.wait_ge(t_max, it * (2 * HEADS) + (2 * HEADS * T0 + 2 * s + 2))
                                if s >= 2:
                                    eng.wait_ge(t_tr, it * HEADS + (HEADS * T0 + s - 1))
                                eng.activation(a["p"][:, s % 2, 0:nk], flat(2 * (s % 2))[:, 0:nk], ACT.Exp,
                                               scale=a["scale"], bias=nmax[:, s:s + 1], accum_out=psumr[:, s:s + 1])\
                                   .then_inc(t_p, 1)
                            if s:
                                eng.wait_ge(t_tr, it * HEADS + (HEADS * T0 + s))
                                eng.activation(a["pt"][:, (s - 1) % 2, 0:nk], flat(4)[:, 0:nk], ACT.Copy)\
                                   .then_inc(t_pt, 1)
                    w.att += n_tiles
                eng.wait_ge(t_done, w.att)
                parts = [(h_hi, q_t[:, :, 0:SEQ]), (hc_hi, q_t[:, :, SEQ:])] if kind == "gqa" else [(y2_hi, mq[:, :, :])]
                for hi, y in parts:
                    for k in range(DC):
                        eng.activation(hi[:, k, :], y[:, k, :], ACT.Copy).then_inc(s_hhi, 1)
                w.h_chunks += DC * len(parts)

            for j, item in enumerate(sched):
                if j in early:
                    prologue(sched[early[j]][1])
                if item[0] == "lin":
                    if j not in early.values():
                        prologue(item[1])
                    linear(item[1])
                    w.events = item[1].e0 + item[1].n * item[1].events
                elif item[0] == "ln":
                    layer_norm(*item[1:])
                elif item[0] == "mod":
                    modulate(*item[1:])
                elif item[0] == "mixer":
                    mixer(item[1])
                elif item[0] == "gqa":
                    norm_gqa()
                    attention("gqa")
                elif item[0] == "mla_norm":
                    norm_mla()
                elif item[0] == "mla":
                    attention("mla")

        @block.tensor
        def _(eng):
            w = Walk()
            eng.wait_ge(s_const, N_CONST)
            eng.wait_ge(s_par, 32)
            eng.wait_ge(s_cact, 2)

            def ada_unit(m, slot, i, pos=None):
                nv = 1 if m < 6 else 2
                c0 = 0 if nv == 1 else DC
                for q in range(2):
                    col = 48 * m + (i * 2 + q) * nv
                    for k in range(DC):
                        mm = eng.matmul(ps[:, B_ADA, at(col, nv)], raw[:, slot, (q * DC + k) * P:(q * DC + k + 1) * P],
                                        c_act[:, c0 + k * nv:c0 + (k + 1) * nv], start=(k == 0), stop=(k == DC - 1),
                                        skip_group_check=True)
                mm.then_inc(s_ada, 1)

            def ada_run(m, n, lo, hi):
                for i in range(lo, hi):
                    g = n + i
                    raw_ready(eng, g, 0, 0, 1)
                    ada_unit(m, g % RAW, i)

            def passes(out, hi_w, lo_w, hi_x, lo_x, first, last):
                eng.matmul(out, lo_w, hi_x, start=first, stop=False, skip_group_check=True)
                eng.matmul(out, hi_w, lo_x, start=False, stop=False, skip_group_check=True)
                return eng.matmul(out, hi_w, hi_x, start=False, stop=last, skip_group_check=True)

            def linear(ln):
                eng.wait_ge(s_evac, ln.e0)
                if ln.src == "hid":
                    eng.wait_ge(s_hid, w.hid)
                else:
                    eng.wait_ge(s_hlo, w.h_chunks)
                for it, u, i in steps(eng, 0, ln.n):
                    eng.wait_ge(s_wlo, i + (ln.g0 + 1))
                    slot = (ln.g0 + u) % 2
                    if ln.evac == "gateup":
                        eng.wait_ge(s_evac, i + (ln.e0 - 1))
                    if ln.row:
                        toks = [(st, t) for st in ln.streams for t in range(NT[st] // P)]
                        for t, (st, tt) in enumerate(toks):
                            hi, lo = operand(ln, st)
                            if t >= 4:
                                eng.wait_ge(s_evac, i * ln.row + (ln.e0 + t - 3))
                            elif ln.n > 1:
                                eng.wait_ge(s_evac, i * ln.row + (ln.e0 + 1 - ln.row + max(range(t, ln.row, 4))))
                            for k in range(ln.kc):
                                ws = slice(k * ln.out, (k + 1) * ln.out)
                                xs = slice(tt * P, (tt + 1) * P)
                                mm = passes(ps[:, t % 4, 0:ln.out], hi[:, k, xs], lo[:, k, xs], w_hi[:, slot, ws],
                                            w_lo[:, slot, ws], k == 0, k == ln.kc - 1)
                            mm.then_inc(s_tile, 1)
                    else:
                        for q in range(ln.tpu):
                            tile = u * ln.tpu + q
                            if ln.evac != "gateup":
                                eng.wait_ge(s_evac, i * ln.tpu + (ln.e0 + q - ln.nbuf + 1))
                            for st in ln.streams:
                                hi, lo = operand(ln, st)
                                for k in range(ln.kc):
                                    ws = slice((q * ln.kc + k) * P, (q * ln.kc + k + 1) * P)
                                    mm = passes(ps[:, tile_bank(ln, tile, st), 0:NT[st]], w_hi[:, slot, ws],
                                                w_lo[:, slot, ws], hi[:, k, 0:NT[st]], lo[:, k, 0:NT[st]], k == 0,
                                                k == ln.kc - 1)
                            mm.then_inc(s_tile, 1)
                    if ln.ada:
                        G = ln.G0 + u * 2 + 1
                        raw_ready(eng, G, 0, it, 2)
                        ada_unit(ln.ada[0], G % RAW, i + ln.ada[1])
                if ln.evac in ("gateup", "relu2"):
                    w.hid += ln.n * ln.events

            def layer_norm(name, st, eps):
                x, n, nt = X[st], w.ln, NT[st] // P
                eng.wait_ge(s_evac, w.events)
                if n == 0:
                    eng.wait_ge(s_x, 16)
                eng.wait_ge(s_xa, DC * w.mod)
                for t in range(nt):
                    for k in range(DC):
                        mm = eng.matmul(ps[:, B_STAT, t:t + 1], x[:, k, t * P:(t + 1) * P], mean_w[:, 0:1],
                                        start=(k == 0), stop=(k == DC - 1), skip_group_check=True)
                mm.then_inc(s_sum, 1)
                eng.wait_ge(s_diag, 2 * n + 1)
                eng.matmul(ps[:, B_MEAN, 0:nt * P], ones[:, :], diag[:, 0, 0:nt, :].rearrange("p a t -> p (a t)"),
                           start=True, stop=True).then_inc(s_bc, 1)
                for k in range(DC):
                    eng.wait_ge(s_sq, DC * n + k + 1)
                    for t in range(nt):
                        mm = eng.matmul(ps[:, B_STAT, 8 + t:9 + t], sq[:, k, t * P:(t + 1) * P], mean_w[:, 0:1],
                                        start=(k == 0 and t == 0), stop=(k == DC - 1), skip_group_check=True)
                mm.then_inc(s_sum, 1)
                eng.wait_ge(s_diag, 2 * n + 2)
                eng.matmul(ps[:, B_RSTD, 0:nt * P], ones[:, :], diag[:, 1, 0:nt, :].rearrange("p a t -> p (a t)"),
                           start=True, stop=True).then_inc(s_bc, 1)
                w.ln += 1

            def mixer(l):
                M = w.mixer
                eng.wait_ge(s_evac, w.events)
                for c in range(4):
                    if c == 0:
                        eng.wait_ge(m_silu, 8 * (M + 1))
                    else:
                        eng.wait_ge(m_rows, 8 * M + 2 * c)
                    cs = slice(c * P, (c + 1) * P)
                    for t in range(4):
                        eng.transpose(ps[:, 4, t * P:(t + 1) * P], proj[:, XBC + t, cs], ident[:, :])
                    for t in range(2):
                        tr = eng.transpose(ps[:, 5, t * P:(t + 1) * P], proj[:, XBC + 4 + t, cs], ident[:, :])
                    tr.then_inc(m_tr, 1)

                def ssd_pre(it):
                    i, (c, g) = 8 * M + it, divmod(it, 2)
                    cs = slice(c * P, (c + 1) * P)
                    eng.wait_ge(m_am, i + 1)
                    eng.wait_ge(m_ab, i + 1)
                    if i:
                        eng.wait_ge(m_sexp, 3 * i)
                        eng.wait_ge(m_mul, 5 * i)
                    for h in range(4):
                        eng.matmul(ps[:, 0, h * P:(h + 1) * P], ss["am"][:, h, :], tri[:, :], start=True, stop=True)
                    for h in range(4):
                        eng.matmul(ps[:, 1, h * P:(h + 1) * P], ss["ab"][:, h, :], tri[:, :], start=True, stop=True)
                    eng.matmul(ps[:, 2, 0:P], proj[:, XBC + 4 + g, cs], proj[:, XBC + 6 + g, cs], start=True, stop=True)
                    ah = a_row[:, c, 4 * g:4 * g + 4]
                    eng.matmul(ps[:, 2, 256:260], past[:, 3, :], ah, start=True, stop=True)
                    eng.matmul(ps[:, 2, 260:264], ones[:, :], ah, start=True, stop=True).then_inc(m_pre, 1)

                def ssd_y(it):
                    i, (c, g) = 8 * M + it, divmod(it, 2)
                    eng.wait_ge(m_mul, 5 * (i + 1))
                    eng.wait_ge(m_sev, SEV[8] * M + SEV[it])
                    for q in range(2):
                        for hh in range(2):
                            h = 2 * q + hh
                            o = ps[hh * HD:(hh + 1) * HD, 3, q * P:(q + 1) * P]
                            mm = eng.matmul(o, xdt[:, h, :], ss["mmat"][:, h, :], start=True, stop=(c == 0),
                                            skip_group_check=True)
                            if c:
                                mm = eng.matmul(o, state[:, g, h * HD:(h + 1) * HD], ss["cdec"][:, h, :], start=False,
                                                stop=True, skip_group_check=True)
                    if c < 3:
                        mm = eng.matmul(ps[:, 3, 2 * P:4 * P], brow[:, c, g * P:(g + 1) * P],
                                        xdec[:, :, :].rearrange("p a t -> p (a t)"), start=True, stop=True,
                                        skip_group_check=True)
                    mm.then_inc(m_y, 1)

                def fox_scores(f):
                    F, (h, i) = 16 * M + f, divmod(f, 4)
                    n, hp = (i + 1) * P, slice((h % 2) * HD, (h % 2 + 1) * HD)
                    eng.wait_ge(m_qs, M + 1)
                    eng.wait_ge(m_fg, 16 * M + 4 * (h + 1))
                    if F:
                        eng.wait_ge(m_fp, F)
                    if f == 0:
                        eng.wait_ge(m_rows, 8 * (M + 1))
                    eng.matmul(ps[:, 4, 0:n], proj[hp, FQ + h // 2, i * P:n], proj[hp, FK + h // 2, 0:n], start=True,
                               stop=False, skip_group_check=True)
                    for j in range(i + 1):
                        eng.matmul(ps[:, 4, 0:(j + 1) * P], tri[:, :] if j == i else ones[:, :],
                                   fcum[:, j, 0:(j + 1) * P], start=False, stop=False, skip_group_check=True)
                    eng.matmul(ps[:, 4, i * P:n], ident[:, :], negmask[:, :], start=False, stop=True,
                               skip_group_check=True).then_inc(m_fs, 1)

                def fox_out(f):
                    F, (h, i) = 16 * M + f, divmod(f, 4)
                    eng.wait_ge(m_fn, 2 * F + 2)
                    if F:
                        eng.wait_ge(m_fpt, F)
                    for j in range(i + 1):
                        tr = eng.transpose(ps[:, 5, j * P:(j + 1) * P], fprob[:, j * P:(j + 1) * P], ident[:, :])
                    tr.then_inc(m_ftr, 1)
                    eng.wait_ge(m_fpt, F + 1)
                    if F:
                        eng.wait_ge(m_fy, F)
                    for j in range(i + 1):
                        mm = eng.matmul(ps[(h % 2) * HD:(h % 2 + 1) * HD, 6, 0:P], vrow[:, j, h * HD:(h + 1) * HD],
                                        fprobT[:, j, :], start=(j == 0), stop=(j == i), skip_group_check=True)
                    mm.then_inc(m_fo, 1)

                ada = 0
                for it in range(8):
                    ssd_pre(it)
                    fox_scores(2 * it)
                    ssd_y(it)
                    fox_out(2 * it)
                    fox_scores(2 * it + 1)
                    fox_out(2 * it + 1)
                    if l == 1:
                        n = 2 if it < 4 else 1
                        ada_run(7, w.stream, ada, ada + n)
                        ada += n
                for g in range(2):
                    eng.wait_ge(m_ysq, 4 * M + 2 * g + 2)
                    for q in range(2):
                        mm = eng.matmul(ps[:, g, :], ones[:, :], proj[:, Z + 2 * g + q, :], start=(q == 0), stop=(q == 1))
                    mm.then_inc(m_ms, 1)
                w.mixer += 1
                w.h_chunks += DC

            def swap(x, b, which):
                eng.matmul(ps[:, 4 + b, :], swaps[:, which, :], x, start=True, stop=True).then_inc(r_sw, 1)

            def norm_gqa():
                def mean_square(j):
                    b = j % 2
                    eng.wait_ge(n_sq, w.nsq + j + 1)
                    if j >= 2:
                        eng.wait_ge(n_sd, w.nms + j - 1)
                    eng.matmul(ps[:, 2 * b, :], blocks[:, :], gp[:, b, 0:SEQ], start=True, stop=True)
                    eng.matmul(ps[:, 2 * b + 1, 0:CTX], blocks[:, :], gp[:, b, SEQ:], start=True, stop=True)\
                       .then_inc(n_ms, 1)

                n = len(GQA_JOBS)
                eng.wait_ge(s_evac, w.events)
                for j, (x, t, _) in enumerate(GQA_JOBS):
                    mean_square(j)
                    eng.wait_ge(n_out, w.nout + 2 * j + 2)
                    if j >= 2:
                        eng.wait_ge(r_out, 3 * (w.rope + j - 1))
                    swap(x[:, t, 0:SEQ], j % 2, 0)
                w.nsq, w.nms, w.nout, w.rope = w.nsq + n, w.nms + n, w.nout + 2 * n, w.rope + n

            def norm_mla():
                eng.wait_ge(s_evac, w.events)
                eng.wait_ge(n_sq, w.nsq + KVC)
                for c0, n, bank in ((0, SEQ, 0), (SEQ, CTX, 1)):
                    for t in range(KVC):
                        mm = eng.matmul(ps[:, bank, 0:n], ones[:, :], msq[:, t, c0:c0 + n], start=(t == 0),
                                        stop=(t == KVC - 1))
                mm.then_inc(n_ms, 1)
                eng.wait_ge(n_sq, w.nsq + KVC + QC)
                for t in range(QC):
                    mm = eng.matmul(ps[:, 2, :], ones[:, :], msq[:, KVC + t, 0:SEQ], start=(t == 0), stop=(t == QC - 1))
                mm.then_inc(n_ms, 1)
                swap(kpe[:, 0:SEQ], 0, 1)
                w.nsq += KVC + QC
                w.nms += 2
                w.rope += 1
                w.h_chunks += QC + KVC

            def rope_mla():
                eng.wait_ge(s_evac, w.events)
                for j in range(4):
                    if j >= 2:
                        eng.wait_ge(r_out, 3 * (w.rope + j - 1))
                    swap(qpe[:, j, :], j % 2, 1)
                w.rope += 4

            def attention(kind):
                a = ATT[kind]
                if kind == "gqa":
                    eng.wait_ge(r_out, 3 * w.rope)
                for n_tiles, _, k0, nk in a["runs"]:
                    T0 = w.att
                    with eng.Fori(0, n_tiles) as it:
                        eng.wait_ge(t_q, it + (T0 + 1))

                        def scores(s):
                            tile, hp = s // 2, slice((s % 2) * HD, (s % 2 + 1) * HD)
                            kt = tile // 4 if kind == "gqa" else tile
                            if s >= 2:
                                eng.wait_ge(t_p, it * HEADS + (HEADS * T0 + s - 1))
                            for c in range(0, nk, SEQ):
                                n = min(SEQ, nk - c)
                                o, ks = ps[:, 2 * (s % 2) + c // SEQ, 0:n], slice(k0 + c, k0 + c + n)
                                mm = eng.matmul(o, a["qs"][hp, tile, :], a["k"][hp, kt, ks], start=True,
                                                stop=(kind == "gqa"), skip_group_check=True)
                                if kind == "mla":
                                    rp = slice((s % 4) * ROPE, (s % 4 + 1) * ROPE)
                                    mm = eng.matmul(o, qpes[rp, s // 4, :], kpe[rp, ks], start=False, stop=True,
                                                    skip_group_check=True)
                            mm.then_inc(t_s, 1)

                        def turn(s):
                            eng.wait_ge(t_p, it * HEADS + (HEADS * T0 + s + 1))
                            if s:
                                eng.wait_ge(t_pt, it * HEADS + (HEADS * T0 + s))
                            for j in range(nk // P):
                                tr = eng.transpose(ps[:, 4 + j // 4, (j % 4) * P:(j % 4 + 1) * P],
                                                   a["p"][:, s % 2, j * P:(j + 1) * P], ident[:, :])
                            tr.then_inc(t_tr, 1)

                        def output(s):
                            v0 = (2 * (s // 8) + s % 2) * HD if kind == "gqa" else s * HD
                            eng.wait_ge(t_pt, it * HEADS + (HEADS * T0 + s + 1))
                            if s == 8:
                                eng.wait_ge(t_row, it * 4 + (4 * T0 + 2))
                            for j in range(nk // P):
                                mm = eng.matmul(ps[:, 6, (s % 8) * HD:(s % 8 + 1) * HD], a["pt"][:, s % 2, j * P:(j + 1) * P],
                                                a["v"][:, k0 // P + j, v0:v0 + HD], start=(j == 0),
                                                stop=(j == nk // P - 1), skip_group_check=True)
                            if s % 8 == 7:
                                mm.then_inc(t_o, 1)

                        for s in range(HEADS + 2):
                            if s < HEADS:
                                scores(s)
                            if 1 <= s <= HEADS:
                                turn(s - 1)
                            if s >= 2:
                                output(s - 2)
                        eng.wait_ge(t_row, it * 4 + (4 * T0 + 4))
                        for j in range(DC):
                            tr = eng.transpose(ps[:, 4 + j // 4, (j % 4) * P:(j % 4 + 1) * P],
                                               a["row"][:, j * P:(j + 1) * P], ident[:, :])
                        tr.then_inc(t_yt, 1)
                    w.att += n_tiles
                w.h_chunks += DC * (2 if kind == "gqa" else 1)

            w.stream = 0
            for item in sched:
                if item[0] == "ada0":
                    ada_run(0, 0, 0, ADA_UNITS)
                    w.stream += ADA_UNITS
                elif item[0] == "lin":
                    ln = item[1]
                    linear(ln)
                    w.events = ln.e0 + ln.n * ln.events
                    w.stream = ln.G0 + ln.n * ln.spu
                elif item[0] == "ln":
                    layer_norm(*item[1:])
                elif item[0] == "mod":
                    w.mod += 1
                    w.h_chunks += DC
                elif item[0] == "mixer":
                    mixer(item[1])
                    if item[1] == 1:
                        w.stream += ADA_UNITS
                elif item[0] == "gqa":
                    norm_gqa()
                    attention("gqa")
                elif item[0] == "mla_norm":
                    norm_mla()
                elif item[0] == "mla":
                    rope_mla()
                    eng.wait_ge(r_out, 3 * w.rope)
                    attention("mla")

        @block.vector
        def _(eng):
            w = Walk()
            eng.wait_ge(s_par, 32)
            eng.wait_ge(s_const, N_CONST)
            eng.sem_inc(s_evac, 4)

            def split_weights(ln, i, it, pos):
                G, slot = ln.G0 + pos * ln.spu, (ln.g0 + pos) % 2
                eng.wait_ge(s_whi, i + (ln.g0 + 1))
                eng.tensor_tensor(w_lo[:, slot, 0:ln.width], raw[:, G % RAW, 0:ln.width],
                                  w_hi[:, slot, 0:ln.width].bitcast(F32), ALU.subtract).then_inc(s_wlo, 1)

            def prologue(ln):
                for i in range(min(2, ln.n)):
                    split_weights(ln, i, 0, i)

            def evacuate(ln, i, it, pos):
                if ln.evac == "gateup":
                    h = w.hid
                    eng.wait_ge(s_gate, i + (h + 1))
                    if pos >= 2 or h:
                        eng.wait_ge(s_hid, i + (h - 1))
                    eng.tensor_tensor(val_t[:, pos % 2, 0:SEQ], ps[:, tile_bank(ln, 2 * pos + 1, "lat"), :],
                                      gate_t[:, pos % 2, 0:SEQ], ALU.mult).then_inc(s_evac, 1)
                    eng.wait_ge(s_hidhi, i + (h + 1))
                    eng.tensor_tensor(hid_lo[:, at(i), :], val_t[:, pos % 2, 0:SEQ].unsqueeze(1),
                                      hid_hi[:, at(i), :].bitcast(F32), ALU.subtract).then_inc(s_hid, 1)
                elif ln.evac == "relu2":
                    h = w.hid
                    for q in range(2):
                        eng.wait_ge(s_gate, i * 2 + (h + q + 1))
                        for st in ln.streams:
                            c = slice(COL0[st], COL0[st] + NT[st])
                            a = eng.tensor_tensor(relu_t[:, q, c], relu_t[:, q, c], relu_t[:, q, c], ALU.mult)
                        a.then_inc(s_evac, 1)
                        eng.wait_ge(s_hidhi, i * 2 + (h + q + 1))
                        for st in ln.streams:
                            c = slice(COL0[st], COL0[st] + NT[st])
                            a = eng.tensor_tensor(HID[st][1][:, at(i * 2 + q), :], relu_t[:, q, c].unsqueeze(1),
                                                  HID[st][0][:, at(i * 2 + q), :].bitcast(F32), ALU.subtract)
                        a.then_inc(s_hid, 1)
                elif ln.row:
                    for t in range(ln.row):
                        eng.wait_ge(s_tile, i * ln.row + (ln.t0 + t + 1))
                        eng.tensor_copy(row_dest(ln, i, t), ps[:, t % 4, 0:ln.out]).then_inc(s_evac, 1)
                else:
                    for q in range(ln.tpu):
                        m = i * ln.tpu + q
                        eng.wait_ge(s_tile, m + (ln.t0 + 1))
                        for st in ln.streams:
                            tile = ps[:, tile_bank(ln, pos * ln.tpu + q, st), 0:NT[st]].unsqueeze(1)
                            if ln.evac == "copy":
                                a = eng.tensor_copy(dest(ln, st, m), tile)
                            else:
                                xm = X[st][:, at(m), :]
                                a = eng.scalar_tensor_tensor(xm, tile, MODT[st][:, at(m + 2 * DC)], xm, ALU.mult,
                                                             ALU.add)
                        a.then_inc(s_evac, 1)

            def linear(ln):
                lag = min(2, ln.n)
                eng.wait_ge(s_evac, ln.e0)
                if ln.evac == "resid":
                    eng.wait_ge(s_xa, DC * w.mod)
                for it, u, i in steps(eng, lag, ln.n):
                    split_weights(ln, i, it, lag + u)
                    evacuate(ln, i - 2, it, u)
                for i in range(ln.n - lag, ln.n):
                    evacuate(ln, i, 0, i)
                w.events = ln.e0 + ln.n * ln.events
                if ln.evac in ("gateup", "relu2"):
                    w.hid += ln.n * ln.events

            def layer_norm(name, st, eps):
                x, n, nt = X[st], w.ln, NT[st] // P
                idb = ident[:, :].unsqueeze(1).broadcast_to([P, nt, P])
                eng.wait_ge(s_sum, 2 * n + 1)
                if n:
                    eng.wait_ge(s_diag, 2 * n)
                eng.tensor_tensor(diag[:, 0, 0:nt, :], idb, ps[:, B_STAT, 0:nt].unsqueeze(2).broadcast_to([P, nt, P]),
                                  ALU.mult).then_inc(s_diag, 1)
                eng.wait_ge(s_bc, 2 * n + 1)
                eng.wait_ge(s_evac, w.events)
                for k in range(DC):
                    eng.tensor_tensor(x[:, k, :], x[:, k, :], ps[:, B_MEAN, 0:NT[st]], ALU.subtract).then_inc(s_cent, 1)
                eng.wait_ge(s_dev, n + 1)
                eng.reciprocal(rstd[:, 0:nt], dev[:, 0:nt]).then_inc(s_rstd, 1)
                eng.wait_ge(s_rstd, n + 1)
                eng.tensor_tensor(diag[:, 1, 0:nt, :], idb, rstd[:, 0:nt].unsqueeze(2).broadcast_to([P, nt, P]),
                                  ALU.mult).then_inc(s_diag, 1)
                eng.wait_ge(s_bc, 2 * n + 2)
                eng.wait_ge(s_cent, DC * n + DC)
                for k in range(DC):
                    eng.tensor_tensor(x[:, k, :], x[:, k, :], ps[:, B_RSTD, 0:NT[st]], ALU.mult).then_inc(s_scal, 1)
                w.ln += 1

            def modulate(m, st):
                nv, v = (1, 0) if m < 6 else (2, int(st == "ctx"))
                x, mod, lo = X[st], MODT[st], H[st][1]
                eng.wait_ge(s_ada, ada_done[m])
                cols_m = ps[:, B_ADA, 48 * m:48 * m + MOD * nv].rearrange("p (a v) -> p a v", v=nv)[:, :, v:v + 1]
                eng.tensor_tensor(mod[:, :].unsqueeze(2), cols_m, pc(f"ada_b_{m}", 0, MOD).unsqueeze(2), ALU.add)\
                   .then_inc(s_mod, 1)
                eng.wait_ge(s_mod, 3 * w.mod + 1)
                eng.tensor_scalar(mod[:, DC:2 * DC], mod[:, DC:2 * DC], 1.0, None, ALU.add).then_inc(s_mod, 1)
                half = 0.5 if m in (0, 2, 3, 5) else 1.0
                eng.tensor_scalar(mod[:, 2 * DC:], mod[:, 2 * DC:], half, None, ALU.mult).then_inc(s_mod, 1)
                eng.wait_ge(s_mod, 3 * w.mod + 3)
                c0 = DC * w.mod
                for k in range(DC + 1):
                    if k < DC:
                        if st == "ctx" and m == 6:
                            eng.wait_ge(s_x, 32)
                        else:
                            eng.wait_ge(s_aff, DC * (w.ln - 1) + k + 1)
                        if c0 + k >= 4:
                            eng.wait_ge(s_h32, c0 + k)
                        if k >= 4:
                            eng.wait_ge(s_hlo, w.h_chunks + k - 3)
                        eng.tensor_scalar(h32[:, k % 4, 0:NT[st]], x[:, k, :], mod[:, DC + k:DC + k + 1],
                                          mod[:, k:k + 1], ALU.mult, ALU.add).then_inc(s_h32, 1)
                    if k:
                        eng.wait_ge(s_hhi, w.h_chunks + k)
                        eng.tensor_tensor(lo[:, k - 1, :], h32[:, (k - 1) % 4, 0:NT[st]],
                                          H[st][0][:, k - 1, :].bitcast(F32), ALU.subtract).then_inc(s_hlo, 1)
                w.mod += 1
                w.h_chunks += DC

            def mixer(l):
                M = w.mixer
                n0 = [NSP * M]

                def step(ins):
                    ins.then_inc(m_sp, 1)
                    n0[0] += 1
                    eng.wait_ge(m_sp, n0[0])

                v, n, e, d, z, z2, p, dt = (sp[k][:, :, :] for k in ("v", "n", "e", "d", "z", "z2", "p", "dt"))
                eng.wait_ge(s_evac, w.events)
                step(eng.tensor_tensor(v, dtrow[:, :, :], pc(f"dt_bias_{l}", 0, 12).unsqueeze(1)
                                       .broadcast_to([P, 4, 12]), ALU.add))
                step(eng.tensor_scalar(sp["v"][:, :, SSD_H:], sp["v"][:, :, SSD_H:], -1.0, None, ALU.mult))
                step(eng.tensor_scalar(n, v, -1.0, None, ALU.mult))
                step(eng.tensor_tensor(n, n, v, ALU.min))
                eng.wait_ge(m_spe, M + 1)
                step(eng.tensor_scalar(d, e, 2.0, None, ALU.add))
                step(eng.reciprocal(d, d))
                step(eng.tensor_tensor(z, e, d, ALU.mult))
                step(eng.tensor_tensor(z2, z, z, ALU.mult))
                step(eng.tensor_scalar(p, z2, LOG1P[7], None, ALU.mult))
                for k in range(6, 0, -1):
                    step(eng.scalar_tensor_tensor(p, p, LOG1P[k], z2, ALU.add, ALU.mult))
                step(eng.scalar_tensor_tensor(p, p, LOG1P[0], z, ALU.add, ALU.mult))
                step(eng.tensor_scalar(n, v, 0.0, None, ALU.max))
                step(eng.scalar_tensor_tensor(dt, p, 2.0, n, ALU.mult, ALU.add))
                eng.wait_ge(m_ahd, M + 1)
                step(eng.scalar_tensor_tensor(a_row[:, :, :], sp["dt"][:, :, 0:SSD_H], -1.0,
                                              a_head[:, :].unsqueeze(1).broadcast_to([P, 4, SSD_H]), ALU.mult, ALU.mult))
                step(eng.tensor_scalar(logf[:, :, :], sp["dt"][:, :, SSD_H:], -1.0, None, ALU.mult))
                assert n0[0] == NSP * (M + 1)
                eng.tensor_scalar(proj[:, FQ:FQ + 2, :], proj[:, FQ:FQ + 2, :], HD ** -0.5, None, ALU.mult)\
                   .then_inc(m_qs, 1)

                for pr, pair in enumerate(PAIRS):
                    b = 32 * M + 8 * pr
                    if pr >= 2:
                        eng.wait_ge(m_silu, 8 * M + 2 * (pr - 1))
                    for k in range(4):
                        if k:
                            eng.wait_ge(m_conv, b + 2 * k)
                        for q, t in enumerate(pair):
                            acc, tap = cacc[:, 2 * (pr % 2) + q, :], pc(f"conv_w_{l}", 4 * t + 3 - k)
                            if k == 0:
                                a = eng.tensor_scalar(acc, proj[:, XBC + t, :], tap, None, ALU.mult)
                            else:
                                a = eng.scalar_tensor_tensor(acc[:, k:], proj[:, XBC + t, 0:SEQ - k], tap, acc[:, k:],
                                                             ALU.mult, ALU.add)
                            a.then_inc(m_conv, 1)

                b = NSC * M
                for t in range(2):
                    eng.tensor_tensor(proj[:, CG + t, :], proj[:, CG + t, :], proj[:, XIN + t, :], ALU.mult)\
                       .then_inc(m_sc, 1)
                for k in range(3):
                    eng.wait_ge(m_sc, b + 2 * (k + 1))
                    for t in range(2):
                        acc, tap = proj[:, XIN + t, :], pc(f"sconv_w_{l}", 3 * t + 2 - k)
                        if k == 0:
                            a = eng.tensor_scalar(acc, proj[:, CG + t, :], tap, None, ALU.mult)
                        else:
                            a = eng.scalar_tensor_tensor(acc[:, k:], proj[:, CG + t, 0:SEQ - k], tap, acc[:, k:],
                                                         ALU.mult, ALU.add)
                        a.then_inc(m_sc, 1)
                eng.wait_ge(m_sc, b + 8)
                for t in range(2):
                    eng.tensor_tensor(proj[:, BG + t, :], proj[:, BG + t, :], proj[:, XIN + t, :], ALU.mult)\
                       .then_inc(m_sc, 1)

                def ssd_mask(it):
                    i, (c, g) = 8 * M + it, divmod(it, 2)
                    if i:
                        eng.wait_ge(m_pre, i)
                    eng.tensor_tensor(ss["am"][:, :, :], past[:, 3, :].unsqueeze(1).broadcast_to([P, 4, P]),
                                      a_row[:, c, 4 * g:4 * g + 4].unsqueeze(2).broadcast_to([P, 4, P]), ALU.mult)\
                       .then_inc(m_am, 1)

                def ssd_operands(it):
                    i, (c, g) = 8 * M + it, divmod(it, 2)
                    cs, b = slice(c * P, (c + 1) * P), 5 * (8 * M + it)
                    eng.wait_ge(m_pre, i + 1)
                    if i:
                        eng.wait_ge(m_y, i)
                        eng.wait_ge(m_mul, b)
                    if it == 0:
                        eng.wait_ge(m_rows, 8 * (M + 1))
                    eng.wait_ge(m_sexp, 3 * (i + 1))
                    eng.tensor_tensor(cbm[:, :], ps[:, 2, 0:P], tri[:, :], ALU.mult).then_inc(m_mul, 1)
                    eng.tensor_tensor(xdt[:, :, :], xrow[:, c, g * 4 * HD:(g + 1) * 4 * HD]
                                      .rearrange("p (h d) -> p h d", h=4),
                                      sp["dt"][:, c, 4 * g:4 * g + 4].unsqueeze(2).broadcast_to([P, 4, HD]), ALU.mult)\
                       .then_inc(m_mul, 1)
                    eng.wait_ge(m_mul, b + 2)
                    eng.tensor_tensor(ss["mmat"][:, :, :], ss["lmat"][:, :, :],
                                      cbm[:, :].unsqueeze(1).broadcast_to([P, 4, P]), ALU.mult).then_inc(m_mul, 1)
                    eng.tensor_tensor(ss["cdec"][:, :, :], ss["emat"][:, :, :],
                                      proj[:, XBC + 6 + g, cs].unsqueeze(1).broadcast_to([P, 4, P]), ALU.mult)\
                       .then_inc(m_mul, 1)
                    eng.tensor_tensor(xdec[:, :, :], xdt[:, :, :], decs[:, 0:4].unsqueeze(2).broadcast_to([P, 4, HD]),
                                      ALU.mult).then_inc(m_mul, 1)

                def ssd_evac(it):
                    i, (c, g) = 8 * M + it, divmod(it, 2)
                    eng.wait_ge(m_y, i + 1)
                    for q in range(2):
                        y = proj[:, XBC + 2 * g + q, c * P:(c + 1) * P]
                        eng.scalar_tensor_tensor(y, y, pc(f"ssd_d_{l}", 2 * g + q), ps[:, 3, q * P:(q + 1) * P],
                                                 ALU.mult, ALU.add).then_inc(m_sev, 1)
                    new = ps[:, 3, 2 * P:4 * P]
                    b = SEV[8] * M + SEV[it] + 2
                    if c == 0:
                        eng.tensor_copy(state[:, g, :], new).then_inc(m_sev, 1)
                    elif c < 3:
                        sv = state[:, g, :].rearrange("p (h d) -> p h d", h=4)
                        eng.tensor_tensor(sv, sv, decs[:, 4:8].unsqueeze(2).broadcast_to([P, 4, HD]), ALU.mult)\
                           .then_inc(m_sev, 1)
                        eng.wait_ge(m_sev, b + 1)
                        eng.tensor_tensor(state[:, g, :], state[:, g, :], new, ALU.add).then_inc(m_sev, 1)

                def fox_rows(h):
                    if h or M:
                        eng.wait_ge(m_fs, 16 * M + 4 * h)
                    for j in range(4):
                        eng.tensor_scalar(fcum[:, j, 0:(j + 1) * P],
                                          past[:, 3 - j:4, :].rearrange("p a t -> p (a t)"), logf[:, j, h:h + 1], None,
                                          ALU.mult).then_inc(m_fg, 1)

                def fox_max(f):
                    F, n = 16 * M + f, (f % 4 + 1) * P
                    eng.wait_ge(m_fs, F + 1)
                    nm = nmax[:, f % 4:f % 4 + 1]
                    eng.reduce_max(nm, ps[:, 4, 0:n], AX_X).then_inc(m_fmax, 1)
                    eng.wait_ge(m_fmax, 2 * F + 1)
                    eng.tensor_scalar(nm, nm, -1.0, None, ALU.mult).then_inc(m_fmax, 1)

                def fox_norm(f):
                    F, n, r = 16 * M + f, (f % 4 + 1) * P, psumr[:, f % 4:f % 4 + 1]
                    eng.wait_ge(m_fp, F + 1)
                    eng.reciprocal(r, r).then_inc(m_fn, 1)
                    eng.wait_ge(m_fn, 2 * F + 1)
                    eng.tensor_scalar(fprob[:, 0:n], fprob[:, 0:n], r, None, ALU.mult).then_inc(m_fn, 1)

                def fox_evac(f):
                    F, (h, i) = 16 * M + f, divmod(f, 4)
                    hp = slice((h % 2) * HD, (h % 2 + 1) * HD)
                    eng.wait_ge(m_fo, F + 1)
                    eng.tensor_copy(proj[hp, FQ + h // 2, i * P:(i + 1) * P], ps[hp, 6, 0:P]).then_inc(m_fy, 1)

                eng.wait_ge(m_silu, 8 * (M + 1))
                ssd_mask(0)
                for it in range(8):
                    f = 2 * it
                    if f % 4 == 0:
                        fox_rows(f // 4)
                    fox_max(f)
                    ssd_operands(it)
                    if it < 7:
                        ssd_mask(it + 1)
                    fox_norm(f)
                    ssd_evac(it)
                    fox_evac(f)
                    fox_max(f + 1)
                    fox_norm(f + 1)
                    fox_evac(f + 1)
                eng.wait_ge(m_z, 4 * (M + 1))
                eng.wait_ge(m_sev, SEV[8] * (M + 1))
                for t in range(4):
                    eng.tensor_tensor(proj[:, t, :], proj[:, t, :], proj[:, Z + t, :], ALU.mult).then_inc(m_gate, 1)
                for g in range(2):
                    eng.wait_ge(m_sd, 2 * M + g + 1)
                    r = ss[("am", "ab")[g]][:, :, :].rearrange("p a t -> p (a t)")
                    eng.reciprocal(r, r).then_inc(m_rn, 1)
                    eng.wait_ge(m_rn, 6 * M + 3 * g + 1)
                    if g == 0:
                        eng.wait_ge(m_gate, 4 * (M + 1))
                    for q in range(2):
                        t = 2 * g + q
                        eng.scalar_tensor_tensor(proj[:, t, :], proj[:, t, :], pc(f"norm_g_{l}", t), r, ALU.mult,
                                                 ALU.mult).then_inc(m_rn, 1)
                for t in range(DC):
                    src = proj[:, (XBC + t if t < 4 else FQ + t - 4 if t < 6 else BG + t - 6), :]
                    eng.wait_ge(s_hhi, w.h_chunks + t + 1)
                    eng.tensor_tensor(h_lo[:, t, :], src, h_hi[:, t, :].bitcast(F32), ALU.subtract).then_inc(s_hlo, 1)
                w.mixer += 1
                w.h_chunks += DC

            def rotate(x, tab, tmp, b, r):
                eng.wait_ge(r_sw, r + 1)
                eng.tensor_tensor(tmp, ps[:, 4 + b, :], tab[:, 1, :], ALU.mult).then_inc(r_out, 1)
                eng.tensor_tensor(x, x, tab[:, 0, :], ALU.mult).then_inc(r_out, 1)
                eng.wait_ge(r_out, 3 * r + 2)
                eng.tensor_tensor(x, x, tmp, ALU.add).then_inc(r_out, 1)

            def norm_gqa():
                eng.wait_ge(s_rope, 16)
                eng.wait_ge(s_evac, w.events)
                for j, (x, t, gain) in enumerate(GQA_JOBS):
                    b, o = j % 2, w.nout + 2 * j
                    eng.wait_ge(n_sd, w.nms + j + 1)
                    eng.reciprocal(gpt[:, b, :], gpt[:, b, :]).then_inc(n_out, 1)
                    eng.wait_ge(n_out, o + 1)
                    eng.scalar_tensor_tensor(x[:, t, :], x[:, t, :], pc(gain), gpt[:, b, :], ALU.mult, ALU.mult)\
                       .then_inc(n_out, 1)
                    eng.wait_ge(n_out, o + 2)
                    rotate(x[:, t, 0:SEQ], gcos, gp[:, b, 0:SEQ], b, w.rope + j)
                n = len(GQA_JOBS)
                w.nms, w.nout, w.rope = w.nms + n, w.nout + 2 * n, w.rope + n

            def norm_mla():
                eng.wait_ge(s_rope, 32)
                eng.wait_ge(s_evac, w.events)
                o = w.nout
                for p, (x, n, width, gain) in enumerate(((ckv, KVC, KEYS, "mkv_norm"), (cq, QC, SEQ, "mq_norm"))):
                    r = msd[:, p, 0:width]
                    eng.wait_ge(n_sd, w.nms + p + 1)
                    eng.reciprocal(r, r).then_inc(n_out, 1)
                    o += 1
                    eng.wait_ge(n_out, o)
                    for t in range(n):
                        eng.scalar_tensor_tensor(x[:, t, :], x[:, t, :], pc(gain, t), r, ALU.mult, ALU.mult)\
                           .then_inc(n_out, 1)
                    o += n
                eng.wait_ge(n_out, o)
                for t in range(QC + KVC):
                    eng.wait_ge(s_hhi, w.h_chunks + t + 1)
                    x, hi, lo = (ckv, ckvn_hi, ckvn_lo) if t < KVC else (cq, cqn_hi, cqn_lo)
                    c = t if t < KVC else t - KVC
                    eng.tensor_tensor(lo[:, c, :], x[:, c, :], hi[:, c, :].bitcast(F32), ALU.subtract).then_inc(s_hlo, 1)
                rotate(kpe[:, 0:SEQ], mcos, msd[:, 0, 0:SEQ], 0, w.rope)
                w.nms, w.nout, w.rope, w.h_chunks = w.nms + 2, o, w.rope + 1, w.h_chunks + QC + KVC

            def rope_mla():
                eng.wait_ge(s_evac, w.events)
                for j in range(4):
                    if j >= 2:
                        eng.wait_ge(r_out, 3 * (w.rope + j - 1))
                    rotate(qpe[:, j, :], mcos, mp[:, j % 2, 0:SEQ], j % 2, w.rope + j)
                w.rope += 4

            def attention(kind):
                a = ATT[kind]
                eng.wait_ge(r_out, 3 * w.rope)
                for n_tiles, c0, k0, nk in a["runs"]:
                    T0 = w.att
                    with eng.Fori(0, n_tiles) as it:
                        qc = bass.ds(it * P + c0, P)
                        if kind == "mla":
                            eng.tensor_copy(qpes[:, :, :], qpe[:, :, qc])
                        eng.tensor_copy(a["qs"][:, :, :], a["q"][:, :, qc]).then_inc(t_q, 1)

                        def half(g):
                            eng.wait_ge(t_o, it * 2 + (2 * T0 + g + 1))
                            r = psumr[:, 8 * g:8 * g + 8]
                            eng.reciprocal(r, r).then_inc(t_row, 1)
                            eng.wait_ge(t_row, it * 4 + (4 * T0 + 2 * g + 1))
                            eng.tensor_tensor(a["row"][:, g * 512:(g + 1) * 512].rearrange("p (h d) -> p h d", h=8),
                                              ps[:, 6, :].rearrange("p (h d) -> p h d", h=8),
                                              r.unsqueeze(2).broadcast_to([P, 8, HD]), ALU.mult).then_inc(t_row, 1)

                        for s in range(HEADS):
                            nm = nmax[:, s:s + 1]
                            eng.wait_ge(t_s, it * HEADS + (HEADS * T0 + s + 1))
                            eng.reduce_max(nm, flat(2 * (s % 2))[:, 0:nk], AX_X).then_inc(t_max, 1)
                            eng.wait_ge(t_max, it * (2 * HEADS) + (2 * HEADS * T0 + 2 * s + 1))
                            eng.tensor_scalar(nm, nm, -a["scale"], None, ALU.mult).then_inc(t_max, 1)
                            if s == 9:
                                half(0)
                        half(1)
                        eng.wait_ge(t_yt, it + (T0 + 1))
                        eng.tensor_scalar(a["q"][:, :, qc], ps[:, 4:6, :].rearrange("p a (j t) -> p (a j) t", t=P), 1.0, None,
                                          ALU.mult).then_inc(t_done, 1)
                    w.att += n_tiles
                eng.wait_ge(t_done, w.att)
                parts = [(h_hi, h_lo, q_t[:, :, 0:SEQ]), (hc_hi, hc_lo, q_t[:, :, SEQ:])] if kind == "gqa" else \
                        [(y2_hi, y2_lo, mq[:, :, :])]
                for i, (hi, lo, y) in enumerate(parts):
                    for k in range(DC):
                        eng.wait_ge(s_hhi, w.h_chunks + i * DC + k + 1)
                        eng.tensor_tensor(lo[:, k, :], y[:, k, :], hi[:, k, :].bitcast(F32), ALU.subtract)\
                           .then_inc(s_hlo, 1)
                w.h_chunks += DC * len(parts)

            for j, item in enumerate(sched):
                if j in early:
                    prologue(sched[early[j]][1])
                if item[0] == "lin":
                    if j not in early.values():
                        prologue(item[1])
                    linear(item[1])
                elif item[0] == "ln":
                    layer_norm(*item[1:])
                elif item[0] == "mod":
                    modulate(*item[1:])
                elif item[0] == "mixer":
                    mixer(item[1])
                elif item[0] == "gqa":
                    norm_gqa()
                    attention("gqa")
                elif item[0] == "mla_norm":
                    norm_mla()
                elif item[0] == "mla":
                    rope_mla()
                    attention("mla")


STOP = 0


def kernel(**inputs):
    import numpy as np
    import concourse.bacc as bacc
    from concourse.bass_utils import run_bass_kernel_spmd as run

    a = {k: np.asarray(v) for k, v in inputs.items()}
    t = {}

    def tiles(w, kc, per):
        n = w.shape[1] // P
        return np.ascontiguousarray(w.reshape(kc, P, n // per, per, P).transpose(2, 1, 3, 0, 4)
                                    .reshape(n // per, P, per * kc * P))

    def rows(w, kc, n):
        m = w.shape[1] // n
        return np.ascontiguousarray(w.reshape(kc, P, n, m).transpose(2, 1, 0, 3).reshape(n, P, kc * m))

    def cols_of(v):
        return np.asarray(v).reshape(-1, P).T

    t["xT"] = np.ascontiguousarray(a["x"][0].T)
    t["ctxT"] = np.ascontiguousarray(a["ctx_2"][0].T)
    for l in range(DEPTH):
        for s in range(3):
            t[f"ada_{3 * l + s}"] = tiles(a["ada_w"][l][:, s * 3 * D:(s + 1) * 3 * D], DC, 2)
        for s in range(2):
            t[f"ada_{6 + 2 * l + s}"] = tiles(a["w_ada_2"][l][:, s * 3 * D:(s + 1) * 3 * D], DC, 2)
        for which in (1, 2):
            w_in, w_out = a[f"ffn{which}_w_in"][l], a[f"ffn{which}_w_out"][l]
            c0 = 0
            for g, nc_ in enumerate(FF_GROUPS):
                part = slice(c0 * P, (c0 + nc_) * P)
                gate, up = w_in[:, :FF][:, part], w_in[:, FF:][:, part]
                both = np.stack([gate.reshape(D, nc_, P), up.reshape(D, nc_, P)], axis=2).reshape(D, 2 * nc_ * P)
                t[f"ffn{which}_in_{l}_{g}"] = tiles(both, DC, 2)
                t[f"ffn{which}_out_{l}_{g}"] = tiles(w_out[part], nc_, 1)
                c0 += nc_
        w = a["mix_w_in"][l]
        z, xbc, dt, q, k, v, f, bg, cg, xin = np.split(w, np.cumsum([512, 1024, 8, 256, 256, 256, 4, 256, 256]), axis=1)
        t[f"mix_in_{l}"] = tiles(np.concatenate([xbc, z, q, k, cg, xin, bg], axis=1), DC, 2)
        t[f"mix_v_{l}"] = rows(v, DC, 1)
        t[f"mix_dt_{l}"] = rows(np.concatenate([dt, f], axis=1), DC, 1)
        t[f"mix_out_{l}"] = tiles(a["mix_w_out"][l], DC, 2)
        n2 = FF2 // P // G2
        for g in range(n2):
            part = slice(g * G2 * P, (g + 1) * G2 * P)
            t[f"mlp_in_{l}_{g}"] = tiles(a["mlp_w1_2"][l][:, part], DC, 2)
            t[f"mlp_out_{l}_{g}"] = tiles(a["mlp_w2_2"][l][part], G2, 2)
    order = [h for j in range(DC) for h in (8 * (j // 4) + j % 4, 8 * (j // 4) + 4 + j % 4)]
    wq, wk, wv = np.split(a["gqa_w_qkv_2"][0], [HEADS * HD, (HEADS + GQA_KV) * HD], axis=1)
    t["gqa_q"] = tiles(wq.reshape(D, HEADS, HD)[:, order].reshape(D, D), DC, 2)
    t["gqa_k"] = tiles(wk, DC, 2)
    t["gqa_v"] = rows(wv, DC, 1)
    t["gqa_o"] = tiles(a["gqa_w_o_2"][0].reshape(HEADS, HD, D)[order].reshape(D, D), DC, 2)
    wc, wckv, wkpe = np.split(a["mla_w_in_2"][0], [QC * P, (QC + KVC) * P], axis=1)
    t["mla_cq"] = tiles(wc, DC, 1)
    t["mla_ckv"] = tiles(wckv, DC, KVC)
    t["mla_kpe"] = tiles(np.concatenate([wkpe] * 4, axis=1), DC, 1)
    uq = a["mla_w_uq_2"][0].reshape(QC * P, HEADS, HD + ROPE)
    t["mla_q"] = tiles(uq[:, :, :HD].reshape(QC * P, D), QC, 4)
    t["mla_qpe"] = tiles(uq[:, :, HD:].reshape(QC * P, HEADS * ROPE), QC, 4)
    ukv = a["mla_w_ukv_2"][0].reshape(KVC * P, HEADS, 2 * HD)
    t["mla_k"] = tiles(ukv[:, :, :HD].reshape(KVC * P, D), KVC, 8)
    t["mla_v"] = rows(ukv[:, :, HD:].reshape(KVC * P, D), KVC, 2)
    t["mla_o"] = tiles(a["mla_w_o_2"][0], DC, 2)

    def rope(dim):
        axis, quarter = dim // 2, dim // 4
        freq = np.float32(10000.0) ** (-np.arange(0, axis, 2, dtype=np.float32) / np.float32(axis))
        d = np.arange(P) % dim
        tok = np.arange(SEQ)
        pos = np.where((d // axis == 0)[:, None], tok // 64, tok % 64).astype(np.float32)
        ang = (pos * freq[d % quarter][:, None].astype(np.float32)).astype(np.float32)
        sign = np.where((d % axis) < quarter, -1.0, 1.0).astype(np.float32)[:, None]
        swap = np.zeros((P, P), np.float32)
        swap[np.arange(P) ^ quarter, np.arange(P)] = 1.0
        return np.stack([np.cos(ang), np.sin(ang) * sign], axis=1).astype(np.float32), swap

    t["rope_gqa"], swap16 = rope(HD)
    t["rope_mla"], swap8 = rope(ROPE)
    t["swaps"] = np.ascontiguousarray(np.stack([swap16, swap8], axis=1))

    cols, n = param_table()
    par = np.zeros((P, n), np.float32)

    def put(name, v):
        c0, width = cols[name]
        par[:, c0:c0 + width] = np.asarray(v).reshape(P, width)

    put("c1", cols_of(a["c"][0]))
    put("c2", np.stack([cols_of(a["c_2"][0]), cols_of(a["c_ctx_2"])], axis=2))
    put("ln_g_in", cols_of(a["ln_in_g"]))
    put("ln_b_in", cols_of(a["ln_in_b"]))
    for l in range(DEPTH):
        for s in range(3):
            put(f"ada_b_{3 * l + s}", cols_of(a["ada_b"][l][s * 3 * D:(s + 1) * 3 * D]))
            put(f"ln_g_b1_{l}_{s}", cols_of(a["ln_g"][l, s]))
            put(f"ln_b_b1_{l}_{s}", cols_of(a["ln_b"][l, s]))
        for s in range(2):
            put(f"ada_b_{6 + 2 * l + s}", cols_of(a["b_ada_2"][l][s * 3 * D:(s + 1) * 3 * D]))
            put(f"ln_g_b2_{l}_{s}", cols_of(a["ln_g_2"][l, s]))
            put(f"ln_b_b2_{l}_{s}", cols_of(a["ln_b_2"][l, s]))
        put(f"conv_w_{l}", a["ssd_conv_w"][l].reshape(4, 8, P).transpose(2, 1, 0))
        put(f"conv_b_{l}", cols_of(a["ssd_conv_b"][l]))
        put(f"ssd_d_{l}", cols_of(np.repeat(a["ssd_d"][l], SSD_P)))
        put(f"norm_g_{l}", cols_of(a["ssd_norm_g"][l]))
        put(f"sconv_w_{l}", a["sconv_w"][l].reshape(3, 2, P).transpose(2, 1, 0))
        put(f"dt_bias_{l}", np.broadcast_to(np.concatenate([a["ssd_dt_bias"][l], a["fox_f_bias"][l]]), (P, 12)))
        put(f"a_log_{l}", np.broadcast_to(a["ssd_a_log"][l], (P, SSD_H)))
    put("q_norm", np.tile(a["gqa_q_norm_2"][0], 2))
    put("k_norm", np.tile(a["gqa_k_norm_2"][0], 2))
    put("mq_norm", cols_of(a["mla_q_norm_2"][0]))
    put("mkv_norm", cols_of(a["mla_kv_norm_2"][0]))
    t["params"] = par

    used = {"params", "swaps", "xT"} | {i[1].name for i in schedule(STOP) if i[0] == "lin"}
    t = {k: v for k, v in t.items() if not STOP or k in used or k.startswith(("ada_", "ctx", "rope"))}
    nc = bacc.Bacc("TRN2", target_bir_lowering=False, num_devices=1)
    t_in = {k: nc.dram_tensor(k, v.shape, F32, kind="ExternalInput").ap() for k, v in t.items()}
    out = nc.dram_tensor("outT", (D, SEQ), F32, kind="ExternalOutput").ap()
    build(nc, t_in, out, STOP)
    r = run(nc, [t], core_ids=[0])
    return np.ascontiguousarray(r.results[0]["outT"].T).reshape(1, SEQ, D)
```

```python
from contextlib import ExitStack

import concourse.bass as bass
from concourse import mybir

F32 = mybir.dt.float32
F32R = mybir.dt.float32r
ALU = mybir.AluOpType
ACT = mybir.ActivationFunctionType
AX_X = mybir.AxisListType.X

P = 128
D = 1024
DC = D // P
SEQ = 512
CTX = 256
KEYS = SEQ + CTX
DEPTH = 2
FF = 2816
FF_GROUPS = (12, 10)
FF2 = 4096
G2 = 8
SLOT = 2048
RAW = 4
UNROLL = 4
ALPHA = float((2 * DEPTH) ** 0.25)
LN_EPS, RMS_EPS, NORM_EPS = 1e-5, 1e-5, 1e-6
SSD_H, SSD_P = 8, 64
FOX_H, HD = 4, 64
XBC, Z, FQ, FK, CG, XIN, BG = 0, 8, 12, 14, 16, 18, 20
NPROJ = 22
NEG = -1e30
GQA_KV = 4
HEADS = 16
ROPE = 32
QC, KVC = 3, 2
MOD = 24
ADA_UNITS = MOD // 2
LOG1P = [1.0 / (2 * k + 1) for k in range(8)]


class Linear:

    def __init__(self, name, n, tpu, kc, evac, out=P, ada=None, streams=("lat",), src="h", row=0, dst=None):
        self.name, self.n, self.tpu, self.kc, self.evac, self.out = name, n, tpu, kc, evac, out
        self.ada, self.streams, self.src, self.row, self.dst = ada, streams, src, row, dst
        self.width = tpu * kc * out
        self.spu = 2 if ada else 1
        self.tiles = row if row else tpu
        self.events = 1 if evac == "gateup" else self.tiles
        self.nbuf = 4 if row or (self.tiles >= 2 and len(streams) == 1) else 2


def schedule(stop):
    both = ("lat", "ctx")
    s = [("ln", "in", "lat", LN_EPS), ("ada0",), ("mod", 0, "lat")]

    def lin(*a, **k):
        s.append(("lin", Linear(*a, **k)))

    def ffn(l, which, ada):
        for g, nc in enumerate(FF_GROUPS):
            lin(f"ffn{which}_in_{l}_{g}", nc, 2, DC, "gateup", ada=ada if g == 0 else (7, 0) if (l, which) == (0, 1) else None)
            lin(f"ffn{which}_out_{l}_{g}", DC, 1, nc, "resid", src="hid")

    for l in range(DEPTH):
        ffn(l, 1, (3 * l + 1, 0))
        s += [("ln", f"b1_{l}_0", "lat", LN_EPS), ("mod", 3 * l + 1, "lat")]
        if stop == 1:
            return s
        lin(f"mix_in_{l}", NPROJ // 2, 2, DC, "copy", ada=(3 * l + 2, 0), dst="proj")
        lin(f"mix_v_{l}", 1, 1, DC, "rowcopy", out=FOX_H * HD, ada=(3 * l + 2, NPROJ // 2), row=4, dst="vrow")
        lin(f"mix_dt_{l}", 1, 1, DC, "rowcopy", out=SSD_H + FOX_H, ada=(7, FF_GROUPS[1] + l), row=4, dst="dtrow")
        s.append(("mixer", l))
        lin(f"mix_out_{l}", DC // 2, 2, DC, "resid")
        s += [("ln", f"b1_{l}_1", "lat", LN_EPS), ("mod", 3 * l + 2, "lat")]
        if stop == 2:
            return s
        ffn(l, 2, (3 * l + 3, 0))
        s += [("ln", f"b1_{l}_2", "lat", LN_EPS), ("mod", 3 * l + 3, "lat")]
        if stop == 3:
            return s
    s.append(("mod", 6, "ctx"))
    if stop == 4:
        return s
    lin("gqa_q", DC // 2, 2, DC, "copy", streams=both, dst="q")
    lin("gqa_k", 1, 2, DC, "copy", streams=both, dst="k")
    lin("gqa_v", 1, 1, DC, "rowcopy", out=GQA_KV * HD, row=6, streams=both, dst="gv")
    s.append(("gqa",))
    lin("gqa_o", DC // 2, 2, DC, "resid", streams=both)
    for st in both:
        s += [("ln", "b2_0_0", st, NORM_EPS), ("mod", 7, st)]
    if stop == 5:
        return s
    for g in range(FF2 // P // G2):
        lin(f"mlp_in_0_{g}", G2 // 2, 2, DC, "relu2", streams=both, ada=(8, 4 * g) if g < 3 else None)
        lin(f"mlp_out_0_{g}", DC // 2, 2, G2, "resid", src="hid", streams=both, ada=(9, 4 * g) if g < 3 else None)
    for st in both:
        s += [("ln", "b2_0_1", st, NORM_EPS), ("mod", 8, st)]
    if stop == 6:
        return s
    lin("mla_ckv", 1, KVC, DC, "copy", streams=both, dst="ckv")
    lin("mla_kpe", 1, 1, DC, "copy", streams=both, dst="kpe")
    lin("mla_cq", QC, 1, DC, "copy", dst="cq")
    s.append(("mla_norm",))
    lin("mla_k", 1, 8, KVC, "copy", streams=both, src="ckvn", dst="mk")
    lin("mla_v", 2, 1, KVC, "rowcopy", out=512, row=6, streams=both, src="ckvn", dst="mv")
    lin("mla_q", 2, 4, QC, "copy", src="cqn", dst="mq")
    lin("mla_qpe", 1, 4, QC, "copy", src="cqn", dst="qpe")
    s.append(("mla",))
    lin("mla_o", DC // 2, 2, DC, "resid", src="y2")
    s += [("ln", "b2_1_0", "lat", NORM_EPS), ("mod", 9, "lat")]
    if stop == 7:
        return s
    for g in range(FF2 // P // G2):
        lin(f"mlp_in_1_{g}", G2 // 2, 2, DC, "relu2")
        lin(f"mlp_out_1_{g}", DC // 2, 2, G2, "resid", src="hid")
    s.append(("ln", "b2_1_1", "lat", NORM_EPS))
    return s


def vectors(m):
    return 1 if m < 6 else 2


def ada_parts(m):
    return DC * vectors(m) - 1


def number(sched):
    units = tiles = events = ada = parts = 0
    unit_tiles = []
    occupant = []
    last_bank = 0
    ada_done = {}
    events = 4

    def take_ada(which):
        nonlocal ada, parts
        occupant.append(("ada", ada))
        ada += 1
        parts += ada_parts(which)
        ada_done[which] = ada

    for item in sched:
        if item[0] == "ada0":
            for i in range(ADA_UNITS):
                take_ada(0)
        elif item[0] == "lin":
            ln = item[1]
            ln.g0, ln.t0, ln.e0, ln.G0, ln.a0 = units, tiles, events, len(occupant), ada
            ln.p0 = parts
            ln.e_first = events - 1 if last_bank else events
            last_bank = (ln.row - 1) % 4 if ln.row else (ln.n * ln.tpu - 1) % ln.nbuf
            for i in range(ln.n):
                occupant.append(("main", units))
                if ln.ada:
                    take_ada(ln.ada[0])
                units += 1
                tiles += ln.tiles
                unit_tiles.append(tiles)
            events += ln.n * ln.events
    return unit_tiles, occupant, ada_done


def steps(eng, lo, hi):
    full = (hi - lo) // UNROLL
    first = 0
    if full >= 2:
        with eng.Fori(0, full) as it:
            for u in range(UNROLL):
                yield it, u, it * UNROLL + (lo + u)
        first = full * UNROLL
    for i in range(first, hi - lo):
        yield i // UNROLL, i % UNROLL, lo + i


def at(i, n=1):
    return bass.ds(i, n)


def param_table():
    cols, n = {}, 0

    def add(name, width):
        nonlocal n
        cols[name] = (n, width)
        n += width

    add("c1", DC)
    add("c2", 2 * DC)
    for m in range(10):
        add(f"ada_b_{m}", MOD)
    for name in ["in"] + [f"b1_{l}_{i}" for l in range(DEPTH) for i in range(3)] + \
            [f"b2_{l}_{i}" for l in range(DEPTH) for i in range(2)]:
        add(f"ln_g_{name}", DC)
        add(f"ln_b_{name}", DC)
    for l in range(DEPTH):
        add(f"conv_w_{l}", 8 * 4)
        add(f"conv_b_{l}", 8)
        add(f"ssd_d_{l}", 4)
        add(f"norm_g_{l}", 4)
        add(f"sconv_w_{l}", 2 * 3)
        add(f"dt_bias_{l}", SSD_H + FOX_H)
        add(f"a_log_{l}", SSD_H)
    add("q_norm", 1)
    add("k_norm", 1)
    add("mq_norm", QC)
    add("mkv_norm", KVC)
    return cols, n


def build(nc, t_in, out, stop):
    sched = schedule(stop)
    unit_tiles, occupant, ada_done = number(sched)
    cols, n_params = param_table()

    with ExitStack() as ctx:
        arena_bytes = 212800
        arena = ctx.enter_context(nc.sbuf_tensor("arena", [P, arena_bytes // 4], F32))
        base = 16512
        used = {}

        def place(name, shape, dt, offset):
            size = 4
            for d in shape[1:]:
                size *= d
            used[name] = (offset, offset + size)
            assert offset + size <= arena_bytes, (name, offset + size)
            return nc.alloc_sbuf_tensor_at(name, shape, dt, offset=base + offset)

        def after(*names):
            return (max(used[n][1] for n in names) + 31) // 32 * 32

        def sem(name):
            return ctx.enter_context(nc.semaphore(name))

        x_lat = place("x_lat", [P, DC, SEQ], F32, 0)
        h_hi = place("h_hi", [P, DC, SEQ], F32R, after("x_lat"))
        h_lo = place("h_lo", [P, DC, SEQ], F32R, after("h_hi"))
        raw = place("raw", [P, RAW, SLOT], F32, after("h_lo"))
        w_hi = place("w_hi", [P, 2, SLOT], F32R, after("raw"))
        w_lo = place("w_lo", [P, 2, SLOT], F32R, after("w_hi"))
        par = place("par", [P, n_params], F32, after("w_lo"))
        ident = place("ident", [P, P], F32, after("par"))
        ones = place("ones", [P, P], F32, after("ident"))
        tri = place("tri", [P, P], F32, after("ones"))
        past = place("past", [P, 4, P], F32, after("tri"))
        negmask = place("negmask", [P, P], F32, after("past"))
        blocks = place("blocks", [P, P], F32, after("negmask"))
        swaps = place("swaps", [P, 2, P], F32, after("blocks"))
        c_act = place("c_act", [P, 3 * DC], F32, after("swaps"))
        mod_lat = place("mod_lat", [P, MOD], F32, after("c_act"))
        mod_ctx = place("mod_ctx", [P, MOD], F32, after("mod_lat"))
        eps_t = place("eps_t", [P, 3], F32, after("mod_ctx"))
        nmax = place("nmax", [P, HEADS], F32, after("eps_t"))
        psumr = place("psumr", [P, HEADS], F32, after("nmax"))
        ctx0 = (after("psumr") + 63) // 64 * 64
        x_ctx = place("x_ctx", [P, DC, CTX], F32, ctx0)
        hc_hi = place("hc_hi", [P, DC, CTX], F32R, after("x_ctx"))
        hc_lo = place("hc_lo", [P, DC, CTX], F32R, after("hc_hi"))
        ones_r = place("ones_r", [P, P], F32R, arena_bytes - 4 * P)
        kept = place("kept", [P, 2 * MOD], F32, arena_bytes - 4 * P - 8 * MOD)
        A = after("hc_lo")
        hid_hi = place("hid_hi", [P, 12, SEQ], F32R, A)
        hid_lo = place("hid_lo", [P, 12, SEQ], F32R, after("hid_hi"))
        hid2_hi = place("hid2_hi", [P, G2, SEQ], F32R, A)
        hid2_lo = place("hid2_lo", [P, G2, SEQ], F32R, after("hid2_hi"))
        hidc_hi = place("hidc_hi", [P, G2, CTX], F32R, after("hid2_lo"))
        hidc_lo = place("hidc_lo", [P, G2, CTX], F32R, after("hidc_hi"))
        gate_t = place("gate_t", [P, 2, SEQ], F32, after("hid_lo"))
        val_t = place("val_t", [P, 2, SEQ], F32, after("gate_t"))
        relu_t = place("relu_t", [P, 2, KEYS], F32, after("hidc_lo"))
        sq = place("sq", [P, DC, SEQ], F32, A)
        h32 = place("h32", [P, 4, SEQ], F32, after("sq"))
        ada_acc = place("ada_acc", [P, 2, 2, 2 * P], F32, after("val_t"))
        rstd = place("rstd", [P, SEQ], F32, after("h32"))
        x_sum = {"lat": place("x_sum_lat", [P, SEQ], F32, after("ada_acc")),
                 "ctx": place("x_sum_ctx", [P, CTX], F32, after("relu_t"))}
        assert after("x_sum_lat") <= used["kept"][0] and after("x_sum_ctx") <= after("val_t")
        proj = place("proj", [P, NPROJ, SEQ], F32, A)
        vrow = place("vrow", [P, 4, FOX_H * HD], F32, after("proj"))
        xrow = place("xrow", [P, 4, SSD_H * SSD_P], F32, after("vrow"))
        brow = place("brow", [P, 4, 2 * P], F32, after("xrow"))
        dtrow = place("dtrow", [P, 4, 12], F32, after("brow"))
        sp = {n: place(f"sp_{n}", [P, 4, 12], F32, after("dtrow") + 192 * i)
              for i, n in enumerate(["v", "n", "e", "d", "z", "z2", "p", "dt"])}
        a_row = place("a_row", [P, 4, SSD_H], F32, after("sp_dt"))
        logf = place("logf", [P, 4, FOX_H], F32, after("a_row"))
        a_head = place("a_head", [P, SSD_H], F32, after("logf"))
        cacc = place("cacc", [P, 4, SEQ], F32, used["h_hi"][0])
        fcum = place("fcum", [P, 4, SEQ], F32, used["h_lo"][0])
        s_names = ["am", "ab", "lmat", "emat", "mmat", "cdec"]
        ss = {n: place(f"ss_{n}", [P, 4, P], F32, ctx0 + 2048 * i) for i, n in enumerate(s_names)}
        xdt = place("xdt", [P, 4, SSD_P], F32, after("ss_cdec"))
        xdec = place("xdec", [P, 4, SSD_P], F32, after("xdt"))
        state = place("state", [P, 2, 4 * SSD_P], F32, after("xdec"))
        cbm = place("cbm", [P, P], F32, after("state"))
        decs = place("decs", [P, 8], F32, after("cbm"))
        fprob = place("fprob", [P, SEQ], F32, after("decs"))
        fprobT = place("fprobT", [P, 4, P], F32, after("fprob"))
        assert after("fprobT") <= A
        q_t = place("q_t", [P, DC, KEYS], F32, A)
        k_t = place("k_t", [P, 2, KEYS], F32, after("q_t"))
        gv = place("gv", [P, 6, GQA_KV * HD], F32, after("k_t"))
        gp = place("gp", [P, 2, KEYS], F32, after("gv"))
        gpt = place("gpt", [P, 2, KEYS], F32, after("gp"))
        gcos = place("gcos", [P, 2, SEQ], F32, after("gpt"))
        gk_hi = place("gk_hi", [P, 2, KEYS], F32R, after("gcos"))
        gdiag = place("gdiag", [P, 2, SEQ], F32R, after("gk_hi"))
        assert after("gdiag") <= used["kept"][0]
        gq_hi = place("gq_hi", [P, DC, KEYS], F32R, used["w_hi"][0])
        gv_hi = place("gv_hi", [P, 6, GQA_KV * HD], F32R, after("gq_hi"))
        grec = place("grec", [P, SEQ], F32, after("gv_hi"))
        assert after("grec") <= used["par"][0]
        gq_lo = place("gq_lo", [P, DC, KEYS], F32R, used["q_t"][0])
        gk_lo = place("gk_lo", [P, 2, KEYS], F32R, used["k_t"][0])
        gv_lo = place("gv_lo", [P, 6, GQA_KV * HD], F32R, used["gv"][0])
        gprob = place("gprob", [P, 3, SEQ], F32, used["gp"][0])
        gp_lo = place("gp_lo", [P, 3, SEQ], F32R, used["gp"][0])
        gp_hi = place("gp_hi", [P, 3, SEQ], F32R, after("gp_lo"))
        assert after("gp_hi") <= used["gcos"][0]
        mk = place("mk", [P, DC, KEYS], F32, A)
        mv = place("mv", [P, 6, D], F32, after("mk"))
        kpe = place("kpe", [P, KEYS], F32, after("mv"))
        mcos = place("mcos", [P, 2, SEQ], F32, after("kpe"))
        mp = place("mp", [P, 2, KEYS], F32, ctx0)
        mq_hi = place("mq_hi", [P, DC, SEQ], F32R, ctx0)
        mdiag = place("mdiag", [P, 2, SEQ], F32R, after("mq_hi"))
        assert after("mdiag") <= A
        mprob = place("mprob", [P, 3, SEQ], F32, after("mcos"))
        mp_lo = place("mp_lo", [P, 3, SEQ], F32R, after("mcos"))
        assert after("mp_lo") <= used["kept"][0]
        msq = place("msq", [P, QC + KVC, KEYS], F32, A)
        msd = place("msd", [P, 2, KEYS], F32, after("msq"))
        cq = place("cq", [P, QC, SEQ], F32, used["mv"][0])
        ckv = place("ckv", [P, KVC, KEYS], F32, after("cq"))
        mq = place("mq", [P, DC, SEQ], F32, used["h_hi"][0])
        qpe = place("qpe", [P, 4, SEQ], F32, after("mq"))
        mp_hi = place("mp_hi", [P, 3, SEQ], F32R, after("qpe"))
        assert after("mp_hi") <= used["raw"][0]
        mk_hi = place("mk_hi", [P, DC, KEYS], F32R, used["w_hi"][0])
        kpe_hi = place("kpe_hi", [P, KEYS], F32R, after("mk_hi"))
        mrec = place("mrec", [P, SEQ], F32, after("kpe_hi"))
        assert after("mrec") <= used["par"][0]
        mv_hi = place("mv_hi", [P, 6, D], F32R, used["raw"][0])
        qpe_hi = place("qpe_hi", [P, 4, SEQ], F32R, after("mv_hi"))
        assert after("qpe_hi") <= used["w_hi"][0]
        mk_lo = place("mk_lo", [P, DC, KEYS], F32R, used["mk"][0])
        mv_lo = place("mv_lo", [P, 6, D], F32R, used["mv"][0])
        kpe_lo = place("kpe_lo", [P, KEYS], F32R, used["kpe"][0])
        mq_lo = place("mq_lo", [P, DC, SEQ], F32R, used["mq"][0])
        qpe_lo = place("qpe_lo", [P, 4, SEQ], F32R, used["qpe"][0])
        cqn_hi = place("cqn_hi", [P, QC, SEQ], F32R, ctx0)
        cqn_lo = place("cqn_lo", [P, QC, SEQ], F32R, after("cqn_hi"))
        ckvn_hi = place("ckvn_hi", [P, KVC, KEYS], F32R, after("cqn_lo"))
        ckvn_lo = place("ckvn_lo", [P, KVC, KEYS], F32R, after("ckvn_hi"))
        assert after("ckvn_lo") <= A
        y2_hi = place("y2_hi", [P, DC, SEQ], F32R, A)
        y2_lo = place("y2_lo", [P, DC, SEQ], F32R, after("y2_hi"))

        ps = ctx.enter_context(nc.psum_tensor("ps", [P, 8, SEQ], F32))
        B_MEAN, B_VAR, B_ADA = 4, 5, 7

        X = {"lat": x_lat, "ctx": x_ctx}
        H = {"lat": (h_hi, h_lo), "ctx": (hc_hi, hc_lo)}
        HID = {"lat": (hid2_hi, hid2_lo), "ctx": (hidc_hi, hidc_lo)}
        MODT = {"lat": mod_lat, "ctx": mod_ctx}
        NT = {"lat": SEQ, "ctx": CTX}
        COL0 = {"lat": 0, "ctx": SEQ}

        def pc(name, i=0, n=1):
            return par[:, cols[name][0] + i:cols[name][0] + i + n]

        def operand(ln, st):
            if ln.src == "hid":
                return HID[st] if ln.name.startswith("mlp") else (hid_hi, hid_lo)
            if ln.src == "ckvn":
                return ckvn_hi[:, :, COL0[st]:COL0[st] + NT[st]], ckvn_lo[:, :, COL0[st]:COL0[st] + NT[st]]
            return {"h": H[st], "cqn": (cqn_hi, cqn_lo), "y2": (y2_hi, y2_lo)}[ln.src]

        def dest(ln, st, i):
            c0, n = COL0[st], NT[st]
            return {"proj": lambda: proj[:, at(i), :], "q": lambda: q_t[:, at(i), c0:c0 + n],
                    "k": lambda: k_t[:, at(i), c0:c0 + n], "ckv": lambda: ckv[:, at(i), c0:c0 + n],
                    "kpe": lambda: kpe[:, c0:c0 + n].unsqueeze(1), "cq": lambda: cq[:, at(i), :],
                    "mk": lambda: mk[:, at(i), c0:c0 + n], "mq": lambda: mq[:, at(i), :],
                    "qpe": lambda: qpe[:, at(i), :]}[ln.dst]()

        def row_dest(ln, unit, t):
            return {"vrow": lambda: vrow[:, t, :], "dtrow": lambda: dtrow[:, t, :], "gv": lambda: gv[:, t, :],
                    "mv": lambda: mv[:, t, unit * 512:(unit + 1) * 512]}[ln.dst]()

        def tile_bank(ln, tile, st):
            return tile % ln.nbuf + (2 if st == "ctx" else 0)

        s_par = sem("params_loaded")
        s_x = sem("x_loaded")
        s_rope = sem("rope_tables_loaded")
        s_raw = [sem(f"weights_loaded_{i}") for i in range(RAW)]
        s_out = sem("out_stored")
        s_const = sem("constants_ready")
        s_cact = sem("c_activated")
        s_whi = sem("weights_rounded")
        s_wlo = sem("weights_split")
        s_tile = sem("tile_ready")
        s_part = sem("ada_partial_products")
        s_ada = sem("ada_unit_used")
        s_asum = sem("ada_unit_summed")
        s_keep = sem("ada_sums_kept")
        s_evac = sem("tile_evacuated")
        s_gate = sem("gate_activated")
        s_hidhi = sem("hidden_rounded")
        s_hid = sem("hidden_split")
        s_sum = sem("ln_sums")
        s_xsum = sem("ln_partial_sums")
        s_pair = sem("ln_squares_paired")
        s_cent = sem("ln_centred")
        s_sq = sem("ln_squared")
        s_dev = sem("ln_deviation")
        s_rstd = sem("ln_rstd")
        s_scal = sem("ln_scaled")
        s_aff = sem("ln_affine")
        s_mod = sem("modulation_steps")
        s_h32 = sem("h_modulated")
        s_hhi = sem("h_rounded")
        s_hlo = sem("h_split")
        s_xa = sem("x_times_alpha")

        m_sp = sem("softplus_steps")
        m_spe = sem("softplus_exp")
        m_ahd = sem("a_head_exp")
        m_conv = sem("conv_taps")
        m_silu = sem("conv_activated")
        m_tr = sem("rows_transposed")
        m_rows = sem("rows_copied")
        m_ab = sem("ssd_a_spread")
        m_am = sem("ssd_a_masked")
        m_pre = sem("ssd_exponents")
        m_sexp = sem("ssd_decays")
        m_mul = sem("ssd_operands")
        m_y = sem("ssd_products")
        m_sev = sem("ssd_evacuated")
        m_z = sem("z_activated")
        m_gate = sem("ssd_gated")
        m_ysq = sem("ssd_squared")
        m_ms = sem("ssd_mean_squares")
        m_sd = sem("ssd_deviations")
        m_rn = sem("ssd_normed")
        m_qs = sem("fox_q_scaled")
        m_fg = sem("fox_forget_rows")
        m_fs = sem("fox_scores")
        m_fmax = sem("fox_maxima")
        m_fp = sem("fox_exp")
        m_fn = sem("fox_normed")
        m_ftr = sem("fox_transposed")
        m_fpt = sem("fox_probs_copied")
        m_fo = sem("fox_outputs")
        m_fy = sem("fox_evacuated")
        m_sc = sem("sconv_steps")
        n_sq = sem("norm_squared")
        n_ms = sem("norm_mean_squares")
        n_sd = sem("norm_deviations")
        n_out = sem("normed")
        r_sw = sem("rope_swapped")
        r_out = sem("rope_steps")
        t_sh = sem("att_operands_rounded")
        t_sl = sem("att_operands_split")
        t_s = sem("att_scores_for_max")
        t_mx = sem("att_maxima")
        t_cm = sem("att_maxima_joined")
        t_dg = sem("att_max_diagonal")
        t_st = sem("att_scores")
        t_p = sem("att_exp")
        t_pt = sem("att_probs_rounded")
        t_pl = sem("att_probs_split")
        t_pv = sem("att_block_summed")
        t_rc = sem("att_reciprocals")
        t_y = sem("att_head_done")

        SEV = []
        for c in range(4):
            for g in range(2):
                SEV.append((SEV[-1] + last if SEV else 0))
                last = 2 + (1, 2, 2, 0)[c]
        SEV.append(SEV[-1] + last)
        PAIRS = ((4, 5), (6, 7), (0, 1), (2, 3))
        NSP = 20
        NSC = 2 + 6 + 2

        def flat(bank):
            return ps[:, bank:bank + 2, :].rearrange("p a t -> p (a t)")[:, 0:KEYS]

        def parts(x, hi, lo, tiles):
            return [(x[:, t, :], hi[:, t, :], lo[:, t, :]) for t in tiles]

        mla_split = [(kpe[:, :], kpe_hi[:, :], kpe_lo[:, :]), (qpe[:, :, :], qpe_hi[:, :, :], qpe_lo[:, :, :])]
        for t in range(DC):
            mla_split += parts(mk, mk_hi, mk_lo, [t]) + parts(mq, mq_hi, mq_lo, [t])
        ATT = {"gqa": dict(q=(gq_hi, gq_lo), k=(gk_hi, gk_lo), v=(gv_hi, gv_lo), prob=gprob, p=(gp_hi, gp_lo), diag=gdiag,
                           rec=grec, y=q_t, scale=HD ** -0.5, ready=lambda tile: 3 + tile,
                           split=parts(k_t, gk_hi, gk_lo, range(2)) + parts(q_t, gq_hi, gq_lo, range(DC)) +
                                 [(gv[:, :, :], gv_hi[:, :, :], gv_lo[:, :, :])],
                           runs=[(0, SEQ, 0, KEYS), (SEQ, CTX, SEQ, CTX)]),
               "mla": dict(q=(mq_hi, mq_lo), k=(mk_hi, mk_lo), v=(mv_hi, mv_lo), prob=mprob, p=(mp_hi, mp_lo), diag=mdiag,
                           rec=mrec, y=mq, scale=(HD + ROPE) ** -0.5, ready=lambda tile: 4 + 2 * tile,
                           split=mla_split + parts(mv, mv_hi, mv_lo, range(KEYS // P)),
                           runs=[(0, SEQ, 0, KEYS)])}
        KEPT = {"gqa": 7, "mla": 9}
        RING = 3
        B_MAX, B_SUM, B_PT, B_OUT = 0, 2, 4, 6

        class Run:

            def __init__(self, c0, nq, k0, nk):
                self.q, self.nq, self.k0, self.nk, self.qt, self.kb = slice(c0, c0 + nq), nq, k0, nk, nq // P, nk // P
                self.c0 = c0
                self.units = [(t, c // SEQ, k0 + c, min(SEQ, nk - c)) for t in range(self.qt) for c in range(0, nk, SEQ)]
                self.n_runs = -(-nk // SEQ)
                per = -(-len(self.units) // max(1, self.kb - 2))
                self.share = [list(range(len(self.units)))[j * per:(j + 1) * per] for j in range(self.kb)]

        GQA_JOBS = [(q_t, j, "q_norm") for j in range(DC)] + [(k_t, j, "k_norm") for j in range(2)]

        early = {}
        for j, item in enumerate(sched):
            if (item[0] == "ln" and sched[j - 1][0] == "lin") or (item[0] == "mod" and sched[j - 1][0] == "ada0"):
                nxt = next((i for i in range(j, len(sched)) if sched[i][0] not in ("ln", "mod")), None)
                if nxt is not None and sched[nxt][0] == "lin":
                    early[j] = nxt

        class Walk:

            def __init__(self):
                self.ln = self.mod = self.mixer = 0
                self.hid = 0
                self.h_chunks = 0
                self.splits = 0
                self.units = self.heads = self.blocks = 0
                self.nsq = self.nms = self.nout = self.rope = 0
                self.events = 4
                self.xsum = 0

        def raw_ready(eng, g, it, spu):
            eng.wait_ge(s_raw[g % RAW], 16 * (g // RAW + 1) + it * (16 * spu))

        block = ctx.enter_context(nc.Block())

        @block.sync
        def _(eng):
            eng.dma_start(par[:, :], t_in["params"]).then_inc(s_par, 16)
            eng.dma_start(swaps[:, :, :], t_in["swaps"]).then_inc(s_par, 16)
            eng.dma_start(x_lat[:, :, :], t_in["xT"].rearrange("(c p) t -> p c t", p=P)).then_inc(s_x, 16)

            def slot_free(n):
                if n >= RAW:
                    kind, i = occupant[n - RAW]
                    eng.wait_ge(s_wlo if kind == "main" else s_ada, i + 1)

            def load_ada(which, i, slot):
                eng.dma_start(raw[:, slot, :], t_in[f"ada_{which}"][at(i)].rearrange("a p w -> p (a w)"))\
                   .then_inc(s_raw[slot], 16)

            n = 0
            for item in sched:
                if item[0] == "ada0":
                    for i in range(ADA_UNITS):
                        slot_free(n)
                        load_ada(0, i, n % RAW)
                        n += 1
                elif item[0] == "lin":
                    ln = item[1]
                    peel = min(ln.n, RAW // ln.spu)
                    w = t_in[ln.name]
                    if ln.name == "mla_o":
                        eng.wait_ge(t_y, HEADS * sum(len(a["runs"]) for a in ATT.values()))

                    def load(i, g):
                        eng.dma_start(raw[:, g % RAW, 0:ln.width], w[at(i)].rearrange("a p w -> p (a w)"))\
                           .then_inc(s_raw[g % RAW], 16)

                    for i in range(peel):
                        g = n + i * ln.spu
                        slot_free(g)
                        load(i, g)
                        if ln.ada:
                            slot_free(g + 1)
                            load_ada(ln.ada[0], ln.ada[1] + i, (g + 1) % RAW)
                    for it, u, i in steps(eng, peel, ln.n):
                        g = n + (peel + u) * ln.spu
                        eng.wait_ge(s_wlo, i + (ln.g0 - peel + 1))
                        load(i, g)
                        if ln.ada:
                            eng.wait_ge(s_ada, i + (ln.a0 - peel + 1))
                            load_ada(ln.ada[0], i + ln.ada[1], (g + 1) % RAW)
                    n += ln.n * ln.spu
                if item[0] == "lin" and item[1].name == "mix_out_1":
                    ln = item[1]
                    eng.wait_ge(s_tile, ln.t0 + 1)
                    eng.dma_start(x_ctx[:, :, :], t_in["ctxT"].rearrange("(c p) t -> p c t", p=P)).then_inc(s_x, 16)
                if item[0] == "lin" and item[1].name == "gqa_k":
                    eng.wait_ge(s_tile, item[1].t0 + 1)
                    eng.dma_start(gcos[:, :, :], t_in["rope_gqa"]).then_inc(s_rope, 16)
                if item[0] == "lin" and item[1].name == "mla_cq":
                    eng.wait_ge(s_tile, item[1].t0 + 1)
                    eng.dma_start(mcos[:, :, :], t_in["rope_mla"]).then_inc(s_rope, 16)
            n_aff = sum(DC for i in sched if i[0] == "ln")
            eng.wait_ge(s_aff, n_aff)
            if stop:
                eng.wait_ge(s_xa, sum(DC for i in sched if i[0] == "mod"))
            eng.dma_start(out.rearrange("(c p) t -> p c t", p=P), x_lat[:, :, :]).then_inc(s_out, 16)
            eng.wait_ge(s_out, 16)

        @block.gpsimd
        def _(eng):
            n = [0]

            def const(ins):
                ins.then_inc(s_const, 1)
                n[0] += 1

            const(eng.memset(ones[:, :], 1.0))
            const(eng.memset(ident[:, :], 0.0))
            const(eng.memset(negmask[:, :], 0.0))
            const(eng.memset(blocks[:, :], 0.0))
            const(eng.memset(past[:, :, :], 1.0))
            for i, e in enumerate((LN_EPS, RMS_EPS, NORM_EPS)):
                const(eng.memset(eps_t[:, i:i + 1], e))
            eng.wait_ge(s_const, n[0])
            const(eng.affine_select(out=ident[:, :], in_=ident[:, :], compare_op=ALU.not_equal, fill=1.0, base=0,
                                    pattern=[[-1, P]], channel_multiplier=1))
            const(eng.affine_select(out=tri[:, :], in_=ones[:, :], compare_op=ALU.is_ge, fill=0.0, base=0,
                                    pattern=[[1, P]], channel_multiplier=-1))
            const(eng.affine_select(out=past[:, 3, :], in_=past[:, 3, :], compare_op=ALU.is_gt, fill=0.0, base=0,
                                    pattern=[[-1, P]], channel_multiplier=1))
            const(eng.affine_select(out=negmask[:, :], in_=negmask[:, :], compare_op=ALU.is_ge, fill=NEG, base=0,
                                    pattern=[[-1, P]], channel_multiplier=1))
            for b in range(2):
                eng.wait_ge(s_const, n[0])
                const(eng.memset(blocks[b * HD:(b + 1) * HD, b * HD:(b + 1) * HD], 1.0))
            w = Walk()

            def partial_sums(streams, e0):
                for k in range(1, DC - 1):
                    if e0:
                        eng.wait_ge(s_evac, e0 + k + 1)
                    for st in streams:
                        if k > 1:
                            eng.wait_ge(s_xsum, w.xsum + (k - 2) * len(streams) + streams.index(st) + 1)
                        eng.tensor_tensor(x_sum[st][:, :], X[st][:, 0, :] if k == 1 else x_sum[st][:, :], X[st][:, k, :],
                                          ALU.add).then_inc(s_xsum, 1)
                w.xsum += (DC - 2) * len(streams)

            eng.wait_ge(s_const, n[0])
            eng.wait_ge(s_x, 16)
            partial_sums(("lat",), 0)
            for j, item in enumerate(sched):
                if item[0] == "lin" and sched[j + 1][0] == "ln":
                    partial_sums(item[1].streams, item[1].e0)
                elif item[0] == "mod":
                    x, h0 = X[item[2]], DC * w.mod
                    for k in range(DC):
                        eng.wait_ge(s_h32, h0 + k + 1)
                        eng.tensor_scalar(x[:, k, :], x[:, k, :], ALPHA, None, ALU.mult).then_inc(s_xa, 1)
                    w.mod += 1
                elif item[0] == "mixer":
                    b = 8 * w.mixer
                    eng.wait_ge(m_sp, NSP * (w.mixer + 1))
                    for it in range(8):
                        c, g = divmod(it, 2)
                        if it or w.mixer:
                            eng.wait_ge(m_pre, b + it)
                        eng.tensor_copy(ss["ab"][:, :, :], a_row[:, c, 4 * g:4 * g + 4].unsqueeze(2)
                                        .broadcast_to([P, 4, P])).then_inc(m_ab, 1)
                    w.mixer += 1

        N_CONST = 5 + 3 + 4 + 2

        @block.scalar
        def _(eng):
            w = Walk()
            eng.wait_ge(s_par, 32)
            eng.wait_ge(s_const, N_CONST)
            eng.activation(c_act[:, 0:DC], pc("c1", 0, DC), ACT.Silu).then_inc(s_cact, 1)
            eng.activation(c_act[:, DC:3 * DC], pc("c2", 0, 2 * DC), ACT.Silu).then_inc(s_cact, 1)
            eng.activation(ones_r[:, :], ones[:, :], ACT.Copy).then_inc(s_cact, 1)

            def round_weights(ln, i, it, pos):
                G = ln.G0 + pos * ln.spu
                raw_ready(eng, G, it, ln.spu)
                slot = (ln.g0 + pos) % 2
                eng.activation(w_hi[:, slot, 0:ln.width], raw[:, G % RAW, 0:ln.width], ACT.Copy).then_inc(s_whi, 1)

            def ahead(ln, lo=0, hi=2):
                for i in range(lo, min(hi, ln.n)):
                    if ln.g0 + i >= 2:
                        eng.wait_ge(s_tile, unit_tiles[ln.g0 + i - 2])
                    round_weights(ln, i, 0, i)

            def evacuate(ln, i, it, pos):
                if ln.evac == "gateup":
                    t = w.hid + i
                    eng.wait_ge(s_tile, i * 2 + (ln.t0 + 2))
                    eng.activation(gate_t[:, pos % 2, 0:SEQ], ps[:, tile_bank(ln, 2 * pos, "lat"), :], ACT.Silu)\
                       .then_inc(s_gate, 1)
                    eng.wait_ge(s_evac, i + (ln.e0 + 1))
                    eng.activation(hid_hi[:, at(i), :], val_t[:, pos % 2, 0:SEQ].unsqueeze(1), ACT.Copy)\
                       .then_inc(s_hidhi, 1)
                elif ln.evac == "relu2":
                    for q in range(2):
                        eng.wait_ge(s_tile, i * 2 + (ln.t0 + q + 1))
                        eng.wait_ge(s_hid, i * 2 + (w.hid + q - 1))
                        for st in ln.streams:
                            a = eng.activation(relu_t[:, q, COL0[st]:COL0[st] + NT[st]],
                                               ps[:, tile_bank(ln, 2 * pos + q, st), 0:NT[st]], ACT.Relu)
                        a.then_inc(s_gate, 1)
                    for q in range(2):
                        eng.wait_ge(s_evac, i * 2 + (ln.e0 + q + 1))
                        for st in ln.streams:
                            a = eng.activation(HID[st][0][:, at(i * 2 + q), :],
                                               relu_t[:, q, COL0[st]:COL0[st] + NT[st]].unsqueeze(1), ACT.Copy)
                        a.then_inc(s_hidhi, 1)

            def linear(ln, following):
                lag = min(2, ln.n)
                for it, u, i in steps(eng, lag, ln.n):
                    eng.wait_ge(s_tile, (i - 2) * ln.tiles + (ln.t0 + ln.tiles))
                    round_weights(ln, i, it, lag + u)
                    evacuate(ln, i - 2, it, u)
                finish(ln, lag, following)
                if ln.evac in ("gateup", "relu2"):
                    w.hid += ln.n * ln.events

            def finish(ln, lag, following):
                for j, i in enumerate(range(ln.n - lag, ln.n)):
                    first = ln.events > ln.nbuf or (ln.events > 1 and i == ln.n - 1)
                    if first:
                        evacuate(ln, i, 0, i)
                    if following:
                        ahead(following, j, j + 1)
                    if not first:
                        evacuate(ln, i, 0, i)
                if following:
                    ahead(following, lag, 2)

            def layer_norm(name, st, eps):
                x, n, nt = X[st], w.ln, NT[st] // P
                for k in range(DC):
                    eng.wait_ge(s_cent, DC * n + k + 1)
                    eng.activation(sq[:, k, 0:NT[st]], x[:, k, :], ACT.Square).then_inc(s_sq, 1)
                eng.wait_ge(s_sum, 2 * n + 2)
                e = 0 if eps == LN_EPS else 2
                eng.activation(rstd[:, 0:NT[st]], ps[:, B_VAR, 0:NT[st]], ACT.Sqrt, scale=1.0 / D, bias=eps_t[:, e:e + 1])\
                   .then_inc(s_dev, 1)
                for k in range(DC):
                    eng.wait_ge(s_scal, DC * n + k + 1)
                    eng.activation(x[:, k, :], x[:, k, :], ACT.Identity, bias=pc("ln_b_" + name, k),
                                   scale=pc("ln_g_" + name, k)).then_inc(s_aff, 1)
                w.ln += 1

            def modulate(m, st):
                hi = H[st][0]
                for k in range(DC):
                    eng.wait_ge(s_h32, DC * w.mod + k + 1)
                    eng.activation(hi[:, k, :], h32[:, k % 4, 0:NT[st]], ACT.Copy).then_inc(s_hhi, 1)
                w.mod += 1
                w.h_chunks += DC

            def mixer(l):
                M = w.mixer
                eng.activation(a_head[:, :], pc(f"a_log_{l}", 0, SSD_H), ACT.Exp).then_inc(m_ahd, 1)
                eng.wait_ge(m_sp, NSP * M + 4)
                eng.activation(sp["e"][:, :, :], sp["n"][:, :, :], ACT.Exp).then_inc(m_spe, 1)
                for p, pair in enumerate(PAIRS):
                    eng.wait_ge(m_conv, 32 * M + 8 * (p + 1))
                    for q, t in enumerate(pair):
                        eng.activation(proj[:, XBC + t, :], cacc[:, 2 * (p % 2) + q, :], ACT.Silu,
                                       bias=pc(f"conv_b_{l}", t)).then_inc(m_silu, 1)
                for t in range(4):
                    eng.activation(proj[:, Z + t, :], proj[:, Z + t, :], ACT.Silu).then_inc(m_z, 1)
                for c in range(4):
                    eng.wait_ge(m_tr, 4 * M + c + 1)
                    eng.activation(xrow[:, c, :], ps[:, 4, :], ACT.Copy).then_inc(m_rows, 1)
                    eng.activation(brow[:, c, :], ps[:, 5, 0:2 * P], ACT.Copy).then_inc(m_rows, 1)

                def ssd_exp(it):
                    i = 8 * M + it
                    eng.wait_ge(m_pre, i + 1)
                    if i:
                        eng.wait_ge(m_mul, 5 * i)
                        eng.wait_ge(m_sev, SEV[8] * M + SEV[it])
                    eng.activation(ss["lmat"][:, :, :].rearrange("p a t -> p (a t)"), ps[:, 0, :], ACT.Exp)\
                       .then_inc(m_sexp, 1)
                    eng.activation(ss["emat"][:, :, :].rearrange("p a t -> p (a t)"), ps[:, 1, :], ACT.Exp)\
                       .then_inc(m_sexp, 1)
                    eng.activation(decs[:, :], ps[:, 2, 256:264], ACT.Exp).then_inc(m_sexp, 1)

                def fox_exp(f):
                    F, n = 16 * M + f, (f % 4 + 1) * P
                    eng.wait_ge(m_fmax, 2 * F + 2)
                    if F:
                        eng.wait_ge(m_ftr, F)
                    eng.activation(fprob[:, 0:n], ps[:, 4, 0:n], ACT.Exp, bias=nmax[:, f % 4:f % 4 + 1],
                                   accum_out=psumr[:, f % 4:f % 4 + 1]).then_inc(m_fp, 1)

                def fox_copy(f):
                    F, nb = 16 * M + f, f % 4 + 1
                    eng.wait_ge(m_ftr, F + 1)
                    if F:
                        eng.wait_ge(m_fo, F)
                    eng.activation(fprobT[:, 0:nb, :].rearrange("p a t -> p (a t)"), ps[:, 5, 0:nb * P], ACT.Copy)\
                       .then_inc(m_fpt, 1)

                for it in range(8):
                    ssd_exp(it)
                    for f in (2 * it, 2 * it + 1):
                        fox_exp(f)
                        fox_copy(f)
                for t in range(4):
                    eng.wait_ge(m_gate, 4 * M + t + 1)
                    eng.activation(proj[:, Z + t, :], proj[:, t, :], ACT.Square).then_inc(m_ysq, 1)
                for g in range(2):
                    eng.wait_ge(m_ms, 2 * M + g + 1)
                    eng.activation(ss[("am", "ab")[g]][:, :, :].rearrange("p a t -> p (a t)"), ps[:, g, :], ACT.Sqrt,
                                   scale=1.0 / 256, bias=eps_t[:, 1:2]).then_inc(m_sd, 1)
                src = {}
                for t in range(4):
                    src[t] = (proj[:, t, :], m_rn, 6 * M + 3 * (t // 2) + 2 + t % 2)
                for t in range(2):
                    src[4 + t] = (proj[:, FQ + t, :], m_fy, 16 * M + 8 * (t + 1))
                    src[6 + t] = (proj[:, BG + t, :], m_sc, NSC * (M + 1))
                for t in range(DC):
                    eng.wait_ge(src[t][1], src[t][2])
                    eng.activation(h_hi[:, t, :], src[t][0], ACT.Copy).then_inc(s_hhi, 1)
                w.h_chunks += DC
                w.mixer += 1

            def norm_gqa():
                eng.wait_ge(s_evac, w.events)
                for j, (x, t, _) in enumerate(GQA_JOBS):
                    b = j % 2
                    if j >= 2:
                        eng.wait_ge(r_out, 3 * (w.rope + j - 1))
                    eng.activation(gp[:, b, :], x[:, t, :], ACT.Square).then_inc(n_sq, 1)
                    eng.wait_ge(n_ms, w.nms + j + 1)
                    eng.activation(gpt[:, b, :], flat(2 * b), ACT.Sqrt, scale=1.0 / HD, bias=eps_t[:, 2:3])\
                       .then_inc(n_sd, 1)
                n = len(GQA_JOBS)
                w.nsq, w.nms, w.nout, w.rope = w.nsq + n, w.nms + n, w.nout + 2 * n, w.rope + n

            def norm_mla():
                eng.wait_ge(s_evac, w.events)
                eng.wait_ge(s_xa, DC * w.mod)
                for t in range(KVC):
                    eng.activation(msq[:, t, :], ckv[:, t, :], ACT.Square).then_inc(n_sq, 1)
                for t in range(QC):
                    eng.activation(msq[:, KVC + t, 0:SEQ], cq[:, t, :], ACT.Square).then_inc(n_sq, 1)
                eng.wait_ge(n_ms, w.nms + 1)
                eng.activation(msd[:, 0, :], flat(0), ACT.Sqrt, scale=1.0 / (KVC * P), bias=eps_t[:, 2:3])\
                   .then_inc(n_sd, 1)
                eng.wait_ge(n_ms, w.nms + 2)
                eng.activation(msd[:, 1, 0:SEQ], ps[:, 2, :], ACT.Sqrt, scale=1.0 / (QC * P), bias=eps_t[:, 2:3])\
                   .then_inc(n_sd, 1)
                for t in range(KVC):
                    eng.wait_ge(n_out, w.nout + 2 + t)
                    eng.activation(ckvn_hi[:, t, :], ckv[:, t, :], ACT.Copy).then_inc(s_hhi, 1)
                for t in range(QC):
                    eng.wait_ge(n_out, w.nout + KVC + 3 + t)
                    eng.activation(cqn_hi[:, t, :], cq[:, t, :], ACT.Copy).then_inc(s_hhi, 1)
                w.nms += 2
                w.nout += QC + KVC + 2
                w.rope += 1
                w.h_chunks += QC + KVC

            def attention(kind):
                a = ATT[kind]
                eng.wait_ge(s_evac, w.events)
                eng.wait_ge(r_out, 3 * w.rope)
                for x, hi, _ in a["split"]:
                    eng.activation(hi, x, ACT.Copy).then_inc(t_sh, 1)
                for run in map(lambda r: Run(*r), a["runs"]):
                    def rounded(b):
                        eng.wait_ge(t_p, b + 1)
                        eng.activation(a["p"][0][:, b % RING, 0:run.nq], a["prob"][:, b % RING, 0:run.nq], ACT.Copy)\
                           .then_inc(t_pt, 1)

                    last = w.blocks + HEADS * run.kb
                    for b in range(w.blocks, last + 1):
                        if b < last:
                            eng.wait_ge(t_st, b + 1)
                            if b >= RING:
                                eng.wait_ge(t_pv, b - RING + 1)
                            eng.activation(a["prob"][:, b % RING, 0:run.nq], ps[:, B_PT + b % 2, 0:run.nq], ACT.Exp,
                                           scale=a["scale"]).then_inc(t_p, 1)
                        if b > w.blocks:
                            rounded(b - 1)
                    w.blocks = last
                    w.heads += HEADS
                eng.wait_ge(t_y, w.heads)
                outs = [(h_hi, q_t[:, :, 0:SEQ]), (hc_hi, q_t[:, :, SEQ:])] if kind == "gqa" else [(y2_hi, mq[:, :, :])]
                for hi, y in outs:
                    for k in range(DC):
                        eng.activation(hi[:, k, :], y[:, k, :], ACT.Copy).then_inc(s_hhi, 1)
                w.h_chunks += DC * len(outs)

            for j, item in enumerate(sched):
                if j in early:
                    ahead(sched[early[j]][1])
                if item[0] == "lin":
                    if j not in early.values() and sched[j - 1][0] != "lin":
                        ahead(item[1])
                    linear(item[1], sched[j + 1][1] if sched[j + 1][0] == "lin" else None)
                    w.events = item[1].e0 + item[1].n * item[1].events
                elif item[0] == "ln":
                    layer_norm(*item[1:])
                elif item[0] == "mod":
                    modulate(*item[1:])
                elif item[0] == "mixer":
                    mixer(item[1])
                elif item[0] == "gqa":
                    norm_gqa()
                    attention("gqa")
                elif item[0] == "mla_norm":
                    norm_mla()
                elif item[0] == "mla":
                    w.rope += 4
                    attention("mla")

        @block.tensor
        def _(eng):
            w = Walk()
            eng.wait_ge(s_const, N_CONST)
            eng.wait_ge(s_par, 32)

            def ada_sums(m, i, a, b):
                eng.wait_ge(s_ada, a + 1)
                nv = vectors(m)
                for q in range(2):
                    for v in range(nv):
                        mm = eng.matmul(ps[:, B_ADA, at(48 * m + v + (i * 2 + q) * nv)], ada_acc[:, b, v, q * P:(q + 1) * P],
                                        ones[:, 0:1], start=True, stop=True, skip_group_check=True)
                mm.then_inc(s_asum, 1)

            def passes(out, hi_w, lo_w, hi_x, lo_x, first, last):
                eng.matmul(out, lo_w, hi_x, start=first, stop=False, skip_group_check=True)
                eng.matmul(out, hi_w, lo_x, start=False, stop=False, skip_group_check=True)
                return eng.matmul(out, hi_w, hi_x, start=False, stop=last, skip_group_check=True)

            def linear(ln, before, followed):
                if ln.src in ("cqn", "ckvn"):
                    eng.wait_ge(s_hlo, w.h_chunks)

                def chunk_ready(n_st, k):
                    if ln.src == "hid":
                        eng.wait_ge(s_hid, w.hid - ln.kc + k + 1)
                    elif ln.src not in ("cqn", "ckvn"):
                        eng.wait_ge(s_hlo, w.h_chunks - DC * (len(ln.streams) - n_st) + k + 1)

                def main(u, i, first=False):
                    eng.wait_ge(s_wlo, i + (ln.g0 + 1))
                    slot = (ln.g0 + u) % 2
                    if first:
                        eng.wait_ge(s_evac, ln.e_first)
                    elif ln.evac == "gateup":
                        eng.wait_ge(s_evac, i + (ln.e0 - 1))
                    if ln.row:
                        toks = [(st, t) for st in ln.streams for t in range(NT[st] // P)]
                        for t, (st, tt) in enumerate(toks):
                            hi, lo = operand(ln, st)
                            if first and t:
                                eng.wait_ge(s_evac, ln.e0)
                            if t >= 4:
                                eng.wait_ge(s_evac, i * ln.row + (ln.e0 + t - 3))
                            elif ln.n > 1:
                                eng.wait_ge(s_evac, i * ln.row + (ln.e0 + 1 - ln.row + max(range(t, ln.row, 4))))
                            for k in range(ln.kc):
                                ws = slice(k * ln.out, (k + 1) * ln.out)
                                xs = slice(tt * P, (tt + 1) * P)
                                if first and tt == 0:
                                    chunk_ready(ln.streams.index(st), k)
                                mm = passes(ps[:, t % 4, 0:ln.out], hi[:, k, xs], lo[:, k, xs], w_hi[:, slot, ws],
                                            w_lo[:, slot, ws], k == 0, k == ln.kc - 1)
                            mm.then_inc(s_tile, 1)
                    else:
                        for q in range(ln.tpu):
                            tile = u * ln.tpu + q
                            if first and q:
                                eng.wait_ge(s_evac, ln.e0)
                            if ln.evac != "gateup" and not (first and q < ln.nbuf):
                                eng.wait_ge(s_evac, i * ln.tpu + (ln.e0 + q - ln.nbuf + 1))
                            for st in ln.streams:
                                hi, lo = operand(ln, st)
                                for k in range(ln.kc):
                                    ws = slice((q * ln.kc + k) * P, (q * ln.kc + k + 1) * P)
                                    if first and q == 0:
                                        chunk_ready(ln.streams.index(st), k)
                                    mm = passes(ps[:, tile_bank(ln, tile, st), 0:NT[st]], w_hi[:, slot, ws],
                                                w_lo[:, slot, ws], hi[:, k, 0:NT[st]], lo[:, k, 0:NT[st]], k == 0,
                                                k == ln.kc - 1)
                            mm.then_inc(s_tile, 1)

                def ada(ln, pos, i):
                    if ln.ada:
                        ada_sums(ln.ada[0], i + ln.ada[1], i + ln.a0, (ln.a0 + pos) % 2)

                main(0, 0, first=True)
                if before:
                    ada(before, before.n - 1, before.n - 1)
                for it, u, i in steps(eng, 1, ln.n):
                    main(u + 1, i)
                    ada(ln, u, i - 1)
                if not followed:
                    ada(ln, ln.n - 1, ln.n - 1)
                if ln.evac in ("gateup", "relu2"):
                    w.hid += ln.n * ln.events

            def layer_norm(name, st, eps):
                x, n, nt = X[st], w.ln, NT[st]
                eng.wait_ge(s_xsum, w.xsum)
                eng.matmul(ps[:, B_MEAN, 0:nt], ones[:, :], x_sum[st][:, :], start=True, stop=False,
                           skip_group_check=True)
                eng.wait_ge(s_evac, w.events)
                eng.matmul(ps[:, B_MEAN, 0:nt], ones[:, :], x[:, DC - 1, :], start=False, stop=True,
                           skip_group_check=True).then_inc(s_sum, 1)
                for p in range(DC // 2):
                    eng.wait_ge(s_pair, DC // 2 * n + p + 1)
                    mm = eng.matmul(ps[:, B_VAR, 0:nt], ones[:, :], sq[:, 2 * p, 0:nt], start=(p == 0),
                                    stop=(p == DC // 2 - 1), skip_group_check=True)
                mm.then_inc(s_sum, 1)
                w.ln += 1

            def mixer(l):
                M = w.mixer
                eng.wait_ge(s_evac, w.events)
                for c in range(4):
                    if c == 0:
                        eng.wait_ge(m_silu, 8 * (M + 1))
                    else:
                        eng.wait_ge(m_rows, 8 * M + 2 * c)
                    cs = slice(c * P, (c + 1) * P)
                    for t in range(4):
                        eng.transpose(ps[:, 4, t * P:(t + 1) * P], proj[:, XBC + t, cs], ident[:, :])
                    for t in range(2):
                        tr = eng.transpose(ps[:, 5, t * P:(t + 1) * P], proj[:, XBC + 4 + t, cs], ident[:, :])
                    tr.then_inc(m_tr, 1)

                def ssd_pre(it):
                    i, (c, g) = 8 * M + it, divmod(it, 2)
                    cs = slice(c * P, (c + 1) * P)
                    eng.wait_ge(m_am, i + 1)
                    eng.wait_ge(m_ab, i + 1)
                    if i:
                        eng.wait_ge(m_sexp, 3 * i)
                        eng.wait_ge(m_mul, 5 * i)
                    for h in range(4):
                        eng.matmul(ps[:, 0, h * P:(h + 1) * P], ss["am"][:, h, :], tri[:, :], start=True, stop=True)
                    for h in range(4):
                        eng.matmul(ps[:, 1, h * P:(h + 1) * P], ss["ab"][:, h, :], tri[:, :], start=True, stop=True)
                    eng.matmul(ps[:, 2, 0:P], proj[:, XBC + 4 + g, cs], proj[:, XBC + 6 + g, cs], start=True, stop=True)
                    ah = a_row[:, c, 4 * g:4 * g + 4]
                    eng.matmul(ps[:, 2, 256:260], past[:, 3, :], ah, start=True, stop=True)
                    eng.matmul(ps[:, 2, 260:264], ones[:, :], ah, start=True, stop=True).then_inc(m_pre, 1)

                def ssd_y(it):
                    i, (c, g) = 8 * M + it, divmod(it, 2)
                    eng.wait_ge(m_mul, 5 * (i + 1))
                    eng.wait_ge(m_sev, SEV[8] * M + SEV[it])
                    for q in range(2):
                        for hh in range(2):
                            h = 2 * q + hh
                            o = ps[hh * HD:(hh + 1) * HD, 3, q * P:(q + 1) * P]
                            mm = eng.matmul(o, xdt[:, h, :], ss["mmat"][:, h, :], start=True, stop=(c == 0),
                                            skip_group_check=True)
                            if c:
                                mm = eng.matmul(o, state[:, g, h * HD:(h + 1) * HD], ss["cdec"][:, h, :], start=False,
                                                stop=True, skip_group_check=True)
                    if c < 3:
                        mm = eng.matmul(ps[:, 3, 2 * P:4 * P], brow[:, c, g * P:(g + 1) * P],
                                        xdec[:, :, :].rearrange("p a t -> p (a t)"), start=True, stop=True,
                                        skip_group_check=True)
                    mm.then_inc(m_y, 1)

                def fox_scores(f):
                    F, (h, i) = 16 * M + f, divmod(f, 4)
                    n, hp = (i + 1) * P, slice((h % 2) * HD, (h % 2 + 1) * HD)
                    eng.wait_ge(m_qs, M + 1)
                    eng.wait_ge(m_fg, 16 * M + 4 * (h + 1))
                    if F:
                        eng.wait_ge(m_fp, F)
                    if f == 0:
                        eng.wait_ge(m_rows, 8 * (M + 1))
                    eng.matmul(ps[:, 4, 0:n], proj[hp, FQ + h // 2, i * P:n], proj[hp, FK + h // 2, 0:n], start=True,
                               stop=False, skip_group_check=True)
                    for j in range(i + 1):
                        eng.matmul(ps[:, 4, 0:(j + 1) * P], tri[:, :] if j == i else ones[:, :],
                                   fcum[:, j, 0:(j + 1) * P], start=False, stop=False, skip_group_check=True)
                    eng.matmul(ps[:, 4, i * P:n], ident[:, :], negmask[:, :], start=False, stop=True,
                               skip_group_check=True).then_inc(m_fs, 1)

                def fox_out(f):
                    F, (h, i) = 16 * M + f, divmod(f, 4)
                    eng.wait_ge(m_fn, 2 * F + 2)
                    if F:
                        eng.wait_ge(m_fpt, F)
                    for j in range(i + 1):
                        tr = eng.transpose(ps[:, 5, j * P:(j + 1) * P], fprob[:, j * P:(j + 1) * P], ident[:, :])
                    tr.then_inc(m_ftr, 1)
                    eng.wait_ge(m_fpt, F + 1)
                    if F:
                        eng.wait_ge(m_fy, F)
                    for j in range(i + 1):
                        mm = eng.matmul(ps[(h % 2) * HD:(h % 2 + 1) * HD, 6, 0:P], vrow[:, j, h * HD:(h + 1) * HD],
                                        fprobT[:, j, :], start=(j == 0), stop=(j == i), skip_group_check=True)
                    mm.then_inc(m_fo, 1)

                for it in range(8):
                    ssd_pre(it)
                    fox_scores(2 * it)
                    ssd_y(it)
                    fox_out(2 * it)
                    fox_scores(2 * it + 1)
                    fox_out(2 * it + 1)
                for g in range(2):
                    eng.wait_ge(m_ysq, 4 * M + 2 * g + 2)
                    for q in range(2):
                        mm = eng.matmul(ps[:, g, :], ones[:, :], proj[:, Z + 2 * g + q, :], start=(q == 0), stop=(q == 1))
                    mm.then_inc(m_ms, 1)
                w.mixer += 1
                w.h_chunks += DC

            def swap(x, b, which):
                eng.matmul(ps[:, 4 + b, :], swaps[:, which, :], x, start=True, stop=True).then_inc(r_sw, 1)

            def norm_gqa():
                def mean_square(j):
                    b = j % 2
                    eng.wait_ge(n_sq, w.nsq + j + 1)
                    if j >= 2:
                        eng.wait_ge(n_sd, w.nms + j - 1)
                    eng.matmul(ps[:, 2 * b, :], blocks[:, :], gp[:, b, 0:SEQ], start=True, stop=True)
                    eng.matmul(ps[:, 2 * b + 1, 0:CTX], blocks[:, :], gp[:, b, SEQ:], start=True, stop=True)\
                       .then_inc(n_ms, 1)

                n = len(GQA_JOBS)
                eng.wait_ge(s_evac, w.events)
                for j, (x, t, _) in enumerate(GQA_JOBS):
                    mean_square(j)
                    eng.wait_ge(n_out, w.nout + 2 * j + 2)
                    if j >= 2:
                        eng.wait_ge(r_out, 3 * (w.rope + j - 1))
                    swap(x[:, t, 0:SEQ], j % 2, 0)
                w.nsq, w.nms, w.nout, w.rope = w.nsq + n, w.nms + n, w.nout + 2 * n, w.rope + n

            def norm_mla():
                eng.wait_ge(s_evac, w.events)
                eng.wait_ge(n_sq, w.nsq + KVC)
                for c0, n, bank in ((0, SEQ, 0), (SEQ, CTX, 1)):
                    for t in range(KVC):
                        mm = eng.matmul(ps[:, bank, 0:n], ones[:, :], msq[:, t, c0:c0 + n], start=(t == 0),
                                        stop=(t == KVC - 1))
                mm.then_inc(n_ms, 1)
                eng.wait_ge(n_sq, w.nsq + KVC + QC)
                for t in range(QC):
                    mm = eng.matmul(ps[:, 2, :], ones[:, :], msq[:, KVC + t, 0:SEQ], start=(t == 0), stop=(t == QC - 1))
                mm.then_inc(n_ms, 1)
                swap(kpe[:, 0:SEQ], 0, 1)
                w.nsq += KVC + QC
                w.nms += 2
                w.rope += 1
                w.h_chunks += QC + KVC

            def rope_mla():
                eng.wait_ge(s_evac, w.events)
                for j in range(4):
                    if j >= 2:
                        eng.wait_ge(r_out, 3 * (w.rope + j - 1))
                    swap(qpe[:, j, :], j % 2, 1)
                w.rope += 4

            def attention(kind):
                a = ATT[kind]
                (qh, ql), (kh, kl), (vh, vl), (ph, pl) = a["q"], a["k"], a["v"], a["p"]

                def places(s):
                    tile = s // 2
                    return (slice((s % 2) * HD, (s % 2 + 1) * HD), tile, tile // 4 if kind == "gqa" else tile,
                            slice((s % 4) * ROPE, (s % 4 + 1) * ROPE), s // 4)

                for run in map(lambda r: Run(*r), a["runs"]):
                    U = len(run.units)
                    U0, S0, B0 = w.units, w.heads, w.blocks

                    def for_max(s, u):
                        hp, tile, kt, rp, rt = places(s)
                        t, _, k, n = run.units[u]
                        g = U0 + s * U + u
                        if u == 0:
                            eng.wait_ge(t_sl, w.splits + a["ready"](tile))
                        if g >= 2:
                            eng.wait_ge(t_mx, g - 1)
                        qs, ks, o = slice(run.c0 + t * P, run.c0 + (t + 1) * P), slice(k, k + n), ps[:, B_MAX + g % 2, 0:n]
                        mm = passes(o, qh[hp, tile, qs], ql[hp, tile, qs], kh[hp, kt, ks], kl[hp, kt, ks], True,
                                    kind == "gqa")
                        if kind == "mla":
                            mm = passes(o, qpe_hi[rp, rt, qs], qpe_lo[rp, rt, qs], kpe_hi[rp, ks], kpe_lo[rp, ks], False,
                                        True)
                        mm.then_inc(t_s, 1)

                    def scores(s, j):
                        hp, tile, kt, rp, rt = places(s)
                        b = B0 + s * run.kb + j
                        if j == 0:
                            eng.wait_ge(t_dg, S0 + s + 1)
                        if b >= 2:
                            eng.wait_ge(t_p, b - 1)
                        ks, o = slice(run.k0 + j * P, run.k0 + (j + 1) * P), ps[:, B_PT + b % 2, 0:run.nq]
                        passes(o, kh[hp, kt, ks], kl[hp, kt, ks], qh[hp, tile, run.q], ql[hp, tile, run.q], True, False)
                        if kind == "mla":
                            passes(o, kpe_hi[rp, ks], kpe_lo[rp, ks], qpe_hi[rp, rt, run.q], qpe_lo[rp, rt, run.q], False,
                                   False)
                        eng.matmul(o, ones_r[:, :], a["diag"][:, (S0 + s) % 2, 0:run.nq], start=False, stop=True,
                                   skip_group_check=True).then_inc(t_st, 1)

                    def outputs(s, j):
                        b = B0 + s * run.kb + j
                        v0 = (s // 8 if kind == "gqa" else s // 2) * P
                        if s == 0 and j == 0:
                            eng.wait_ge(t_sl, w.splits + len(a["split"]))
                        if j == 0 and S0 + s >= 2:
                            eng.wait_ge(t_y, S0 + s - 1)
                        eng.wait_ge(t_pl, b + 1)
                        first, last = j == 0, j == run.kb - 1
                        vj = (slice(None), run.k0 // P + j, slice(v0, v0 + P))
                        hi, lo = ph[:, b % RING, 0:run.nq], pl[:, b % RING, 0:run.nq]
                        passes(ps[:, B_OUT + s % 2, 0:run.nq], vh[vj], vl[vj], hi, lo, first, last)
                        o = ps[:, B_SUM + s % 2, 0:run.nq]
                        eng.matmul(o, ones_r[:, :], lo, start=first, stop=False, skip_group_check=True)
                        eng.matmul(o, ones_r[:, :], hi, start=False, stop=last, skip_group_check=True)\
                           .then_inc(t_pv, 1)

                    for u in range(U):
                        for_max(0, u)
                    steps_all = [(s, j) for s in range(HEADS) for j in range(run.kb)]
                    for i in range(len(steps_all) + 2):
                        if i < len(steps_all):
                            s, j = steps_all[i]
                            scores(s, j)
                            if s + 1 < HEADS:
                                for u in run.share[j]:
                                    for_max(s + 1, u)
                        if i >= 2:
                            outputs(*steps_all[i - 2])
                    w.units, w.heads, w.blocks = U0 + HEADS * U, S0 + HEADS, B0 + len(steps_all)
                w.splits += len(a["split"])
                w.h_chunks += DC * (2 if kind == "gqa" else 1)

            w.xsum = DC - 2
            for j, item in enumerate(sched):
                if item[0] == "ada0":
                    for i in range(ADA_UNITS):
                        ada_sums(0, i, i, i % 2)
                elif item[0] == "lin":
                    ln = item[1]
                    linear(ln, sched[j - 1][1] if sched[j - 1][0] == "lin" else None, sched[j + 1][0] == "lin")
                    w.events = ln.e0 + ln.n * ln.events
                    if sched[j + 1][0] == "ln":
                        w.xsum += (DC - 2) * len(ln.streams)
                elif item[0] == "ln":
                    layer_norm(*item[1:])
                elif item[0] == "mod":
                    w.mod += 1
                    w.h_chunks += DC
                elif item[0] == "mixer":
                    mixer(item[1])
                elif item[0] == "gqa":
                    norm_gqa()
                    attention("gqa")
                elif item[0] == "mla_norm":
                    norm_mla()
                elif item[0] == "mla":
                    rope_mla()
                    eng.wait_ge(r_out, 3 * w.rope)
                    attention("mla")

        @block.vector
        def _(eng):
            w = Walk()
            eng.wait_ge(s_par, 32)
            eng.wait_ge(s_const, N_CONST)
            eng.wait_ge(s_cact, 3)
            eng.sem_inc(s_evac, 4)

            def split_weights(ln, i, it, pos):
                G, slot = ln.G0 + pos * ln.spu, (ln.g0 + pos) % 2
                eng.wait_ge(s_whi, i + (ln.g0 + 1))
                eng.tensor_tensor(w_lo[:, slot, 0:ln.width], raw[:, G % RAW, 0:ln.width],
                                  w_hi[:, slot, 0:ln.width].bitcast(F32), ALU.subtract).then_inc(s_wlo, 1)

            def ada_unit(m, G, it, spu, i, a, b, parts):
                nv = vectors(m)
                raw_ready(eng, G, it, spu)
                weights = raw[:, G % RAW, :].rearrange("p (q k f) -> p q k f", q=2, k=DC)
                if a[1] >= 2:
                    eng.wait_ge(s_asum, a[0] - 1)
                for k in range(DC):
                    for v in range(nv):
                        acc = ada_acc[:, b, v, :].rearrange("p (q f) -> p q f", q=2)
                        c = (0 if nv == 1 else DC) + k * nv + v
                        if k == 0:
                            ins = eng.tensor_scalar(acc, weights[:, :, k, :], c_act[:, c:c + 1], None, ALU.mult)
                        else:
                            eng.wait_ge(s_part, parts + ((k - 1) * nv + v + 1))
                            ins = eng.scalar_tensor_tensor(acc, weights[:, :, k, :], c_act[:, c:c + 1], acc, ALU.mult,
                                                           ALU.add)
                        last = k == DC - 1 and v == nv - 1
                        ins.then_inc(s_ada if last else s_part, 1)

            def ada(ln, i, it, pos):
                if ln.ada:
                    ada_unit(ln.ada[0], ln.G0 + pos * 2 + 1, it, 2, i + ln.ada[1], (i + ln.a0, ln.a0 + pos),
                             (ln.a0 + pos) % 2, i * ada_parts(ln.ada[0]) + ln.p0)

            def ahead(ln, lo=0, hi=2):
                for i in range(lo, min(hi, ln.n)):
                    split_weights(ln, i, 0, i)

            def evacuate(ln, i, it, pos):
                if ln.evac == "gateup":
                    h = w.hid
                    eng.wait_ge(s_gate, i + (h + 1))
                    if pos >= 2 or h:
                        eng.wait_ge(s_hid, i + (h - 1))
                    eng.tensor_tensor(val_t[:, pos % 2, 0:SEQ], ps[:, tile_bank(ln, 2 * pos + 1, "lat"), :],
                                      gate_t[:, pos % 2, 0:SEQ], ALU.mult).then_inc(s_evac, 1)
                    eng.wait_ge(s_hidhi, i + (h + 1))
                    eng.tensor_tensor(hid_lo[:, at(i), :], val_t[:, pos % 2, 0:SEQ].unsqueeze(1),
                                      hid_hi[:, at(i), :].bitcast(F32), ALU.subtract).then_inc(s_hid, 1)
                elif ln.evac == "relu2":
                    h = w.hid
                    for q in range(2):
                        eng.wait_ge(s_gate, i * 2 + (h + q + 1))
                        for st in ln.streams:
                            c = slice(COL0[st], COL0[st] + NT[st])
                            a = eng.tensor_tensor(relu_t[:, q, c], relu_t[:, q, c], relu_t[:, q, c], ALU.mult)
                        a.then_inc(s_evac, 1)
                    for q in range(2):
                        eng.wait_ge(s_hidhi, i * 2 + (h + q + 1))
                        for st in ln.streams:
                            c = slice(COL0[st], COL0[st] + NT[st])
                            a = eng.tensor_tensor(HID[st][1][:, at(i * 2 + q), :], relu_t[:, q, c].unsqueeze(1),
                                                  HID[st][0][:, at(i * 2 + q), :].bitcast(F32), ALU.subtract)
                        a.then_inc(s_hid, 1)
                elif ln.row:
                    for t in range(ln.row):
                        eng.wait_ge(s_tile, i * ln.row + (ln.t0 + t + 1))
                        eng.tensor_copy(row_dest(ln, i, t), ps[:, t % 4, 0:ln.out]).then_inc(s_evac, 1)
                else:
                    for q in range(ln.tpu):
                        m = i * ln.tpu + q
                        eng.wait_ge(s_tile, m + (ln.t0 + 1))
                        for st in ln.streams:
                            tile = ps[:, tile_bank(ln, pos * ln.tpu + q, st), 0:NT[st]].unsqueeze(1)
                            if ln.evac == "copy":
                                a = eng.tensor_copy(dest(ln, st, m), tile)
                            else:
                                xm = X[st][:, at(m), :]
                                a = eng.scalar_tensor_tensor(xm, tile, MODT[st][:, at(m + 2 * DC)], xm, ALU.mult,
                                                             ALU.add)
                        a.then_inc(s_evac, 1)

            def finish(ln, lag, following):
                for j, i in enumerate(range(ln.n - lag, ln.n)):
                    first = ln.events > ln.nbuf or (ln.events > 1 and i == ln.n - 1)
                    if first:
                        evacuate(ln, i, 0, i)
                    if following:
                        ahead(following, j, j + 1)
                    if not first:
                        evacuate(ln, i, 0, i)
                if following:
                    ahead(following, lag, 2)

            def linear(ln, following):
                lag = min(2, ln.n)
                eng.wait_ge(s_evac, ln.e0)
                if ln.evac == "resid":
                    eng.wait_ge(s_xa, DC * w.mod)
                late = len(ln.streams) > 1
                if lag == 2:
                    ada(ln, 0, 0, 0)
                for it, u, i in steps(eng, lag, ln.n):
                    if not late:
                        ada(ln, i - 1, it, u + 1)
                    split_weights(ln, i, it, lag + u)
                    evacuate(ln, i - 2, it, u)
                    if late:
                        ada(ln, i - 1, it, u + 1)
                if not late:
                    ada(ln, ln.n - 1, 0, ln.n - 1)
                finish(ln, lag, following)
                if late:
                    ada(ln, ln.n - 1, 0, ln.n - 1)
                w.events = ln.e0 + ln.n * ln.events
                if ln.evac in ("gateup", "relu2"):
                    w.hid += ln.n * ln.events

            def layer_norm(name, st, eps):
                x, n, nt = X[st], w.ln, NT[st]

                def pair(p):
                    eng.wait_ge(s_sq, DC * n + 2 * p + 2)
                    eng.tensor_tensor(sq[:, 2 * p, 0:nt], sq[:, 2 * p, 0:nt], sq[:, 2 * p + 1, 0:nt], ALU.add)\
                       .then_inc(s_pair, 1)

                eng.wait_ge(s_sum, 2 * n + 1)
                eng.wait_ge(s_evac, w.events)
                for k in range(DC):
                    eng.scalar_tensor_tensor(x[:, k, :], ps[:, B_MEAN, 0:nt], -1.0 / D, x[:, k, :], ALU.mult, ALU.add)\
                       .then_inc(s_cent, 1)
                    if k >= 3 and k % 2:
                        pair(k // 2 - 1)
                pair(DC // 2 - 1)
                eng.wait_ge(s_dev, n + 1)
                eng.reciprocal(rstd[:, 0:nt], rstd[:, 0:nt]).then_inc(s_rstd, 1)
                eng.wait_ge(s_rstd, n + 1)
                eng.wait_ge(s_cent, DC * n + DC)
                for k in range(DC):
                    eng.tensor_tensor(x[:, k, :], x[:, k, :], rstd[:, 0:nt], ALU.mult).then_inc(s_scal, 1)
                w.ln += 1

            def modulate(m, st):
                nv, v = (1, 0) if m < 6 else (2, int(st == "ctx"))
                x, mod, lo = X[st], MODT[st], H[st][1]
                eng.wait_ge(s_asum, ada_done[m])
                if m in KEPT.values():
                    eng.wait_ge(s_keep, sorted(KEPT.values()).index(m) + 1)
                sums = kept[:, :] if m in KEPT.values() else ps[:, B_ADA, 48 * m:48 * m + MOD * nv]
                cols_m = sums.rearrange("p (a v) -> p a v", v=nv)[:, :, v:v + 1]
                eng.tensor_tensor(mod[:, :].unsqueeze(2), cols_m, pc(f"ada_b_{m}", 0, MOD).unsqueeze(2), ALU.add)\
                   .then_inc(s_mod, 1)
                eng.wait_ge(s_mod, 3 * w.mod + 1)
                eng.tensor_scalar(mod[:, DC:2 * DC], mod[:, DC:2 * DC], 1.0, None, ALU.add).then_inc(s_mod, 1)
                half = 0.5 if m in (0, 2, 3, 5) else 1.0
                eng.tensor_scalar(mod[:, 2 * DC:], mod[:, 2 * DC:], half, None, ALU.mult).then_inc(s_mod, 1)
                eng.wait_ge(s_mod, 3 * w.mod + 3)
                c0 = DC * w.mod
                for k in range(DC + 1):
                    if k < DC:
                        if st == "ctx" and m == 6:
                            eng.wait_ge(s_x, 32)
                        else:
                            eng.wait_ge(s_aff, DC * (w.ln - 1) + k + 1)
                        if c0 + k >= 4:
                            eng.wait_ge(s_h32, c0 + k)
                        if k >= 4:
                            eng.wait_ge(s_hlo, w.h_chunks + k - 3)
                        eng.tensor_scalar(h32[:, k % 4, 0:NT[st]], x[:, k, :], mod[:, DC + k:DC + k + 1],
                                          mod[:, k:k + 1], ALU.mult, ALU.add).then_inc(s_h32, 1)
                    if k:
                        eng.wait_ge(s_hhi, w.h_chunks + k)
                        eng.tensor_tensor(lo[:, k - 1, :], h32[:, (k - 1) % 4, 0:NT[st]],
                                          H[st][0][:, k - 1, :].bitcast(F32), ALU.subtract).then_inc(s_hlo, 1)
                w.mod += 1
                w.h_chunks += DC

            def mixer(l):
                M = w.mixer
                n0 = [NSP * M]

                def step(ins):
                    ins.then_inc(m_sp, 1)
                    n0[0] += 1
                    eng.wait_ge(m_sp, n0[0])

                v, n, e, d, z, z2, p, dt = (sp[k][:, :, :] for k in ("v", "n", "e", "d", "z", "z2", "p", "dt"))
                eng.wait_ge(s_evac, w.events)
                step(eng.tensor_tensor(v, dtrow[:, :, :], pc(f"dt_bias_{l}", 0, 12).unsqueeze(1)
                                       .broadcast_to([P, 4, 12]), ALU.add))
                step(eng.tensor_scalar(sp["v"][:, :, SSD_H:], sp["v"][:, :, SSD_H:], -1.0, None, ALU.mult))
                step(eng.tensor_scalar(n, v, -1.0, None, ALU.mult))
                step(eng.tensor_tensor(n, n, v, ALU.min))
                eng.wait_ge(m_spe, M + 1)
                step(eng.tensor_scalar(d, e, 2.0, None, ALU.add))
                step(eng.reciprocal(d, d))
                step(eng.tensor_tensor(z, e, d, ALU.mult))
                step(eng.tensor_tensor(z2, z, z, ALU.mult))
                step(eng.tensor_scalar(p, z2, LOG1P[7], None, ALU.mult))
                for k in range(6, 0, -1):
                    step(eng.scalar_tensor_tensor(p, p, LOG1P[k], z2, ALU.add, ALU.mult))
                step(eng.scalar_tensor_tensor(p, p, LOG1P[0], z, ALU.add, ALU.mult))
                step(eng.tensor_scalar(n, v, 0.0, None, ALU.max))
                step(eng.scalar_tensor_tensor(dt, p, 2.0, n, ALU.mult, ALU.add))
                eng.wait_ge(m_ahd, M + 1)
                step(eng.scalar_tensor_tensor(a_row[:, :, :], sp["dt"][:, :, 0:SSD_H], -1.0,
                                              a_head[:, :].unsqueeze(1).broadcast_to([P, 4, SSD_H]), ALU.mult, ALU.mult))
                step(eng.tensor_scalar(logf[:, :, :], sp["dt"][:, :, SSD_H:], -1.0, None, ALU.mult))
                assert n0[0] == NSP * (M + 1)
                eng.tensor_scalar(proj[:, FQ:FQ + 2, :], proj[:, FQ:FQ + 2, :], HD ** -0.5, None, ALU.mult)\
                   .then_inc(m_qs, 1)

                for pr, pair in enumerate(PAIRS):
                    b = 32 * M + 8 * pr
                    if pr >= 2:
                        eng.wait_ge(m_silu, 8 * M + 2 * (pr - 1))
                    for k in range(4):
                        if k:
                            eng.wait_ge(m_conv, b + 2 * k)
                        for q, t in enumerate(pair):
                            acc, tap = cacc[:, 2 * (pr % 2) + q, :], pc(f"conv_w_{l}", 4 * t + 3 - k)
                            if k == 0:
                                a = eng.tensor_scalar(acc, proj[:, XBC + t, :], tap, None, ALU.mult)
                            else:
                                a = eng.scalar_tensor_tensor(acc[:, k:], proj[:, XBC + t, 0:SEQ - k], tap, acc[:, k:],
                                                             ALU.mult, ALU.add)
                            a.then_inc(m_conv, 1)

                b = NSC * M
                for t in range(2):
                    eng.tensor_tensor(proj[:, CG + t, :], proj[:, CG + t, :], proj[:, XIN + t, :], ALU.mult)\
                       .then_inc(m_sc, 1)
                for k in range(3):
                    eng.wait_ge(m_sc, b + 2 * (k + 1))
                    for t in range(2):
                        acc, tap = proj[:, XIN + t, :], pc(f"sconv_w_{l}", 3 * t + 2 - k)
                        if k == 0:
                            a = eng.tensor_scalar(acc, proj[:, CG + t, :], tap, None, ALU.mult)
                        else:
                            a = eng.scalar_tensor_tensor(acc[:, k:], proj[:, CG + t, 0:SEQ - k], tap, acc[:, k:],
                                                         ALU.mult, ALU.add)
                        a.then_inc(m_sc, 1)
                eng.wait_ge(m_sc, b + 8)
                for t in range(2):
                    eng.tensor_tensor(proj[:, BG + t, :], proj[:, BG + t, :], proj[:, XIN + t, :], ALU.mult)\
                       .then_inc(m_sc, 1)

                def ssd_mask(it):
                    i, (c, g) = 8 * M + it, divmod(it, 2)
                    if i:
                        eng.wait_ge(m_pre, i)
                    eng.tensor_tensor(ss["am"][:, :, :], past[:, 3, :].unsqueeze(1).broadcast_to([P, 4, P]),
                                      a_row[:, c, 4 * g:4 * g + 4].unsqueeze(2).broadcast_to([P, 4, P]), ALU.mult)\
                       .then_inc(m_am, 1)

                def ssd_operands(it):
                    i, (c, g) = 8 * M + it, divmod(it, 2)
                    cs, b = slice(c * P, (c + 1) * P), 5 * (8 * M + it)
                    eng.wait_ge(m_pre, i + 1)
                    if i:
                        eng.wait_ge(m_y, i)
                        eng.wait_ge(m_mul, b)
                    if it == 0:
                        eng.wait_ge(m_rows, 8 * (M + 1))
                    eng.wait_ge(m_sexp, 3 * (i + 1))
                    eng.tensor_tensor(cbm[:, :], ps[:, 2, 0:P], tri[:, :], ALU.mult).then_inc(m_mul, 1)
                    eng.tensor_tensor(xdt[:, :, :], xrow[:, c, g * 4 * HD:(g + 1) * 4 * HD]
                                      .rearrange("p (h d) -> p h d", h=4),
                                      sp["dt"][:, c, 4 * g:4 * g + 4].unsqueeze(2).broadcast_to([P, 4, HD]), ALU.mult)\
                       .then_inc(m_mul, 1)
                    eng.wait_ge(m_mul, b + 2)
                    eng.tensor_tensor(ss["mmat"][:, :, :], ss["lmat"][:, :, :],
                                      cbm[:, :].unsqueeze(1).broadcast_to([P, 4, P]), ALU.mult).then_inc(m_mul, 1)
                    eng.tensor_tensor(ss["cdec"][:, :, :], ss["emat"][:, :, :],
                                      proj[:, XBC + 6 + g, cs].unsqueeze(1).broadcast_to([P, 4, P]), ALU.mult)\
                       .then_inc(m_mul, 1)
                    eng.tensor_tensor(xdec[:, :, :], xdt[:, :, :], decs[:, 0:4].unsqueeze(2).broadcast_to([P, 4, HD]),
                                      ALU.mult).then_inc(m_mul, 1)

                def ssd_evac(it):
                    i, (c, g) = 8 * M + it, divmod(it, 2)
                    eng.wait_ge(m_y, i + 1)
                    for q in range(2):
                        y = proj[:, XBC + 2 * g + q, c * P:(c + 1) * P]
                        eng.scalar_tensor_tensor(y, y, pc(f"ssd_d_{l}", 2 * g + q), ps[:, 3, q * P:(q + 1) * P],
                                                 ALU.mult, ALU.add).then_inc(m_sev, 1)
                    new = ps[:, 3, 2 * P:4 * P]
                    b = SEV[8] * M + SEV[it] + 2
                    if c == 0:
                        eng.tensor_copy(state[:, g, :], new).then_inc(m_sev, 1)
                    elif c < 3:
                        sv = state[:, g, :].rearrange("p (h d) -> p h d", h=4)
                        eng.tensor_tensor(sv, sv, decs[:, 4:8].unsqueeze(2).broadcast_to([P, 4, HD]), ALU.mult)\
                           .then_inc(m_sev, 1)
                        eng.wait_ge(m_sev, b + 1)
                        eng.tensor_tensor(state[:, g, :], state[:, g, :], new, ALU.add).then_inc(m_sev, 1)

                def fox_rows(h):
                    if h or M:
                        eng.wait_ge(m_fs, 16 * M + 4 * h)
                    for j in range(4):
                        eng.tensor_scalar(fcum[:, j, 0:(j + 1) * P],
                                          past[:, 3 - j:4, :].rearrange("p a t -> p (a t)"), logf[:, j, h:h + 1], None,
                                          ALU.mult).then_inc(m_fg, 1)

                def fox_max(f):
                    F, n = 16 * M + f, (f % 4 + 1) * P
                    eng.wait_ge(m_fs, F + 1)
                    nm = nmax[:, f % 4:f % 4 + 1]
                    eng.reduce_max(nm, ps[:, 4, 0:n], AX_X).then_inc(m_fmax, 1)
                    eng.wait_ge(m_fmax, 2 * F + 1)
                    eng.tensor_scalar(nm, nm, -1.0, None, ALU.mult).then_inc(m_fmax, 1)

                def fox_norm(f):
                    F, n, r = 16 * M + f, (f % 4 + 1) * P, psumr[:, f % 4:f % 4 + 1]
                    eng.wait_ge(m_fp, F + 1)
                    eng.reciprocal(r, r).then_inc(m_fn, 1)
                    eng.wait_ge(m_fn, 2 * F + 1)
                    eng.tensor_scalar(fprob[:, 0:n], fprob[:, 0:n], r, None, ALU.mult).then_inc(m_fn, 1)

                def fox_evac(f):
                    F, (h, i) = 16 * M + f, divmod(f, 4)
                    hp = slice((h % 2) * HD, (h % 2 + 1) * HD)
                    eng.wait_ge(m_fo, F + 1)
                    eng.tensor_copy(proj[hp, FQ + h // 2, i * P:(i + 1) * P], ps[hp, 6, 0:P]).then_inc(m_fy, 1)

                eng.wait_ge(m_silu, 8 * (M + 1))
                ssd_mask(0)
                for it in range(8):
                    f = 2 * it
                    if f % 4 == 0:
                        fox_rows(f // 4)
                    fox_max(f)
                    ssd_operands(it)
                    if it < 7:
                        ssd_mask(it + 1)
                    fox_norm(f)
                    ssd_evac(it)
                    fox_evac(f)
                    fox_max(f + 1)
                    fox_norm(f + 1)
                    fox_evac(f + 1)
                eng.wait_ge(m_z, 4 * (M + 1))
                eng.wait_ge(m_sev, SEV[8] * (M + 1))
                for t in range(4):
                    eng.tensor_tensor(proj[:, t, :], proj[:, t, :], proj[:, Z + t, :], ALU.mult).then_inc(m_gate, 1)
                for g in range(2):
                    eng.wait_ge(m_sd, 2 * M + g + 1)
                    r = ss[("am", "ab")[g]][:, :, :].rearrange("p a t -> p (a t)")
                    eng.reciprocal(r, r).then_inc(m_rn, 1)
                    eng.wait_ge(m_rn, 6 * M + 3 * g + 1)
                    if g == 0:
                        eng.wait_ge(m_gate, 4 * (M + 1))
                    for q in range(2):
                        t = 2 * g + q
                        eng.scalar_tensor_tensor(proj[:, t, :], proj[:, t, :], pc(f"norm_g_{l}", t), r, ALU.mult,
                                                 ALU.mult).then_inc(m_rn, 1)
                for t in range(DC):
                    src = proj[:, (XBC + t if t < 4 else FQ + t - 4 if t < 6 else BG + t - 6), :]
                    eng.wait_ge(s_hhi, w.h_chunks + t + 1)
                    eng.tensor_tensor(h_lo[:, t, :], src, h_hi[:, t, :].bitcast(F32), ALU.subtract).then_inc(s_hlo, 1)
                w.mixer += 1
                w.h_chunks += DC

            def rotate(x, tab, tmp, b, r):
                eng.wait_ge(r_sw, r + 1)
                eng.tensor_tensor(tmp, ps[:, 4 + b, :], tab[:, 1, :], ALU.mult).then_inc(r_out, 1)
                eng.tensor_tensor(x, x, tab[:, 0, :], ALU.mult).then_inc(r_out, 1)
                eng.wait_ge(r_out, 3 * r + 2)
                eng.tensor_tensor(x, x, tmp, ALU.add).then_inc(r_out, 1)

            def norm_gqa():
                eng.wait_ge(s_rope, 16)
                eng.wait_ge(s_evac, w.events)
                for j, (x, t, gain) in enumerate(GQA_JOBS):
                    b, o = j % 2, w.nout + 2 * j
                    eng.wait_ge(n_sd, w.nms + j + 1)
                    eng.reciprocal(gpt[:, b, :], gpt[:, b, :]).then_inc(n_out, 1)
                    eng.wait_ge(n_out, o + 1)
                    eng.scalar_tensor_tensor(x[:, t, :], x[:, t, :], pc(gain), gpt[:, b, :], ALU.mult, ALU.mult)\
                       .then_inc(n_out, 1)
                    eng.wait_ge(n_out, o + 2)
                    rotate(x[:, t, 0:SEQ], gcos, gp[:, b, 0:SEQ], b, w.rope + j)
                n = len(GQA_JOBS)
                w.nms, w.nout, w.rope = w.nms + n, w.nout + 2 * n, w.rope + n

            def norm_mla():
                eng.wait_ge(s_rope, 32)
                eng.wait_ge(s_evac, w.events)
                o = w.nout
                for p, (x, n, width, gain) in enumerate(((ckv, KVC, KEYS, "mkv_norm"), (cq, QC, SEQ, "mq_norm"))):
                    r = msd[:, p, 0:width]
                    eng.wait_ge(n_sd, w.nms + p + 1)
                    eng.reciprocal(r, r).then_inc(n_out, 1)
                    o += 1
                    eng.wait_ge(n_out, o)
                    for t in range(n):
                        eng.scalar_tensor_tensor(x[:, t, :], x[:, t, :], pc(gain, t), r, ALU.mult, ALU.mult)\
                           .then_inc(n_out, 1)
                    o += n
                eng.wait_ge(n_out, o)
                for t in range(QC + KVC):
                    eng.wait_ge(s_hhi, w.h_chunks + t + 1)
                    x, hi, lo = (ckv, ckvn_hi, ckvn_lo) if t < KVC else (cq, cqn_hi, cqn_lo)
                    c = t if t < KVC else t - KVC
                    eng.tensor_tensor(lo[:, c, :], x[:, c, :], hi[:, c, :].bitcast(F32), ALU.subtract).then_inc(s_hlo, 1)
                rotate(kpe[:, 0:SEQ], mcos, msd[:, 0, 0:SEQ], 0, w.rope)
                w.nms, w.nout, w.rope, w.h_chunks = w.nms + 2, o, w.rope + 1, w.h_chunks + QC + KVC

            def rope_mla():
                eng.wait_ge(s_evac, w.events)
                for j in range(4):
                    if j >= 2:
                        eng.wait_ge(r_out, 3 * (w.rope + j - 1))
                    rotate(qpe[:, j, :], mcos, mp[:, j % 2, 0:SEQ], j % 2, w.rope + j)
                w.rope += 4

            def attention(kind):
                a = ATT[kind]
                eng.wait_ge(s_asum, ada_done[KEPT[kind]])
                eng.tensor_copy(kept[:, :], ps[:, B_ADA, 48 * KEPT[kind]:48 * KEPT[kind] + 2 * MOD]).then_inc(s_keep, 1)
                eng.wait_ge(r_out, 3 * w.rope)
                for i, (x, hi, lo) in enumerate(a["split"]):
                    eng.wait_ge(t_sh, w.splits + i + 1)
                    eng.tensor_tensor(lo, x, hi.bitcast(F32), ALU.subtract).then_inc(t_sl, 1)
                w.splits += len(a["split"])
                for run in map(lambda r: Run(*r), a["runs"]):
                    U = len(run.units)
                    U0, S0, B0 = w.units, w.heads, w.blocks

                    def maximum(s, u):
                        t, r, _, n = run.units[u]
                        m = nmax[:, (S0 + s) % 2 * 8:(S0 + s) % 2 * 8 + 8].rearrange("p (r t) -> p r t", r=2)
                        if u == 0 and S0 + s >= 2:
                            eng.wait_ge(t_dg, S0 + s - 1)
                        eng.wait_ge(t_s, U0 + s * U + u + 1)
                        eng.reduce_max(m[:, r, t:t + 1], ps[:, B_MAX + (U0 + s * U + u) % 2, 0:n], AX_X).then_inc(t_mx, 1)
                        if u < U - 1:
                            return
                        eng.wait_ge(t_mx, U0 + (s + 1) * U)
                        eng.tensor_tensor(m[:, 0, 0:run.qt], m[:, 0, 0:run.qt], m[:, run.n_runs - 1, 0:run.qt], ALU.max)\
                           .then_inc(t_cm, 1)
                        eng.wait_ge(t_cm, S0 + s + 1)
                        if s >= 2:
                            eng.wait_ge(t_st, B0 + (s - 1) * run.kb)
                        elif B0:
                            eng.wait_ge(t_st, B0)
                        eng.scalar_tensor_tensor(a["diag"][:, (S0 + s) % 2, 0:run.nq].rearrange("p (t q) -> p t q", q=P),
                                                 ident[:, :].unsqueeze(1).broadcast_to([P, run.qt, P]), -1.0,
                                                 m[:, 0, 0:run.qt].unsqueeze(2).broadcast_to([P, run.qt, P]), ALU.mult,
                                                 ALU.mult).then_inc(t_dg, 1)

                    def remainder(s, j):
                        b = B0 + s * run.kb + j
                        eng.wait_ge(t_pt, b + 1)
                        x = b % RING
                        eng.tensor_tensor(a["p"][1][:, x, 0:run.nq], a["prob"][:, x, 0:run.nq],
                                          a["p"][0][:, x, 0:run.nq].bitcast(F32), ALU.subtract).then_inc(t_pl, 1)

                    def normalise(s, half):
                        hp, n = slice((s % 2) * HD, (s % 2 + 1) * HD), run.nq // 2
                        c = slice(half * n, (half + 1) * n)
                        if S0 + s >= 2:
                            eng.wait_ge(t_y, S0 + s - 1)
                        eng.wait_ge(t_pv, B0 + (s + 1) * run.kb)
                        eng.reciprocal(a["rec"][hp, c], ps[hp, B_SUM + s % 2, c]).then_inc(t_rc, 1)
                        if half:
                            eng.wait_ge(t_rc, 2 * (S0 + s) + 2)
                            eng.tensor_tensor(a["y"][hp, s // 2, run.q], ps[hp, B_OUT + s % 2, 0:run.nq], a["rec"][hp, 0:run.nq],
                                              ALU.mult).then_inc(t_y, 1)

                    for u in range(U):
                        maximum(0, u)
                    for s in range(HEADS):
                        for j in range(run.kb):
                            if s + 1 < HEADS:
                                for u in run.share[j]:
                                    maximum(s + 1, u)
                            remainder(s, j)
                            for half in range(2):
                                if s and j == min(2 + half, run.kb - 1):
                                    normalise(s - 1, half)
                    for half in range(2):
                        normalise(HEADS - 1, half)
                    w.units, w.heads, w.blocks = U0 + HEADS * U, S0 + HEADS, B0 + HEADS * run.kb
                eng.wait_ge(t_y, w.heads)
                outs = [(h_hi, h_lo, q_t[:, :, 0:SEQ]), (hc_hi, hc_lo, q_t[:, :, SEQ:])] if kind == "gqa" else \
                        [(y2_hi, y2_lo, mq[:, :, :])]
                for i, (hi, lo, y) in enumerate(outs):
                    for k in range(DC):
                        eng.wait_ge(s_hhi, w.h_chunks + i * DC + k + 1)
                        eng.tensor_tensor(lo[:, k, :], y[:, k, :], hi[:, k, :].bitcast(F32), ALU.subtract)\
                           .then_inc(s_hlo, 1)
                w.h_chunks += DC * len(outs)

            for j, item in enumerate(sched):
                if j in early:
                    ahead(sched[early[j]][1])
                if item[0] == "ada0":
                    for i in range(ADA_UNITS):
                        ada_unit(0, i, 0, 1, i, (i, i), i % 2, i * ada_parts(0))
                elif item[0] == "lin":
                    if j not in early.values() and sched[j - 1][0] != "lin":
                        ahead(item[1])
                    linear(item[1], sched[j + 1][1] if sched[j + 1][0] == "lin" else None)
                elif item[0] == "ln":
                    layer_norm(*item[1:])
                elif item[0] == "mod":
                    modulate(*item[1:])
                elif item[0] == "mixer":
                    mixer(item[1])
                elif item[0] == "gqa":
                    norm_gqa()
                    attention("gqa")
                elif item[0] == "mla_norm":
                    norm_mla()
                elif item[0] == "mla":
                    rope_mla()
                    attention("mla")


STOP = 0


def kernel(**inputs):
    import numpy as np
    import concourse.bacc as bacc
    from concourse.bass_utils import run_bass_kernel_spmd as run

    a = {k: np.asarray(v) for k, v in inputs.items()}
    t = {}

    def tiles(w, kc, per):
        n = w.shape[1] // P
        return np.ascontiguousarray(w.reshape(kc, P, n // per, per, P).transpose(2, 1, 3, 0, 4)
                                    .reshape(n // per, P, per * kc * P))

    def rows(w, kc, n):
        m = w.shape[1] // n
        return np.ascontiguousarray(w.reshape(kc, P, n, m).transpose(2, 1, 0, 3).reshape(n, P, kc * m))

    def cols_of(v):
        return np.asarray(v).reshape(-1, P).T

    t["xT"] = np.ascontiguousarray(a["x"][0].T)
    t["ctxT"] = np.ascontiguousarray(a["ctx_2"][0].T)
    for l in range(DEPTH):
        for s in range(3):
            t[f"ada_{3 * l + s}"] = tiles(a["ada_w"][l][:, s * 3 * D:(s + 1) * 3 * D], DC, 2)
        for s in range(2):
            t[f"ada_{6 + 2 * l + s}"] = tiles(a["w_ada_2"][l][:, s * 3 * D:(s + 1) * 3 * D], DC, 2)
        for which in (1, 2):
            w_in, w_out = a[f"ffn{which}_w_in"][l], a[f"ffn{which}_w_out"][l]
            c0 = 0
            for g, nc_ in enumerate(FF_GROUPS):
                part = slice(c0 * P, (c0 + nc_) * P)
                gate, up = w_in[:, :FF][:, part], w_in[:, FF:][:, part]
                both = np.stack([gate.reshape(D, nc_, P), up.reshape(D, nc_, P)], axis=2).reshape(D, 2 * nc_ * P)
                t[f"ffn{which}_in_{l}_{g}"] = tiles(both, DC, 2)
                t[f"ffn{which}_out_{l}_{g}"] = tiles(w_out[part], nc_, 1)
                c0 += nc_
        w = a["mix_w_in"][l]
        z, xbc, dt, q, k, v, f, bg, cg, xin = np.split(w, np.cumsum([512, 1024, 8, 256, 256, 256, 4, 256, 256]), axis=1)
        t[f"mix_in_{l}"] = tiles(np.concatenate([xbc, z, q, k, cg, xin, bg], axis=1), DC, 2)
        t[f"mix_v_{l}"] = rows(v, DC, 1)
        t[f"mix_dt_{l}"] = rows(np.concatenate([dt, f], axis=1), DC, 1)
        t[f"mix_out_{l}"] = tiles(a["mix_w_out"][l], DC, 2)
        n2 = FF2 // P // G2
        for g in range(n2):
            part = slice(g * G2 * P, (g + 1) * G2 * P)
            t[f"mlp_in_{l}_{g}"] = tiles(a["mlp_w1_2"][l][:, part], DC, 2)
            t[f"mlp_out_{l}_{g}"] = tiles(a["mlp_w2_2"][l][part], G2, 2)
    order = [h for j in range(DC) for h in (8 * (j // 4) + j % 4, 8 * (j // 4) + 4 + j % 4)]
    wq, wk, wv = np.split(a["gqa_w_qkv_2"][0], [HEADS * HD, (HEADS + GQA_KV) * HD], axis=1)
    t["gqa_q"] = tiles(wq.reshape(D, HEADS, HD)[:, order].reshape(D, D), DC, 2)
    t["gqa_k"] = tiles(wk, DC, 2)
    t["gqa_v"] = rows(wv, DC, 1)
    t["gqa_o"] = tiles(a["gqa_w_o_2"][0].reshape(HEADS, HD, D)[order].reshape(D, D), DC, 2)
    wc, wckv, wkpe = np.split(a["mla_w_in_2"][0], [QC * P, (QC + KVC) * P], axis=1)
    t["mla_cq"] = tiles(wc, DC, 1)
    t["mla_ckv"] = tiles(wckv, DC, KVC)
    t["mla_kpe"] = tiles(np.concatenate([wkpe] * 4, axis=1), DC, 1)
    uq = a["mla_w_uq_2"][0].reshape(QC * P, HEADS, HD + ROPE)
    t["mla_q"] = tiles(uq[:, :, :HD].reshape(QC * P, D), QC, 4)
    t["mla_qpe"] = tiles(uq[:, :, HD:].reshape(QC * P, HEADS * ROPE), QC, 4)
    ukv = a["mla_w_ukv_2"][0].reshape(KVC * P, HEADS, 2 * HD)
    t["mla_k"] = tiles(ukv[:, :, :HD].reshape(KVC * P, D), KVC, 8)
    t["mla_v"] = rows(ukv[:, :, HD:].reshape(KVC * P, D), KVC, 2)
    t["mla_o"] = tiles(a["mla_w_o_2"][0], DC, 2)

    def rope(dim):
        axis, quarter = dim // 2, dim // 4
        freq = np.float32(10000.0) ** (-np.arange(0, axis, 2, dtype=np.float32) / np.float32(axis))
        d = np.arange(P) % dim
        tok = np.arange(SEQ)
        pos = np.where((d // axis == 0)[:, None], tok // 64, tok % 64).astype(np.float32)
        ang = (pos * freq[d % quarter][:, None].astype(np.float32)).astype(np.float32)
        sign = np.where((d % axis) < quarter, -1.0, 1.0).astype(np.float32)[:, None]
        swap = np.zeros((P, P), np.float32)
        swap[np.arange(P) ^ quarter, np.arange(P)] = 1.0
        return np.stack([np.cos(ang), np.sin(ang) * sign], axis=1).astype(np.float32), swap

    t["rope_gqa"], swap16 = rope(HD)
    t["rope_mla"], swap8 = rope(ROPE)
    t["swaps"] = np.ascontiguousarray(np.stack([swap16, swap8], axis=1))

    cols, n = param_table()
    par = np.zeros((P, n), np.float32)

    def put(name, v):
        c0, width = cols[name]
        par[:, c0:c0 + width] = np.asarray(v).reshape(P, width)

    put("c1", cols_of(a["c"][0]))
    put("c2", np.stack([cols_of(a["c_2"][0]), cols_of(a["c_ctx_2"])], axis=2))
    put("ln_g_in", cols_of(a["ln_in_g"]))
    put("ln_b_in", cols_of(a["ln_in_b"]))
    for l in range(DEPTH):
        for s in range(3):
            put(f"ada_b_{3 * l + s}", cols_of(a["ada_b"][l][s * 3 * D:(s + 1) * 3 * D]))
            put(f"ln_g_b1_{l}_{s}", cols_of(a["ln_g"][l, s]))
            put(f"ln_b_b1_{l}_{s}", cols_of(a["ln_b"][l, s]))
        for s in range(2):
            put(f"ada_b_{6 + 2 * l + s}", cols_of(a["b_ada_2"][l][s * 3 * D:(s + 1) * 3 * D]))
            put(f"ln_g_b2_{l}_{s}", cols_of(a["ln_g_2"][l, s]))
            put(f"ln_b_b2_{l}_{s}", cols_of(a["ln_b_2"][l, s]))
        put(f"conv_w_{l}", a["ssd_conv_w"][l].reshape(4, 8, P).transpose(2, 1, 0))
        put(f"conv_b_{l}", cols_of(a["ssd_conv_b"][l]))
        put(f"ssd_d_{l}", cols_of(np.repeat(a["ssd_d"][l], SSD_P)))
        put(f"norm_g_{l}", cols_of(a["ssd_norm_g"][l]))
        put(f"sconv_w_{l}", a["sconv_w"][l].reshape(3, 2, P).transpose(2, 1, 0))
        put(f"dt_bias_{l}", np.broadcast_to(np.concatenate([a["ssd_dt_bias"][l], a["fox_f_bias"][l]]), (P, 12)))
        put(f"a_log_{l}", np.broadcast_to(a["ssd_a_log"][l], (P, SSD_H)))
    put("q_norm", np.tile(a["gqa_q_norm_2"][0], 2))
    put("k_norm", np.tile(a["gqa_k_norm_2"][0], 2))
    put("mq_norm", cols_of(a["mla_q_norm_2"][0]))
    put("mkv_norm", cols_of(a["mla_kv_norm_2"][0]))
    t["params"] = par

    used = {"params", "swaps", "xT"} | {i[1].name for i in schedule(STOP) if i[0] == "lin"}
    t = {k: v for k, v in t.items() if not STOP or k in used or k.startswith(("ada_", "ctx", "rope"))}
    nc = bacc.Bacc("TRN2", target_bir_lowering=False, num_devices=1)
    t_in = {k: nc.dram_tensor(k, v.shape, F32, kind="ExternalInput").ap() for k, v in t.items()}
    out = nc.dram_tensor("outT", (D, SEQ), F32, kind="ExternalOutput").ap()
    build(nc, t_in, out, STOP)
    r = run(nc, [t], core_ids=[0])
    return np.ascontiguousarray(r.results[0]["outT"].T).reshape(1, SEQ, D)
```
